# Optimizing a Trainium2 kernel written in Bass

```python
import math
import jax, jax.numpy as jnp
from jax import lax
import numpy as np

D_MODEL = 1024
BATCH = 1
SEQ = 2048
DEPTH = 1
DEC_BATCH = 8
DEC_SEQ = 4
PAST_LEN = 16384
PAGE_SIZE = 128

HG_WIDTH = D_MODEL // 2
HG_DK = 128
HG_DV = 128
HG_HEADS = HG_WIDTH // HG_DK
HG_CHUNK = 64
CM_WIDTH = D_MODEL - HG_WIDTH
CM_GROUPS = 4
CM_GROUP_DIM = CM_WIDTH // CM_GROUPS
CM_CHUNK = 128
IN_WIDTH = 4 * HG_WIDTH + 2 * CM_WIDTH
N_MEM = 256
X_HEADS = 4
X_HEAD_DIM = D_MODEL // X_HEADS
D_FF = 4 * D_MODEL
EPS = 1e-6

kernel_name = "hybrid_hgrn2_gmlp_memxattn_step"

def rmsnorm(x, g):
    xf = x.astype(jnp.float32)
    y = xf * lax.rsqrt(jnp.mean(xf * xf, axis=-1, keepdims=True) + EPS)
    return (y * g.astype(jnp.float32)).astype(x.dtype)

def layernorm(x, g, b):
    xf = x.astype(jnp.float32)
    mu = jnp.mean(xf, axis=-1, keepdims=True)
    var = jnp.mean(jnp.square(xf - mu), axis=-1, keepdims=True)
    y = (xf - mu) * lax.rsqrt(var + EPS)
    return (y * g.astype(jnp.float32) + b.astype(jnp.float32)).astype(x.dtype)

def hgrn2_chunk(S, inp):
    q, k, logf, v = inp
    C = q.shape[1]
    b = jnp.cumsum(logf, axis=1)
    causal = jnp.tril(jnp.ones((C, C), dtype=bool))
    diff = b[:, :, None] - b[:, None, :]
    decay = jnp.exp(jnp.where(causal[None, :, :, None, None], diff, -jnp.inf))
    A = jnp.einsum('bthk,bshk,btshk->bhts', q, k, decay)
    o = (jnp.einsum('bhts,bshv->bthv', A, v)
         + jnp.einsum('bthk,bhkv->bthv', q * jnp.exp(b), S))
    b_last = b[:, -1]
    k_dec = k * jnp.exp(b_last[:, None] - b)
    S_new = jnp.exp(b_last)[..., None] * S + jnp.einsum('bshk,bshv->bhkv', k_dec, v)
    return S_new, o

def hgrn2_scan(S0, q, k, logf, v):
    B, L = q.shape[0], q.shape[1]
    C = min(HG_CHUNK, L)
    n = L // C
    def to_chunks(a):
        return jnp.moveaxis(a.reshape(B, n, C, HG_HEADS, a.shape[-1]), 1, 0)
    S_last, o = lax.scan(hgrn2_chunk, S0, (to_chunks(q), to_chunks(k), to_chunks(logf), to_chunks(v)))
    o = jnp.moveaxis(o, 0, 1).reshape(B, L, HG_HEADS, HG_DV)
    return S_last, o

def chunk_gmlp(u, vn, w_s, b_s):
    B, L, _ = u.shape
    T = min(CM_CHUNK, L)
    n = L // T
    uu = u.reshape(B, n, T, CM_GROUPS, CM_GROUP_DIM)
    vv = vn.reshape(B, n, T, CM_GROUPS, CM_GROUP_DIM)
    wm = jnp.where(jnp.tril(jnp.ones((T, T), dtype=bool))[None], w_s[:, :T, :T], 0.0).astype(vn.dtype)
    mixed = jnp.einsum('gts,bnsgc->bntgc', wm, vv) + b_s[:, :T].T.astype(vn.dtype)[None, None, :, :, None]
    return (uu * mixed).reshape(B, L, CM_WIDTH)

def decoder_layer(x, S0, mem_k, mem_v, lb, g_mix, w_in, hg_norm_g, ln_v_g, ln_v_b, w_s, b_s,
                  w_out, g_cross, w_cq, w_co, g_mlp, w_up, w_down):
    B, L, _ = x.shape
    hn = rmsnorm(x, g_mix)
    z = hn @ w_in
    zq, zf, zi, zg, zu, zv = jnp.split(
        z, [HG_WIDTH, 2 * HG_WIDTH, 3 * HG_WIDTH, 4 * HG_WIDTH, 4 * HG_WIDTH + CM_WIDTH], axis=-1)
    hs = (B, L, HG_HEADS, HG_DK)
    zf32 = zf.astype(jnp.float32).reshape(hs)
    q = jax.nn.silu(zq.astype(jnp.float32)).reshape(hs)
    f = lb + (1.0 - lb) * jax.nn.sigmoid(zf32)
    logf = jnp.log(f)
    k = (1.0 - lb) * jax.nn.sigmoid(-zf32)
    v = zi.astype(jnp.float32).reshape(B, L, HG_HEADS, HG_DV)
    S_new, o = hgrn2_scan(S0.astype(jnp.float32), q, k, logf, v)
    o = o * lax.rsqrt(jnp.mean(o * o, axis=-1, keepdims=True) + EPS) * hg_norm_g.astype(jnp.float32).reshape(HG_HEADS, HG_DV)
    o_hg = (o.reshape(B, L, HG_WIDTH) * jax.nn.sigmoid(zg.astype(jnp.float32))).astype(x.dtype)
    u = jax.nn.gelu(zu)
    vn = layernorm(jax.nn.gelu(zv), ln_v_g, ln_v_b)
    o_cm = chunk_gmlp(u, vn, w_s, b_s)
    x = x + jnp.concatenate([o_hg, o_cm], axis=-1) @ w_out
    hq = (rmsnorm(x, g_cross) @ w_cq).reshape(B, L, X_HEADS, X_HEAD_DIM)
    s = jnp.einsum('blhd,bmhd->bhlm', hq.astype(jnp.float32), mem_k.astype(jnp.float32)) * (X_HEAD_DIM ** -0.5)
    p = jax.nn.softmax(s, axis=-1).astype(x.dtype)
    ca = jnp.einsum('bhlm,bmhd->blhd', p, mem_v.astype(x.dtype)).reshape(B, L, D_MODEL)
    x = x + ca @ w_co
    hm = rmsnorm(x, g_mlp) @ w_up
    x = x + jnp.square(jax.nn.relu(hm)) @ w_down
    return x, S_new, vn

def setup_inputs(seed: int = 0) -> dict:
    key = jax.random.key(seed)
    ks = jax.random.split(key, 32)
    def nrm(k, shape, scale):
        return jax.random.normal(k, shape, jnp.float32) * scale
    def gain(k, shape):
        return 1.0 + 0.02 * jax.random.normal(k, shape, jnp.float32)
    return {
        "x_prompt": nrm(ks[0], (BATCH, SEQ, D_MODEL), 1.0),
        "x_sample": nrm(ks[1], (DEC_BATCH, DEC_SEQ, D_MODEL), 1.0),
        "mem_prompt": nrm(ks[2], (BATCH, N_MEM, D_MODEL), 1.0),
        "state_hgrn": nrm(ks[3], (DEPTH, DEC_BATCH, HG_HEADS, HG_DK, HG_DV), 0.3),
        "cache_mem_k": nrm(ks[4], (DEPTH, DEC_BATCH, N_MEM, X_HEADS, X_HEAD_DIM), 1.0),
        "cache_mem_v": nrm(ks[5], (DEPTH, DEC_BATCH, N_MEM, X_HEADS, X_HEAD_DIM), 1.0),
        "lb_param": nrm(ks[6], (DEPTH + 1, HG_WIDTH), 0.5),
        "g_mix": gain(ks[7], (DEPTH, D_MODEL)),
        "w_in": nrm(ks[8], (DEPTH, D_MODEL, IN_WIDTH), D_MODEL ** -0.5),
        "hg_norm_g": gain(ks[9], (DEPTH, HG_WIDTH)),
        "ln_v_g": gain(ks[10], (DEPTH, CM_WIDTH)),
        "ln_v_b": nrm(ks[11], (DEPTH, CM_WIDTH), 0.02),
        "w_s": nrm(ks[12], (DEPTH, CM_GROUPS, CM_CHUNK, CM_CHUNK), CM_CHUNK ** -0.5),
        "b_s": gain(ks[13], (DEPTH, CM_GROUPS, CM_CHUNK)),
        "w_out": nrm(ks[14], (DEPTH, D_MODEL, D_MODEL), D_MODEL ** -0.5),
        "g_cross": gain(ks[15], (DEPTH, D_MODEL)),
        "g_mem": gain(ks[16], (DEPTH, D_MODEL)),
        "w_cq": nrm(ks[17], (DEPTH, D_MODEL, D_MODEL), D_MODEL ** -0.5),
        "w_ck": nrm(ks[18], (DEPTH, D_MODEL, D_MODEL), D_MODEL ** -0.5),
        "w_cv": nrm(ks[19], (DEPTH, D_MODEL, D_MODEL), D_MODEL ** -0.5),
        "w_co": nrm(ks[20], (DEPTH, D_MODEL, D_MODEL), D_MODEL ** -0.5),
        "g_mlp": gain(ks[21], (DEPTH, D_MODEL)),
        "w_up": nrm(ks[22], (DEPTH, D_MODEL, D_FF), D_MODEL ** -0.5),
        "w_down": nrm(ks[23], (DEPTH, D_FF, D_MODEL), D_FF ** -0.5),
        "g_final": gain(ks[24], (D_MODEL,)),
    }

def reference(x_prompt, x_sample, mem_prompt, state_hgrn, cache_mem_k, cache_mem_v,
              lb_param, g_mix, w_in, hg_norm_g, ln_v_g, ln_v_b, w_s, b_s, w_out,
              g_cross, g_mem, w_cq, w_ck, w_cv, w_co, g_mlp, w_up, w_down, g_final):
    lb_all = jnp.cumsum(jax.nn.softmax(lb_param.astype(jnp.float32), axis=0), axis=0)
    xp, xs = x_prompt, x_sample
    S_p_list, S_s_list, mk_list, mv_list, cmv_list = [], [], [], [], []
    for l in range(DEPTH):
        lb = lb_all[l].reshape(HG_HEADS, HG_DK)
        mem_n = rmsnorm(mem_prompt, g_mem[l])
        mk = (mem_n @ w_ck[l]).reshape(BATCH if False else mem_prompt.shape[0], N_MEM, X_HEADS, X_HEAD_DIM)
        mv = (mem_n @ w_cv[l]).reshape(mem_prompt.shape[0], N_MEM, X_HEADS, X_HEAD_DIM)
        S0_p = jnp.zeros((xp.shape[0], HG_HEADS, HG_DK, HG_DV), jnp.float32)
        xp, S_p, _ = decoder_layer(xp, S0_p, mk, mv, lb, g_mix[l], w_in[l], hg_norm_g[l], ln_v_g[l], ln_v_b[l],
                                   w_s[l], b_s[l], w_out[l], g_cross[l], w_cq[l], w_co[l], g_mlp[l], w_up[l], w_down[l])
        xs, S_s, vn_s = decoder_layer(xs, state_hgrn[l], cache_mem_k[l], cache_mem_v[l], lb, g_mix[l], w_in[l],
                                      hg_norm_g[l], ln_v_g[l], ln_v_b[l], w_s[l], b_s[l], w_out[l], g_cross[l],
                                      w_cq[l], w_co[l], g_mlp[l], w_up[l], w_down[l])
        S_p_list.append(S_p.astype(state_hgrn.dtype))
        S_s_list.append(S_s.astype(state_hgrn.dtype))
        mk_list.append(mk.astype(cache_mem_k.dtype))
        mv_list.append(mv.astype(cache_mem_v.dtype))
        cmv_list.append(vn_s)
    y_prompt = rmsnorm(xp, g_final)
    y_sample = rmsnorm(xs, g_final)
    state_hgrn_prompt = jnp.stack(S_p_list)
    state_hgrn_sample = jnp.stack(S_s_list)
    mem_k_prompt = jnp.stack(mk_list)
    mem_v_prompt = jnp.stack(mv_list)
    cm_v_sample = jnp.stack(cmv_list)
    return (y_prompt, y_sample, state_hgrn_prompt, state_hgrn_sample, mem_k_prompt, mem_v_prompt, cm_v_sample)


_drawn_inputs = setup_inputs


def setup_inputs(seed=0):
    import zlib

    import numpy as np

    out = dict(_drawn_inputs(seed))
    spreads = {}
    factors = {'hg_norm_g': 8.0,
     'ln_v_g': 7.622,
     'ln_v_b': 7.611,
     'b_s': 6.128,
     'g_cross': 8.0,
     'g_mem': 2.848,
     'g_mlp': 3.258,
     'g_final': 8.174}
    for name, (base, spread) in spreads.items():
        noise = np.random.default_rng([zlib.crc32(name.encode()), seed]).standard_normal(out[name].shape)
        drawn = base * np.exp(spread * noise) if base else spread * noise
        out[name] = __import__('jax').numpy.asarray(drawn.astype(out[name].dtype))
    for name, factor in factors.items():
        out[name] = (out[name] * factor).astype(out[name].dtype)
    return out
```

```python
import concourse.bass as bass
from concourse import mybir
from contextlib import ExitStack

F32 = mybir.dt.float32
F32R = mybir.dt.float32r
ACT = mybir.ActivationFunctionType
ALU = mybir.AluOpType
AX = mybir.AxisListType

P = 128
D = 1024
KD = D // P
SEQ = 2048
BT = 512
NB = SEQ // BT
TT = BT // P
HG = 512
H = 4
FF = 4096
NM = 256
MT = NM // P
XD = 256
DB, DS = 8, 4
NS = DB * DS
EPS = 1e-6
RING = 8
RAW = 4
LEVELS = 8
SLOTS = LEVELS - 1 + 2
UNITS = TT * 2
ATT_SCALE = XD ** -0.5

W_TILES = {"mem": 4 * KD, "block": 28 * KD}
SG = NS + DS
SLV = 3
WS = 4
KV = 4

PE_STEPS = (["n1", "zf", "zq", "zt", "zi", "zg", "zv", "lv", "kt", "o", "zu", "mix", "ot"]
            + [f"st{j}" for j in range(4)] + ["wo0"] + [f"st{j}" for j in range(4, 8)] + ["wo1"]
            + ["n2", "cq0", "cq1", "qt"]
            + [s for b in range(DB + 1) for s in ([f"kt{b}_0", f"kt{b}_1"] if b < DB else [])
               + ([f"sc{b - 1}"] if b else [])]
            + ["pt"] + [f"ca{b}" for b in range(DB)] + ["cat", "co0", "co1", "n3"]
            + [s for e in range(9) for s in ([f"up{e}"] if e < 8 else []) + ([f"ht{e - 1}"] if e else [])]
            + [f"dn{r}_{c}" for r in range(4) for c in range(2)])
ACT_STEPS = (["rstd_n1", "zf_rows", "zq_rows", "sig", "v_rows", "gate", "logf", "decays", "zv_gelu", "kd_rows", "o_rows",
              "zu_gelu", "rstd_ln", "rstd_o", "rstd_n2", "q_rows0", "q_rows1"]
             + [f"kts{b}_0" for b in range(DB)] + ["p_exp"] + ["ca_rows", "rstd_n3"] + [f"relu{e}" for e in range(8)]
             + ["rstd_y"])
DVE_STEPS = (["var_n1", "xn1", "xt1", "qq", "args", "scaled", "vm", "att", "var_ln", "vn", "var_o", "mixed_cm", "mixed",
              "xt_ot"]
             + [f"new{j}" for j in range(4)] + ["x_wo0"] + [f"new{j}" for j in range(4, 8)] + ["x_wo1"]
             + ["var_n2", "xn2", "xt2", "qm"] + [f"kts{b}_1" for b in range(DB)]
             + ["max", "p_rows", "pm", "xt_ca", "x_co0", "x_co1", "var_n3", "xn3", "xt3"]
             + [s for e in range(9) for s in ([f"sq{e}"] if e < 8 else []) + ([f"hts{e - 1}"] if e else [])]
             + ["x_dn0", "x_dn1", "var_y", "y"])


class Event:

    def __init__(self, sem, mem=0, block=0, step=1, prime=0):
        self.sem, self.step, self.prime = sem, step, prime
        self.per = {"mem": mem, "block": block}

    def at(self, pos, i):
        phase, b = pos
        before = self.per["mem"] if phase == "block" else 0
        return b * (self.per["block"] * self.step) + (i + (before + 1)) * self.step + self.prime


class Links:

    def __init__(self, sem, **per):
        self.sem, self.per = sem, per
        self.n, self.pos = 0, ("mem", 0)

    def start(self, pos):
        self.n, self.pos = 0, pos

    def next(self):
        self.n += 1
        phase, b = self.pos
        before = {"mem": 0, "block": self.per["mem"], "sample": self.per["mem"] + NB * self.per["block"]}[phase]
        return b * self.per["block"] + (before + self.n)

    def end(self):
        want = self.per[self.pos[0]]
        assert self.n == want, (self.sem, self.pos[0], self.n, want)


def block_jobs():
    jobs = [("n1", t) for t in range(TT)] + ["zf", "zq", "zi"]
    jobs += [("lv", 0), "zg"]
    for u in range(UNITS):
        jobs += [("kt", u)] + ([("lv", u + 1)] if u + 1 < UNITS else []) + [("out", u)]
        jobs += {1: ["zv"], 3: ["zu"], 5: [("mix", 0), ("mix", 1)]}.get(u, [])
    jobs += [("ot", t) for t in range(TT)] + [("wo", 0), ("wo", 1)]
    jobs += [("n2", t) for t in range(TT)] + [("cq", 0), ("cq", 1)]
    jobs += [("sc", t) for t in range(TT)]
    jobs += [("pt", 0), ("pt", 1), ("ca", 0), ("pt", 2), ("ca", 1), ("pt", 3), ("ca", 2), ("ca", 3)]
    jobs += [("co", 0), ("co", 1)]
    jobs += [("n3", t) for t in range(TT)]
    jobs += [("up", 0)]
    for e in range(FF // 512 - 1):
        jobs += [("up", e + 1), ("dn", e, 0), ("dn", e, 1)]
    jobs += [("dn", FF // 512 - 1, 0), ("dn", FF // 512 - 1, 1)]
    return jobs


def mem_jobs():
    jobs = [("nm", t) for t in range(MT)]
    for c in range(2):
        jobs += [("ck", c), ("ckt", c)]
    return jobs + [("cv", 0), ("cv", 1)]


def weight_tiles(job):
    name = job if isinstance(job, str) else job[0]
    if name in ("zf", "zq", "zi", "zg", "zv", "zu", "wo", "cq", "co", "up", "ck", "cv"):
        return KD
    return 4 if name == "dn" else 0


class Steps:

    def __init__(self, sem, names):
        self.sem, self.names, self.n = sem, names, 0

    def did(self, name):
        assert self.names[self.n] == name, (self.names[self.n], name)
        self.n += 1
        return self.sem


class Jobs:

    def __init__(self):
        self.lists = {"mem": mem_jobs(), "block": block_jobs()}
        self.of, self.counts = {}, {}
        for phase, jobs in self.lists.items():
            assert len(jobs) % 2 == 0, (phase, len(jobs))
            tiles = done = 0
            for i, job in enumerate(jobs):
                n = weight_tiles(job)
                self.of[phase, job] = (i % 2, i // 2, tiles, tiles + n - 1, done)
                tiles += n
                done += not n
            assert tiles == W_TILES[phase], (phase, tiles)
            self.counts[phase] = (len(jobs) // 2, tiles, done)


def program(nc, I, O):
    jobs = Jobs()
    ctx = ExitStack()

    def sb(name, shape, dt=F32, stack=ctx):
        return stack.enter_context(nc.sbuf_tensor(name, shape, dt))

    def sem(name):
        return ctx.enter_context(nc.semaphore(name))

    def event(name, mem=0, block=0, step=1, prime=0):
        return Event(sem(name), mem, block, step, prime)

    with ctx:
        w_raw = sb("w_raw", [P, RAW, 512])
        with ExitStack() as z:
            w_smp = [sb(f"w_smp{i}", [P, KD, 512], F32, z) for i in (2, 3)]
        w_hi = sb("w_hi", [P, RING, 512], F32R)
        w_lo = sb("w_lo", [P, RING, 512], F32R)
        zero = sb("zero", [P, 1])
        ident = sb("ident", [P, P])
        ones = sb("ones", [P, P])
        masks = sb("masks", [P, LEVELS, P])
        ws_t = sb("ws_t", [P, H, P])
        hgg_row = sb("hgg_row", [P, HG])
        lng_row = sb("lng_row", [P, HG])
        lnb_row = sb("lnb_row", [P, HG])
        bs_col = sb("bs_col", [P, H])
        lb = sb("lb", [P, H])
        oml = sb("oml", [P, H])
        gain = sb("gain", [P, D])
        ss = sb("ss", [P, 16])
        var = sb("var", [P, 16])
        lnv = sb("lnv", [P, 16])
        y0 = sb("y0", [P, 16])
        yt = sb("yt", [P, 16])
        rstd = sb("rstd", [P, 16])
        state = sb("state", [P, H, P])
        own = sb("own", [NS, DB])
        tri_own = sb("tri_own", [NS, DB, DS])
        w4 = sb("w4", [NS, H, DS])
        b4 = sb("b4", [NS, H])
        with ExitStack() as z:
            w_smp = [sb(f"w_smp{i}", [P, KD, 512], F32, z) for i in (0, 1)] + w_smp
        kt_hi = sb("kt_hi", [P, KD, NM], F32R)
        kt_lo = sb("kt_lo", [P, KD, NM], F32R)
        v_hi = sb("v_hi", [P, MT, D], F32R)
        v_lo = sb("v_lo", [P, MT, D], F32R)
        with ExitStack() as z:
            kv = [sb(f"kv{i}", [P, MT, D], F32, z) for i in range(KV)]
        a_hi = sb("a_hi", [P, KD, BT], F32R)
        a_lo = sb("a_lo", [P, KD, BT], F32R)
        with ExitStack() as y:
            s0 = sb("s0", [P, DB, H, P], F32, y)
            gains = sb("gains", [NS, 3, D], F32, y)
            xs = sb("xs", [NS, D], F32, y)
            xns = sb("xns", [NS, D], F32, y)
            xt = sb("xt", [P, KD, NS], F32, y)
            with ExitStack() as z:
                vm = sb("vm", [NS, DB, HG], F32, z)
                zfq = sb("zfq", [NS, 2, HG], F32, z)
                v_s, gate_s, vn_s, o_s = (sb(n, [NS, HG], F32, z) for n in ("v_s", "gate_s", "vn_s", "o_s"))
                u_s = sb("u_s", [NS, HG], F32, z)
                kk_s, qq_s, bb_s = (sb(n, [P, H, NS], F32, z) for n in ("kk_s", "qq_s", "bb_s"))
                dec_s = sb("dec_s", [P, SLV + 1, H, NS], F32, z)
                qe_m = sb("qe_m", [P, H, DB, SG], F32, z)
                el_s = sb("el_s", [P, H, DB], F32, z)
                tmp_s = sb("tmp_s", [NS, H, SLV, NS], F32, z)
                att_s = sb("att_s", [NS, H, NS], F32, z)
                kd_s = sb("kd_s", [NS, HG], F32, z)
                ws_s = sb("ws_s", [NS, H, DB, DS], F32, z)
                st_s = sb("st_s", [NS, 6], F32, z)
                mv_s = sb("mv_s", [NS, 2], F32, z)
            with ExitStack() as z:
                kts = [sb(f"kts{i}", [P, KD, NM], F32, z) for i in range(2)]
                qm = sb("qm", [P, KD, DB, SG], F32, z)
                pm = sb("pm", [P, KD, DB, SG], F32, z)
                q_s = sb("q_s", [NS, D], F32, z)
                mx_s, sum_s, rinv_s = (sb(n, [NS, H], F32, z) for n in ("mx_s", "sum_s", "rinv_s"))
            with ExitStack() as z:
                relu_s = [sb(f"relu_s{i}", [NS, 512], F32, z) for i in range(2)]
                hts = sb("hts", [P, FF // P, NS], F32, z)
        with ExitStack() as z:
            x = sb("x", [P, TT, D], F32, z)
        with ExitStack() as z:
            kk = sb("kk", [P, H, BT], F32, z)
            qq = sb("qq", [P, H, BT], F32, z)
        sb("zone_x", [P, TT, D])
        with ExitStack() as z:
            bb = sb("bb", [P, H, BT], F32, z)
            vv = sb("vv", [P, TT, HG], F32, z)
            gate = sb("gate", [P, TT, HG], F32, z)
            vn = sb("vn", [P, TT, HG], F32, z)
            uu = sb("uu", [P, TT, HG], F32, z)
            dec = [sb(f"dec{i}", [P, SLOTS, 2, P], F32, z) for i in range(2)]
            att = [sb(f"att{i}", [P, 2, P], F32, z) for i in range(2)]
            kdt = [sb(f"kdt{i}", [P, 2, P], F32, z) for i in range(2)]
            mtmp = sb("mtmp", [P, LEVELS, P], F32, z)
            e_last = [sb(f"e_last{i}", [P, 2], F32, z) for i in range(2)]
            stats = sb("stats", [P, TT, 6], F32, z)
            mv = sb("mv", [P, TT, 2], F32, z)
        with ExitStack() as z:
            b_hi = sb("b_hi", [P, KD, BT], F32R, z)
            b_lo = sb("b_lo", [P, KD, BT], F32R, z)
            pp = sb("pp", [P, TT, D], F32, z)
            pt_hi = [sb(f"pt_hi{i}", [P, MT, BT], F32R, z) for i in range(2)]
            pt_lo = [sb(f"pt_lo{i}", [P, MT, BT], F32R, z) for i in range(2)]
            mx = sb("mx", [P, TT, H], F32, z)
            psums = sb("psums", [P, TT, H], F32, z)
            rinv = sb("rinv", [P, TT, H], F32, z)
        with ExitStack() as z:
            ht_hi = [sb(f"ht_hi{i}", [P, 4, BT], F32R, z) for i in range(2)]
            ht_lo = [sb(f"ht_lo{i}", [P, 4, BT], F32R, z) for i in range(2)]
            relu = sb("relu", [P, 4, BT], F32, z)
            xn = [sb(f"xn{i}", [P, D], F32, z) for i in range(2)]
            junk = [sb(f"junk{i}", [P, D], F32, z) for i in range(2)]
        with ExitStack() as z:
            kn = [sb(f"kn{i}", [P, MT, 512], F32, z) for i in range(4)]
            ws_raw = sb("ws_raw", [P, H, P], F32, z)
            tri = sb("tri", [P, 1, P], F32, z)
            lbp = sb("lbp", [P, 2, H], F32, z)
            lbm = sb("lbm", [P, H], F32, z)
        half = [ctx.enter_context(nc.psum_tensor(f"half{i}", [P, 4, 512], F32)) for i in range(2)]

        hf, tl, dn = zip(jobs.counts["mem"], jobs.counts["block"])
        consts_in = sem("consts_in")
        w_in = [Event(sem(f"w_in{i}"), *(n // RAW for n in tl), step=16) for i in range(RAW)]
        w_rounded = sem("w_rounded")
        w_split = event("w_split", *tl, prime=RAW)
        w_used = event("w_used", *tl, prime=RING)
        pe_done = event("pe_done", *dn)
        evacuated = [event(f"evacuated{i}", *hf, prime=1) for i in range(2)]
        x_in = [event(f"x_in{t}", 0, 2, 16) for t in range(TT)]
        gain_in = event("gain_in", 0, 4, 16)
        ssq_ready = event("ssq_ready", 1, 4)
        var_ready = event("var_ready", 1, 6)
        rstd0_ready = event("rstd0_ready", 1, 6)
        xn_ready = event("xn_ready", MT, 4 * TT)
        y_out = [event(f"y_out{i}", 0, TT // 2, 16, prime=16) for i in range(2)]
        hi_ready = event("hi_ready", MT + 4, 4 * TT + 2 + H + H)
        sig_ready = event("sig_ready", 0, 1)
        logf_ready = event("logf_ready", 0, 1)
        vn_ready = event("vn_ready", 0, 1)
        args_ready = event("args_ready", 0, UNITS)
        decays_ready = event("decays_ready", 0, UNITS)
        scaled_ready = event("scaled_ready", 0, UNITS)
        att_ready = event("att_ready", 0, UNITS)
        o_ready = event("o_ready", 0, UNITS)
        mixed_ready = event("mixed_ready", 0, TT)
        max_ready = event("max_ready", 0, TT)
        exp_ready = event("exp_ready", 0, TT)
        p_ready = event("p_ready", 0, TT)
        relu_ready = event("relu_ready", 0, 8)
        sq_ready = event("sq_ready", 0, 8)
        ht_hi_ready = event("ht_hi_ready", 0, 8)
        ws_transposed, lb_args, lb_exps, setup_ready = (
            sem(n) for n in ("ws_transposed", "lb_args", "lb_exps", "setup_ready"))
        kn_out, s_out = sem("kn_out"), sem("s_out")
        act_sem, dve_sem = sem("act_chain"), sem("dve_chain")
        s_consts_in, s_first_in, s0_in, vn_out, s_out_done = (
            sem(n) for n in ("s_consts_in", "s_first_in", "s0_in", "vn_out", "s_out_done"))
        ws_in = [sem(f"ws_in{i}") for i in range(WS)]
        kv_in = [sem(f"kv_in{i}") for i in range(KV)]
        pe_s, act_s, dve_s = (Steps(sem(n), names) for n, names in (
            ("pe_steps", PE_STEPS), ("act_steps", ACT_STEPS), ("dve_steps", DVE_STEPS)))

        def step(name):
            steps, = (x for x in (pe_s, act_s, dve_s) if name in x.names)
            return steps.sem, steps.names.index(name) + 1

        def bank(i):
            return half[i // 4][:, i % 4, :]

        def own_columns(m):
            return m[:, :, :, 0:DS]

        def of_request(m, k, b):
            return m[:, k].rearrange("p b s -> p (b s)")[:, b * NS:b * NS + NS]

        last_block = ("block", NB - 1)
        SQ = slice(0, NS)

        def keys_part(eng, r, part, copy):
            eng.wait_ge(*step(f"kt{r}_{part}"))
            if r >= 2:
                eng.wait_ge(*step(f"sc{r - 2}"))
            ps = half[1][:, 2 * part:2 * part + 2, :].rearrange("p a (i m) -> p (a i) m", m=NM)
            return copy(kts[r % 2][:, 4 * part:4 * part + 4, :], ps)


        def done(pos, job, f=0):
            _, _, _, last, n = jobs.of[pos[0], job]
            if weight_tiles(job):
                return w_used.sem, w_used.at(pos, last + f * (4 * KD))
            return pe_done.sem, pe_done.at(pos, n)

        def out(pos, job, f=0):
            h, use, *_ = jobs.of[pos[0], job]
            return evacuated[h].sem, evacuated[h].at(pos, use + f * 3)

        def evacuated_of(pos, job):
            return evacuated[jobs.of[pos[0], job][0]].sem

        def out_of(pos, job):
            return half[jobs.of[pos[0], job][0]]

        def feature_tiles(ps, width=P):
            return ps[:, 0:2, :].rearrange("p a (k c) -> p (a k) c", c=width)

        block = ctx.enter_context(nc.Block())

        n_consts = 12

        @block.sync
        def _(sp):
            for i in range(2):
                sp.sem_inc(y_out[i].sem, 16)
            for dst, src in ((ident[:], I["c_ident"]), (ones[:], I["c_ones"]), (tri[:, 0, :], I["c_tri"]),
                             (masks[:], I["c_masks"]),
                             (ws_raw[:], I["w_s"][0].rearrange("g t s -> t g s")),
                             (hgg_row[:], I["hg_norm_g"][0:1, :].broadcast_to([P, HG])),
                             (lng_row[:], I["ln_v_g"][0:1, :].broadcast_to([P, HG])),
                             (lnb_row[:], I["ln_v_b"][0:1, :].broadcast_to([P, HG])),
                             (bs_col[:], I["b_s"][0].rearrange("g t -> t g")),
                             (lbp[:], I["lb_param"].rearrange("r (h p) -> p r h", p=P)),
                             (x[:, 0:MT, :], I["mem_prompt"][0].rearrange("(t p) d -> p t d", p=P)),
                             (gain[:], I["g_mem"][0:1, :].broadcast_to([P, D]))):
                with nc.allow_non_contiguous_dma(reason="small constants"):
                    sp.dma_start(dst, src).then_inc(consts_in, 16)

            def load(pos, i0, w, row0, col0, n=KD, slot0=0):
                for k in range(n):
                    s = (slot0 + k) % RAW
                    sp.wait_ge(w_split.sem, w_split.at(pos, i0 + k) - RAW)
                    sp.dma_start(w_raw[:, s, :], w[bass.ds(row0 + k * P, P), bass.ds(col0, 512)]).then_inc(w_in[s].sem, 16)

            def load_gain(pos, i, g):
                sp.wait_ge(xn_ready.sem, xn_ready.at(pos, i * TT - 1))
                sp.dma_start(gain[:], g.broadcast_to([P, D])).then_inc(gain_in.sem, 16)

            def load_x(pos, b):
                for t in range(TT):
                    sp.dma_start(x[:, t, :], I["x_prompt"][0, bass.ds(b * BT + t * P, P), :]).then_inc(x_in[t].sem, 16)

            pos = ("mem", 0)
            for i, (w, c) in enumerate((w, c) for w in ("w_ck", "w_cv") for c in range(2)):
                load(pos, i * KD, I[w][0], 0, c * 512)

            with nc.allow_non_contiguous_dma(reason="small constants"):
                sp.dma_start(own[:], I["c_own"]).then_inc(s_consts_in, 16)
                sp.dma_start(tri_own[:], I["c_tri_own"]).then_inc(s_consts_in, 16)
                for r in range(DB):
                    rows = slice(r * DS, r * DS + DS)
                    for g in range(H):
                        sp.dma_start(w4[rows, g, :], I["w_s"][0, g, 0:DS, 0:DS].rearrange("t s -> s t")).then_inc(
                            s_consts_in, 16)
                    sp.dma_start(b4[rows, :], I["b_s"][0, :, 0:DS].rearrange("g t -> t g")).then_inc(s_consts_in, 16)

            with sp.Fori(0, NB) as b:
                pos = ("block", b)
                for i, col in enumerate((512, 0, 1024, 1536, 2560, 2048)):
                    load(pos, i * KD, I["w_in"][0], 0, col)
                    if i == 0:
                        sp.wait_ge(y_out[0].sem, y_out[0].at(pos, -1))
                        sp.wait_ge(y_out[1].sem, y_out[1].at(pos, -1))
                        load_x(pos, b)
                        load_gain(pos, 0, I["g_mix"][0:1, :])
                load_gain(pos, 1, I["g_cross"][0:1, :])
                load(pos, 6 * KD, I["w_out"][0], 0, 0)
                sp.wait_ge(*out(pos, ("lv", UNITS - 1)))
                load_x(pos, b)
                load(pos, 7 * KD, I["w_out"][0], 0, 512)
                for c in range(2):
                    load(pos, (8 + c) * KD, I["w_cq"][0], 0, c * 512)
                load_gain(pos, 2, I["g_mlp"][0:1, :])
                for c in range(2):
                    load(pos, (10 + c) * KD, I["w_co"][0], 0, c * 512)
                load(pos, 12 * KD, I["w_up"][0], 0, 0)
                load_gain(pos, 3, I["g_final"][None, :])
                with sp.Fori(0, FF // 512 - 1) as e:
                    load(("block", b), 13 * KD + e * (2 * KD), I["w_up"][0], 0, e * 512 + 512)
                    for c in range(2):
                        load(("block", b), 14 * KD + 4 * c + e * (2 * KD), I["w_down"][0], e * 512, c * 512, 4)
                for c in range(2):
                    load(pos, 27 * KD + 4 * c, I["w_down"][0], FF - 512, c * 512, 4)

            chunks = ([(n, I["w_in"][0], 0, col) for n, col in (("zf", 512), ("zq", 0), ("zi", 1024), ("zg", 1536),
                                                                 ("zv", 2560), ("zu", 2048))]
                      + [(f"{n}{c}", I[w][0], 0, c * 512) for n, w in (("wo", "w_out"), ("cq", "w_cq"), ("co", "w_co"))
                         for c in range(2)]
                      + [(f"up{e}", I["w_up"][0], 0, e * 512) for e in range(8)]
                      + [(f"dn{r}_{c}", I["w_down"][0], r * D, c * 512) for r in range(4) for c in range(2)])

            def load_s(i0, i1):
                for i in range(i0, i1):
                    if i >= WS:
                        sp.wait_ge(*step(chunks[i - WS][0]))
                    _, w, row, col = chunks[i]
                    sp.dma_start(w_smp[i % WS][:], w[row:row + D, col:col + 512].rearrange("(k p) c -> p k c", p=P)
                                 ).then_inc(ws_in[i % WS], 16)

            def load_kv(src, i0):
                for r in range(DB):
                    i = i0 + r
                    if i >= KV:
                        sp.wait_ge(*step(f"kt{i - KV}_1" if i - KV < DB else f"ca{i - KV - DB}"))
                    sp.dma_start(kv[i % KV][:], src[0, r].rearrange("(t p) h d -> p t (h d)", p=P)
                                 ).then_inc(kv_in[i % KV], 16)

            sp.wait_ge(*out(last_block, ("ca", H - 1)))
            load_s(0, 2)
            for i in range(2):
                sp.wait_ge(y_out[i].sem, y_out[i].at(last_block, TT // 2 - 1))
            sp.dma_start(xs[:], I["x_sample"].rearrange("b t d -> (b t) d")).then_inc(s_first_in, 16)
            for i, g in enumerate(("g_mix", "g_cross", "g_mlp")):
                sp.dma_start(gains[:, i, :], I[g][0:1, :].broadcast_to([NS, D])).then_inc(s_first_in, 16)
            sp.wait_ge(w_used.sem, w_used.at(last_block, W_TILES["block"] - 1))
            load_s(2, 4)
            sp.dma_start(s0[:], I["state_hgrn"][0].rearrange("b h k v -> k b h v")).then_inc(s0_in, 16)
            sp.dma_start(O[2][0, 0].rearrange("h k v -> k h v"), state[:]).then_inc(s_out, 16)
            load_s(4, 10)
            load_kv(I["cache_mem_k"], 0)
            load_s(10, 11)
            load_kv(I["cache_mem_v"], DB)
            load_s(11, len(chunks))
            sp.wait_ge(s_out, 16)

        @block.gpsimd
        def _(pool):
            pool.sem_inc(w_split.sem, RAW)
            nc.gpsimd.memset(zero[:], 0.0).then_inc(w_rounded, 1)
            pool.wait_ge(w_rounded, 1)
            with pool.Fori(0, (W_TILES["mem"] + NB * W_TILES["block"]) // RING) as g:
                for k in range(RING):
                    s = k % RAW
                    pool.wait_ge(w_in[s].sem, g * (16 * RING // RAW) + 16 * (k // RAW + 1))
                    pool.wait_ge(w_used.sem, g * RING + (k + 1))
                    nc.gpsimd.tensor_tensor(w_hi[:, k, :], w_raw[:, s, :], zero[:].to_broadcast([P, 512]),
                                            ALU.add).then_inc(w_rounded, 1)
                    pool.wait_ge(w_rounded, g * RING + (k + 2))
                    nc.gpsimd.tensor_tensor(w_lo[:, k, :], w_raw[:, s, :], w_hi[:, k, :].bitcast(F32),
                                            ALU.subtract).then_inc(w_split.sem, 1)

        @block.tensor
        def _(pe):
            pe.sem_inc(w_used.sem, RING)
            for h in range(2):
                pe.sem_inc(evacuated[h].sem, 1)

            def begin(pos, job, f=0, needs=()):
                h, use, *_ = jobs.of[pos[0], job]
                last = {h: use - 1}
                for j in needs:
                    hj, uj, *_ = jobs.of[pos[0], j]
                    last[hj] = max(last.get(hj, uj), uj)
                for hj, uj in sorted(last.items()):
                    pe.wait_ge(evacuated[hj].sem, evacuated[hj].at(pos, uj + f * 3))
                return half[h]

            def gemm(pos, job, kind, hi, lo, tiles=4, f=0, needs=()):
                ps = begin(pos, job, f, needs)
                n, t0 = weight_tiles(job), jobs.of[pos[0], job][2]
                for k in range(n):
                    s = (t0 + k) % RING
                    pe.wait_ge(w_split.sem, w_split.at(pos, t0 + k + f * (4 * KD)))
                    for j in range(tiles):
                        col = slice(j * P, j * P + P)
                        if kind == "T":
                            parts = ((w_lo[:, s, col], hi[:, k, :]), (w_hi[:, s, col], lo[:, k, :]),
                                     (w_hi[:, s, col], hi[:, k, :]))
                        else:
                            parts = ((lo[:, k, col], w_hi[:, s, :]), (hi[:, k, col], w_lo[:, s, :]),
                                     (hi[:, k, col], w_hi[:, s, :]))
                        for i, (l, r) in enumerate(parts):
                            m = nc.tensor.matmul(ps[:, j, :], l, r, start=(k == 0 and i == 0),
                                                 stop=(k == n - 1 and i == 2))
                    m.then_inc(w_used.sem, 1)

            def transposes(pos, job, tiles, needs=()):
                ps = begin(pos, job, 0, needs)
                for i, t in enumerate(tiles):
                    m = nc.tensor.transpose(ps[:, i // 4, (i % 4) * P:(i % 4) * P + P], t, ident[:])
                m.then_inc(pe_done.sem, 1)

            def three(out, lhs, rhs, first, last):
                (lh, ll), (rh, rl) = lhs, rhs
                for i, (l, r) in enumerate(((ll, rh), (lh, rl), (lh, rh))):
                    m = nc.tensor.matmul(out, l, r, start=(first and i == 0), stop=(last and i == 2))
                return m

            def norm(pos, tag, nt, x0):
                for t in range(nt):
                    pe.wait_ge(xn_ready.sem, xn_ready.at(pos, x0 + t))
                    transposes(pos, (tag, t), [xn[t % 2][:, k * P:k * P + P] for k in range(KD)])

            pe.wait_ge(consts_in, 16 * n_consts)
            for g in range(H):
                m = nc.tensor.transpose(half[1][:, 0, g * P:g * P + P], ws_raw[:, g, :], ident[:])
            m.then_inc(ws_transposed, 1)
            pe.wait_ge(setup_ready, 1)

            pos = ("mem", 0)
            norm(pos, "nm", MT, 0)
            for c in range(2):
                gemm(pos, ("ck", c), "M", a_hi, a_lo, MT, needs=[("nm", MT - 1)])
                transposes(pos, ("ckt", c), [kn[c][:, t, j * P:j * P + P] for j in range(4) for t in range(MT)],
                           [("ck", c)])
            for c in range(2):
                gemm(pos, ("cv", c), "M", a_hi, a_lo, MT)

            with pe.Fori(0, NB) as b:
                pos = ("block", b)

                def within_chunk(u):
                    c, p = divmod(u, 2)
                    pe.wait_ge(scaled_ready.sem, scaled_ready.at(pos, u))
                    ps = begin(pos, ("lv", u))
                    for j in range(2):
                        tok = slice(c * P, c * P + P)
                        for l in range(LEVELS):
                            lhs, rhs = ((kk[:, 2 * p + j, tok], qq[:, 2 * p + j, tok]) if l == 0 else
                                        [dec[u % 2][:, l - 1, j, :]] * 2)
                            m = nc.tensor.matmul(ps[:, 2 * j + l // 4, (l % 4) * P:(l % 4) * P + P], lhs, rhs,
                                                 start=True, stop=True)
                    m.then_inc(pe_done.sem, 1)

                def rows_and_state(u):
                    c, p = divmod(u, 2)
                    pe.wait_ge(att_ready.sem, att_ready.at(pos, u))
                    ps = begin(pos, ("out", u), 0, [("kt", u), "zi" if u < 2 else ("out", u - 2)])
                    for j in range(2):
                        h = 2 * p + j
                        v = vv[:, c, h * P:h * P + P]
                        o = ps[:, 0, j * P:j * P + P]
                        nc.tensor.matmul(o, att[u % 2][:, j, :], v, start=True, stop=False)
                        nc.tensor.matmul(o, dec[u % 2][:, SLOTS - 2, j, :], state[:, h, :], start=False, stop=True)
                        m = nc.tensor.matmul(ps[:, 1, j * P:j * P + P], kdt[u % 2][:, j, :], v, start=True, stop=True)
                    m.then_inc(pe_done.sem, 1)

                norm(pos, "n1", TT, 0)
                gemm(pos, "zf", "T", a_hi, a_lo, needs=[("n1", TT - 1)])
                gemm(pos, "zq", "T", a_hi, a_lo)
                gemm(pos, "zi", "M", a_hi, a_lo)
                within_chunk(0)
                gemm(pos, "zg", "M", a_hi, a_lo)
                for u in range(UNITS):
                    transposes(pos, ("kt", u), [dec[u % 2][:, SLOTS - 1, j, :] for j in range(2)])
                    if u + 1 < UNITS:
                        within_chunk(u + 1)
                    rows_and_state(u)
                    if u == 1:
                        gemm(pos, "zv", "M", a_hi, a_lo)
                    if u == 3:
                        gemm(pos, "zu", "M", a_hi, a_lo)
                    if u == 5:
                        pe.wait_ge(vn_ready.sem, vn_ready.at(pos, 0))
                        for m2 in range(2):
                            ps = begin(pos, ("mix", m2))
                            for t in range(2):
                                for g in range(H):
                                    col = slice(g * P, g * P + P)
                                    m = nc.tensor.matmul(ps[:, t, col], ws_t[:, g, :], vn[:, 2 * m2 + t, col],
                                                         start=True, stop=True)
                            m.then_inc(pe_done.sem, 1)
                for t in range(TT):
                    pe.wait_ge(mixed_ready.sem, mixed_ready.at(pos, t))
                    transposes(pos, ("ot", t), [vv[:, t, k * P:k * P + P] for k in range(H)]
                               + [uu[:, t, k * P:k * P + P] for k in range(H)])
                for c in range(2):
                    gemm(pos, ("wo", c), "M", a_hi, a_lo, needs=[("ot", TT - 1)])
                norm(pos, "n2", TT, TT)
                for c in range(2):
                    gemm(pos, ("cq", c), "T", a_hi, a_lo, needs=[("n2", TT - 1)])
                for t in range(TT):
                    ps = begin(pos, ("sc", t), 0, [("cq", 1)])
                    q = slice(t * P, t * P + P)
                    for h in range(H):
                        for k in (2 * h, 2 * h + 1):
                            m = three(ps[:, h // 2, (h % 2) * NM:(h % 2) * NM + NM],
                                      (b_hi[:, k, q], b_lo[:, k, q]), (kt_hi[:, k, :], kt_lo[:, k, :]),
                                      k == 2 * h, k == 2 * h + 1)
                    m.then_inc(pe_done.sem, 1)

                def p_transposed(h):
                    if h == 0:
                        pe.wait_ge(p_ready.sem, p_ready.at(pos, TT - 1))
                    transposes(pos, ("pt", h), [pp[:, t, h * NM + m * P:h * NM + m * P + P]
                                                for m in range(MT) for t in range(TT)])

                def attended(h):
                    ps = begin(pos, ("ca", h), 0, [("pt", h)])
                    for dd in range(2):
                        for mm in range(MT):
                            col = slice(h * XD + dd * P, h * XD + dd * P + P)
                            m = three(ps[:, dd, :], (v_hi[:, mm, col], v_lo[:, mm, col]),
                                      (pt_hi[h % 2][:, mm, :], pt_lo[h % 2][:, mm, :]), mm == 0, mm == MT - 1)
                    m.then_inc(pe_done.sem, 1)

                p_transposed(0)
                for h in range(H):
                    if h + 1 < H:
                        p_transposed(h + 1)
                    attended(h)
                for c in range(2):
                    gemm(pos, ("co", c), "M", a_hi, a_lo, needs=[("ca", H - 1)])
                norm(pos, "n3", TT, 2 * TT)

                def down(e, f=0):
                    for c in range(2):
                        gemm(pos, ("dn", e, c), "M", ht_hi[e % 2], ht_lo[e % 2], f=f, needs=[("up", e)])

                gemm(pos, ("up", 0), "T", a_hi, a_lo, needs=[("n3", TT - 1)])
                with pe.Fori(0, 3) as f:
                    for e in range(2):
                        gemm(pos, ("up", e + 1), "T", a_hi, a_lo, f=f)
                        down(e, f)
                gemm(pos, ("up", 7), "T", a_hi, a_lo)
                down(6)
                down(7)

            def gemm_s(i, name, src, b, first=True, last=True):
                pe.wait_ge(ws_in[i % WS], 16 * (i // WS + 1))
                for k in range(KD):
                    m = nc.tensor.matmul(bank(b)[SQ, :], src[:, k, :], w_smp[i % WS][:, k, :],
                                         start=(first and k == 0), stop=(last and k == KD - 1))
                m.then_inc(pe_s.did(name), 1)

            def to_columns(name, b, tiles):
                for i, t in enumerate(tiles):
                    m = nc.tensor.transpose(bank(b)[:, i * NS:i * NS + NS], t, ident[0:NS, 0:NS])
                m.then_inc(pe_s.did(name), 1)

            def tiles_of(t, n=KD):
                return [t[:, k * P:k * P + P] for k in range(n)]

            for h in range(2):
                pe.wait_ge(evacuated[h].sem, evacuated[h].at(last_block, jobs.counts["block"][0] - 1))
            pe.wait_ge(*step("xn1"))
            to_columns("n1", 0, tiles_of(xns))
            pe.wait_ge(*step("xt1"))
            gemm_s(0, "zf", xt, 1)
            gemm_s(1, "zq", xt, 2)
            pe.wait_ge(*step("zf_rows"))
            pe.wait_ge(*step("zq_rows"))
            to_columns("zt", 0, tiles_of(zfq[:, 0, :], H) + tiles_of(zfq[:, 1, :], H))
            gemm_s(2, "zi", xt, 3)
            gemm_s(3, "zg", xt, 4)
            gemm_s(4, "zv", xt, 5)
            pe.wait_ge(*step("scaled"))
            for h in range(H):
                for l in range(SLV):
                    lhs, rhs = (kk_s[:, h, :], qq_s[:, h, :]) if l == 0 else [dec_s[:, l - 1, h, :]] * 2
                    c = (h * SLV + l) * NS
                    m = nc.tensor.matmul(bank(1)[SQ, c:c + NS], lhs, rhs, start=True, stop=True)
            m.then_inc(pe_s.did("lv"), 1)
            for h in range(H):
                m = nc.tensor.transpose(bank(2)[SQ, h * P:h * P + P], dec_s[:, SLV, h, :], ident[:])
            m.then_inc(pe_s.did("kt"), 1)
            pe.wait_ge(s0_in, 16)
            pe.wait_ge(*step("v_rows"))
            pe.wait_ge(*step("att"))
            for h in range(H):
                o = bank(3)[SQ, h * P:h * P + P]
                nc.tensor.matmul(o, att_s[:, h, :], v_s[:, h * P:h * P + P], start=True, stop=False)
                for r in range(DB):
                    m = nc.tensor.matmul(o, of_request(qe_m, h, r), s0[:, r, h, :], start=False, stop=(r == DB - 1))
            m.then_inc(pe_s.did("o"), 1)
            gemm_s(5, "zu", xt, 6)
            pe.wait_ge(*step("vn"))
            for g in range(H):
                m = nc.tensor.matmul(bank(7)[SQ, g * P:g * P + P], ws_s[:, g].rearrange("p b t -> p (b t)"),
                                     vn_s[:, g * P:g * P + P], start=True, stop=True)
            m.then_inc(pe_s.did("mix"), 1)
            pe.wait_ge(*step("mixed"))
            to_columns("ot", 0, tiles_of(o_s, H) + tiles_of(u_s, H))

            def new_tokens(j):
                h, r0 = divmod(j, 2)
                col = slice(h * P, h * P + P)
                if j >= 4:
                    pe.wait_ge(*step(f"new{j - 4}"))
                m = nc.tensor.matmul(bank(4 + j % 4), kd_s[:, col], vm[:, 4 * r0:4 * r0 + 4, col], start=True, stop=True)
                m.then_inc(pe_s.did(f"st{j}"), 1)

            pe.wait_ge(*step("gate"))
            pe.wait_ge(*step("zu_gelu"))
            pe.wait_ge(*step("mixed_cm"))
            pe.wait_ge(*step("kd_rows"))
            pe.wait_ge(*step("vm"))
            for j in range(4):
                new_tokens(j)
            pe.wait_ge(*step("xt_ot"))
            gemm_s(6, "wo0", xt, 1)
            for j in range(4, 8):
                new_tokens(j)
            gemm_s(7, "wo1", xt, 2)
            pe.wait_ge(*step("xn2"))
            to_columns("n2", 0, tiles_of(xns))
            pe.wait_ge(*step("xt2"))
            gemm_s(8, "cq0", xt, 1)
            gemm_s(9, "cq1", xt, 2)
            pe.wait_ge(*step("q_rows0"))
            pe.wait_ge(*step("q_rows1"))
            to_columns("qt", 3, tiles_of(q_s))
            pe.wait_ge(*step("qm"))
            for r in range(DB + 1):
                if r < DB:
                    pe.wait_ge(kv_in[r % KV], 16 * (r // KV + 1))
                    for part in range(2):
                        if r:
                            pe.wait_ge(*step(f"kts{r - 1}_{part}"))
                        for i in range(4):
                            for t in range(MT):
                                d0 = (4 * part + i) * P
                                m = nc.tensor.transpose(bank(4 + 2 * part + i // 2)[:, (i % 2) * NM + t * P:][:, 0:P],
                                                        kv[r % KV][:, t, d0:d0 + P], ident[:])
                        m.then_inc(pe_s.did(f"kt{r}_{part}"), 1)
                if r:
                    pe.wait_ge(*step(f"kts{r - 1}_0"))
                    pe.wait_ge(*step(f"kts{r - 1}_1"))
                    for k in range(KD):
                        m = nc.tensor.matmul(bank(k // 2)[SQ, 0:NM], of_request(qm, k, r - 1),
                                             kts[(r - 1) % 2][:, k, :], start=(r == 1 and k % 2 == 0),
                                             stop=(r == DB and k % 2 == 1))
                    m.then_inc(pe_s.did(f"sc{r - 1}"), 1)
            pe.wait_ge(*step("p_rows"))
            to_columns("pt", 4, tiles_of(q_s))
            pe.wait_ge(*step("pm"))
            for r in range(DB):
                i = DB + r
                pe.wait_ge(kv_in[i % KV], 16 * (i // KV + 1))
                for h in range(H):
                    for t in range(MT):
                        m = nc.tensor.matmul(bank(h)[SQ, 0:XD], of_request(pm, h * MT + t, r),
                                             kv[i % KV][:, t, h * XD:h * XD + XD],
                                             start=(r == 0 and t == 0), stop=(r == DB - 1 and t == MT - 1))
                m.then_inc(pe_s.did(f"ca{r}"), 1)
            pe.wait_ge(*step("ca_rows"))
            to_columns("cat", 4, tiles_of(xns))
            pe.wait_ge(*step("xt_ca"))
            gemm_s(10, "co0", xt, 5)
            gemm_s(11, "co1", xt, 6)
            pe.wait_ge(*step("xn3"))
            to_columns("n3", 0, tiles_of(xns))
            pe.wait_ge(*step("xt3"))
            for e in range(9):
                if e < 8:
                    if e >= 2:
                        pe.wait_ge(*step(f"sq{e - 2}"))
                    gemm_s(12 + e, f"up{e}", xt, 1 + e % 2)
                if e:
                    pe.wait_ge(*step(f"sq{e - 1}"))
                    if e >= 3:
                        pe.wait_ge(*step(f"hts{e - 3}"))
                    to_columns(f"ht{e - 1}", 3 + (e - 1) % 2, tiles_of(relu_s[(e - 1) % 2], 4))
            for r in range(4):
                pe.wait_ge(*step(f"hts{2 * r + 1}"))
                for c in range(2):
                    gemm_s(20 + 2 * r + c, f"dn{r}_{c}", hts[:, r * KD:r * KD + KD], 5 + c, r == 0, r == 3)

        @block.scalar
        def _(act):
            link = Links(act_sem, mem=1, block=6 + UNITS, sample=7)
            tables = nc.scalar.preload_act_table_set

            def rsqrt(pos, i, n):
                tables("natural_log_exp_and_others")
                act.wait_ge(var_ready.sem, var_ready.at(pos, i))
                nc.scalar.activation(lnv[:, 0:n], var[:, 0:n], ACT.Ln).then_inc(act_sem, 1)
                act.wait_ge(act_sem, link.next())
                nc.scalar.activation(y0[:, 0:n], lnv[:, 0:n], ACT.Exp, scale=-0.5).then_inc(rstd0_ready.sem, 1)

            def squares(nt):
                for t in range(nt // 2):
                    ins = nc.scalar.activation(relu[:, 2 * t:2 * t + 2, :].rearrange("p a c -> p (a c)"),
                                               x[:, t, :], ACT.Square, accum_out=ss[:, t:t + 1])
                ins.then_inc(ssq_ready.sem, 1)

            def round_hi(pos, job, dst, src, scale=1.0):
                act.wait_ge(*done(pos, job))
                nc.scalar.activation(dst, src, ACT.Copy, scale=scale).then_inc(hi_ready.sem, 1)

            def norm_hi(pos, tag, nt):
                for t in range(nt):
                    round_hi(pos, (tag, t), a_hi[:, :, t * P:t * P + P], feature_tiles(out_of(pos, (tag, t))))

            tables("natural_log_exp_and_others")
            act.wait_ge(lb_args, 1)
            nc.scalar.activation(lbp[:], lbp[:], ACT.Exp).then_inc(lb_exps, 1)

            pos = ("mem", 0)
            link.start(pos)
            act.wait_ge(consts_in, 16 * n_consts)
            squares(MT)
            rsqrt(pos, 0, MT)
            norm_hi(pos, "nm", MT)
            for c in range(2):
                act.wait_ge(*done(pos, ("ck", c)))
                nc.scalar.copy(kn[c][:], out_of(pos, ("ck", c))[:, 0:MT, :]).then_inc(evacuated_of(pos, ("ck", c)), 1)
                act.wait_ge(*out(pos, ("ck", c)))
                act.dma_start(O[4][0, 0].rearrange("(t p) h d -> p t (h d)", p=P)[:, :, c * 512:c * 512 + 512],
                              kn[c][:]).then_inc(kn_out, 16)
                round_hi(pos, ("ckt", c), kt_hi[:, 4 * c:4 * c + 4, :], feature_tiles(out_of(pos, ("ckt", c)), NM))
            for c in range(2):
                ps = out_of(pos, ("cv", c))[:, 0:MT, :]
                act.wait_ge(*done(pos, ("cv", c)))
                nc.scalar.copy(kn[2 + c][:], ps)
                round_hi(pos, ("cv", c), v_hi[:, :, c * 512:c * 512 + 512], ps)
                act.wait_ge(hi_ready.sem, hi_ready.at(pos, MT + 2 + c))
                act.dma_start(O[5][0, 0].rearrange("(t p) h d -> p t (h d)", p=P)[:, :, c * 512:c * 512 + 512],
                              kn[2 + c][:]).then_inc(kn_out, 16)
            act.wait_ge(kn_out, 64)
            link.end()

            with act.Fori(0, NB) as b:
                pos = ("block", b)
                link.start(pos)

                def decays(u):
                    tables("natural_log_exp_and_others")
                    act.wait_ge(args_ready.sem, args_ready.at(pos, u))
                    nc.scalar.activation(dec[u % 2][:], dec[u % 2][:], ACT.Abs).then_inc(act_sem, 1)
                    act.wait_ge(act_sem, link.next())
                    nc.scalar.activation(dec[u % 2][:], dec[u % 2][:], ACT.Exp, scale=-1.0).then_inc(decays_ready.sem, 1)

                def unit_out(u):
                    c, p = divmod(u, 2)
                    act.wait_ge(*done(pos, ("kt", u)))
                    nc.scalar.copy(
                        kdt[u % 2][:], out_of(pos, ("kt", u))[:, 0, 0:2 * P].rearrange("p (j c) -> p j c", c=P)).then_inc(evacuated_of(pos, ("kt", u)), 1)
                    act.wait_ge(*done(pos, ("out", u)))
                    ps = out_of(pos, ("out", u))
                    nc.scalar.copy(vv[:, c, 2 * p * P:2 * p * P + 2 * P], ps[:, 0, 0:2 * P])
                    for j in range(2):
                        h = 4 * c + 2 * p + j
                        ins = nc.scalar.activation(ps[:, 2, j * P:j * P + P], ps[:, 0, j * P:j * P + P], ACT.Square,
                                                   accum_out=ss[:, h:h + 1])
                    ins.then_inc(o_ready.sem, 1)

                tables("natural_log_exp_and_others")
                for t in range(TT // 2):
                    act.wait_ge(x_in[t].sem, x_in[t].at(pos, 0))
                squares(TT)
                rsqrt(pos, 0, TT)
                norm_hi(pos, "n1", TT)
                tables("sigmoid_and_others")
                act.wait_ge(*done(pos, "zf"))
                nc.scalar.activation(kk[:], out_of(pos, "zf")[:], ACT.Sigmoid, scale=-1.0)
                nc.scalar.activation(bb[:], out_of(pos, "zf")[:], ACT.Sigmoid).then_inc(evacuated_of(pos, "zf"), 1)
                act.wait_ge(*done(pos, "zq"))
                nc.scalar.activation(qq[:], out_of(pos, "zq")[:], ACT.Sigmoid).then_inc(sig_ready.sem, 1)
                tables("natural_log_exp_and_others")
                act.wait_ge(*out(pos, "zf"))
                for h in range(H):
                    ins = nc.scalar.activation(bb[:, h, :], bb[:, h, :], ACT.Ln, scale=oml[:, h:h + 1],
                                               bias=lb[:, h:h + 1])
                ins.then_inc(logf_ready.sem, 1)
                decays(0)
                act.wait_ge(*done(pos, "zi"))
                nc.scalar.copy(vv[:], out_of(pos, "zi")[:]).then_inc(evacuated_of(pos, "zi"), 1)
                decays(1)
                tables("sigmoid_and_others")
                act.wait_ge(*done(pos, "zg"))
                nc.scalar.activation(gate[:], out_of(pos, "zg")[:], ACT.Sigmoid).then_inc(evacuated_of(pos, "zg"), 1)
                for u in range(UNITS):
                    unit_out(u)
                    if u + 2 < UNITS:
                        decays(u + 2)
                    for at, name, dst in ((1, "zv", vn), (3, "zu", uu)):
                        if u == at:
                            tables("gelu_apprx_tanh_and_others")
                            act.wait_ge(*done(pos, name))
                            nc.scalar.activation(dst[:], out_of(pos, name)[:],
                                                                     ACT.Gelu_apprx_tanh).then_inc(evacuated_of(pos, name), 1)
                    if u == 2:
                        rsqrt(pos, 1, TT)
                rsqrt(pos, 2, TT * H)
                for t in range(TT):
                    round_hi(pos, ("ot", t), a_hi[:, :, t * P:t * P + P], feature_tiles(out_of(pos, ("ot", t))))
                act.wait_ge(*out(pos, ("wo", 1)))
                squares(TT)
                rsqrt(pos, 3, TT)
                norm_hi(pos, "n2", TT)
                for c in range(2):
                    round_hi(pos, ("cq", c), b_hi[:, 4 * c:4 * c + 4, :], out_of(pos, ("cq", c))[:], ATT_SCALE)
                for t in range(TT):
                    tables("natural_log_exp_and_others")
                    act.wait_ge(max_ready.sem, max_ready.at(pos, t))
                    ps = out_of(pos, ("sc", t))
                    for h in range(H):
                        ins = nc.scalar.activation(pp[:, t, h * NM:h * NM + NM],
                                                   ps[:, h // 2, (h % 2) * NM:(h % 2) * NM + NM], ACT.Exp,
                                                   bias=mx[:, t, h:h + 1], accum_out=psums[:, t, h:h + 1])
                    ins.then_inc(evacuated_of(pos, ("sc", t)), 1)
                for job in ("pt", 0), ("pt", 1), ("ca", 0), ("pt", 2), ("ca", 1), ("pt", 3), ("ca", 2), ("ca", 3):
                    name, h = job
                    ps = out_of(pos, job)[:, 0:2, :]
                    round_hi(pos, job, pt_hi[h % 2][:] if name == "pt" else a_hi[:, 2 * h:2 * h + 2, :], ps)
                act.wait_ge(*out(pos, ("co", 1)))
                squares(TT)
                rsqrt(pos, 4, TT)
                norm_hi(pos, "n3", TT)

                def relu_square(e, f=0):
                    h, use, t0, last, _ = jobs.of["block", ("up", e)]
                    act.wait_ge(w_used.sem, w_used.at(pos, last + f * (4 * KD)))
                    if e:
                        hb, ub, *_ = jobs.of["block", ("up", e - 1)]
                        act.wait_ge(evacuated[hb].sem, evacuated[hb].at(pos, ub + f * 3))
                    nc.scalar.activation(relu[:], half[h][:], ACT.Relu).then_inc(relu_ready.sem, 1)
                    act.wait_ge(sq_ready.sem, sq_ready.at(pos, e + f * 2))
                    nc.scalar.copy(ht_hi[e % 2][:], relu[:]).then_inc(ht_hi_ready.sem, 1)

                relu_square(0)
                with act.Fori(0, 3) as f:
                    relu_square(1, f)
                    relu_square(2, f)
                relu_square(7)
                act.wait_ge(*out(pos, ("dn", 7, 1)))
                squares(TT)
                rsqrt(pos, 5, TT)
                for t in range(TT):
                    act.wait_ge(xn_ready.sem, xn_ready.at(pos, 3 * TT + t))
                    act.dma_start(O[0][0, bass.ds(b * BT + t * P, P), :], xn[t % 2][:]).then_inc(y_out[t % 2].sem, 16)
                link.end()
            for i in range(2):
                act.wait_ge(y_out[i].sem, y_out[i].at(last_block, TT // 2 - 1))

            link.start(("sample", 0))

            def rsqrt_s(tag, n):
                tables("natural_log_exp_and_others")
                act.wait_ge(*step("var_" + tag))
                nc.scalar.activation(lnv[SQ, 0:n], var[SQ, 0:n], ACT.Ln).then_inc(act_sem, 1)
                act.wait_ge(act_sem, link.next())
                nc.scalar.activation(y0[SQ, 0:n], lnv[SQ, 0:n], ACT.Exp, scale=-0.5).then_inc(act_s.did("rstd_" + tag), 1)

            rsqrt_s("n1", 1)
            for i, n in enumerate(("zf", "zq")):
                act.wait_ge(*step(n))
                nc.scalar.copy(zfq[:, i, :], bank(1 + i)[SQ, :]).then_inc(act_s.did(n + "_rows"), 1)
            tables("sigmoid_and_others")
            act.wait_ge(*step("zt"))
            zt = bank(0)[:, 0:2 * H * NS].rearrange("p (a h s) -> p a h s", a=2, h=H)
            nc.scalar.activation(kk_s[:], zt[:, 0], ACT.Sigmoid, scale=-1.0)
            nc.scalar.activation(bb_s[:], zt[:, 0], ACT.Sigmoid)
            nc.scalar.activation(qq_s[:], zt[:, 1], ACT.Sigmoid).then_inc(act_s.did("sig"), 1)
            act.wait_ge(*step("zi"))
            nc.scalar.copy(v_s[:], bank(3)[SQ, :]).then_inc(act_s.did("v_rows"), 1)
            act.wait_ge(*step("zg"))
            nc.scalar.activation(gate_s[:], bank(4)[SQ, :], ACT.Sigmoid).then_inc(act_s.did("gate"), 1)
            tables("natural_log_exp_and_others")
            act.wait_ge(*step("sig"))
            for h in range(H):
                ins = nc.scalar.activation(bb_s[:, h, :], bb_s[:, h, :], ACT.Ln, scale=oml[:, h:h + 1], bias=lb[:, h:h + 1])
            ins.then_inc(act_s.did("logf"), 1)
            act.wait_ge(*step("args"))
            nc.scalar.activation(dec_s[:], dec_s[:], ACT.Abs).then_inc(act_sem, 1)
            act.wait_ge(act_sem, link.next())
            nc.scalar.activation(dec_s[:], dec_s[:], ACT.Exp, scale=-1.0).then_inc(act_s.did("decays"), 1)
            tables("gelu_apprx_tanh_and_others")
            act.wait_ge(*step("zv"))
            nc.scalar.activation(vn_s[:], bank(5)[SQ, :], ACT.Gelu_apprx_tanh).then_inc(act_s.did("zv_gelu"), 1)
            act.wait_ge(*step("kt"))
            nc.scalar.copy(kd_s[:], bank(2)[SQ, :]).then_inc(act_s.did("kd_rows"), 1)
            act.wait_ge(*step("o"))
            nc.scalar.copy(o_s[:], bank(3)[SQ, :]).then_inc(act_s.did("o_rows"), 1)
            act.wait_ge(*step("zu"))
            nc.scalar.activation(u_s[:], bank(6)[SQ, :], ACT.Gelu_apprx_tanh).then_inc(act_s.did("zu_gelu"), 1)
            rsqrt_s("ln", 1)
            act.wait_ge(*step("vn"))
            act.dma_start(O[6][0].rearrange("b t c -> (b t) c"), vn_s[:]).then_inc(vn_out, 16)
            rsqrt_s("o", H)
            rsqrt_s("n2", 1)
            for c in range(2):
                act.wait_ge(*step(f"cq{c}"))
                nc.scalar.activation(q_s[:, c * 512:c * 512 + 512], bank(1 + c)[SQ, :],
                                                            ACT.Copy, scale=ATT_SCALE).then_inc(act_s.did(f"q_rows{c}"), 1)
            act.wait_ge(*step("new7"))
            act.dma_start(O[3][0].rearrange("b h k v -> k b h v"), s0[:]).then_inc(s_out_done, 16)

            for r in range(DB):
                keys_part(act, r, 0, nc.scalar.copy).then_inc(act_s.did(f"kts{r}_0"), 1)
            tables("natural_log_exp_and_others")
            act.wait_ge(*step("max"))
            for h in range(H):
                ins = nc.scalar.activation(q_s[:, h * NM:h * NM + NM], bank(h)[SQ, 0:NM], ACT.Exp,
                                           bias=mx_s[:, h:h + 1], accum_out=sum_s[:, h:h + 1])
            ins.then_inc(act_s.did("p_exp"), 1)
            act.wait_ge(*step(f"ca{DB - 1}"))
            nc.scalar.copy(xns[:].rearrange("p (h d) -> p h d", h=H), half[0][SQ, :, 0:XD]).then_inc(act_s.did("ca_rows"), 1)
            rsqrt_s("n3", 1)
            for e in range(8):
                act.wait_ge(*step(f"up{e}"))
                if e >= 2:
                    act.wait_ge(*step(f"ht{e - 2}"))
                nc.scalar.activation(relu_s[e % 2][:], bank(1 + e % 2)[SQ, :], ACT.Relu).then_inc(act_s.did(f"relu{e}"), 1)
            rsqrt_s("y", 1)
            act.wait_ge(*step("y"))
            act.dma_start(O[1].rearrange("b t d -> (b t) d"), xns[:]).then_inc(s_out_done, 16)
            act.wait_ge(vn_out, 16)
            act.wait_ge(s_out_done, 32)
            link.end()

        @block.vector
        def _(dve):
            link = Links(dve_sem, mem=5, block=55, sample=35)

            def newton(pos, i, n, inv):
                nc.vector.tensor_scalar(var[:, 0:n], ss[:, 0:n], inv, EPS, ALU.mult, ALU.add).then_inc(var_ready.sem, 1)
                refine(pos, i, n)

            def refine(pos, i, n):
                dve.wait_ge(rstd0_ready.sem, rstd0_ready.at(pos, i))
                nc.vector.scalar_tensor_tensor(yt[:, 0:n], y0[:, 0:n], -0.5, y0[:, 0:n], ALU.mult, ALU.mult).then_inc(dve_sem, 1)
                dve.wait_ge(dve_sem, link.next())
                nc.vector.tensor_tensor(yt[:, 0:n], yt[:, 0:n], var[:, 0:n], ALU.mult).then_inc(dve_sem, 1)
                dve.wait_ge(dve_sem, link.next())
                nc.vector.scalar_tensor_tensor(rstd[:, 0:n], yt[:, 0:n], 1.5, y0[:, 0:n], ALU.add, ALU.mult).then_inc(dve_sem, 1)
                dve.wait_ge(dve_sem, link.next())

            def rest_lo(pos, job, i, dst, hi, src, scale=None):
                dve.wait_ge(hi_ready.sem, hi_ready.at(pos, i))
                if scale is None:
                    ins = nc.vector.tensor_tensor(dst, src, hi.bitcast(F32), ALU.subtract)
                else:
                    ins = nc.vector.scalar_tensor_tensor(dst, src, scale, hi.bitcast(F32), ALU.mult, ALU.subtract)
                ins.then_inc(evacuated_of(pos, job), 1)

            def norm(pos, i, ri, nt, x0, g, tag=None, hi0=0):
                for t in range(nt // 2, nt):
                    ins = nc.vector.tensor_tensor_reduce(out=junk[t - nt // 2][:], in0=x[:, t, :], in1=x[:, t, :], scale=1.0,
                                                         scalar=0.0, op0=ALU.mult, op1=ALU.add,
                                                         accum_out=ss[:, t:t + 1])
                ins.then_inc(dve_sem, 1)
                dve.wait_ge(dve_sem, link.next())
                dve.wait_ge(ssq_ready.sem, ssq_ready.at(pos, i))
                newton(pos, ri, nt, 1.0 / D)
                if g is not None:
                    dve.wait_ge(gain_in.sem, gain_in.at(pos, g))
                for t in range(nt):
                    if t >= 2 and tag:
                        dve.wait_ge(*done(pos, (tag, t - 2)))
                    if tag is None or t < 2:
                        dve.wait_ge(y_out[t % 2].sem, y_out[t % 2].at(pos, t // 2 - 1 if tag is None else
                                          (-1 if tag in ("n1", "n2", "n3") else -1)))
                    nc.vector.scalar_tensor_tensor(xn[t % 2][:], x[:, t, :], rstd[:, t:t + 1], gain[:],
                                                               ALU.mult, ALU.mult).then_inc(xn_ready.sem, 1)
                for t in range(nt if tag else 0):
                    rest_lo(pos, (tag, t), hi0 + t, a_lo[:, :, t * P:t * P + P], a_hi[:, :, t * P:t * P + P],
                            feature_tiles(out_of(pos, (tag, t))))

            pos = ("mem", 0)
            link.start(pos)
            dve.wait_ge(consts_in, 16 * n_consts)
            nc.vector.memset(state[:], 0.0)
            nc.vector.tensor_tensor(lbm[:], lbp[:, 0, :], lbp[:, 1, :], ALU.max).then_inc(dve_sem, 1)
            dve.wait_ge(dve_sem, link.next())
            for r in range(2):
                ins = nc.vector.tensor_tensor(lbp[:, r, :], lbp[:, r, :], lbm[:], ALU.subtract)
            ins.then_inc(lb_args, 1)
            dve.wait_ge(lb_exps, 1)
            nc.vector.tensor_tensor(lbm[:], lbp[:, 0, :], lbp[:, 1, :], ALU.add).then_inc(lb_exps, 1)
            dve.wait_ge(lb_exps, 2)
            nc.vector.reciprocal(lbm[:], lbm[:]).then_inc(lb_exps, 1)
            dve.wait_ge(lb_exps, 3)
            nc.vector.tensor_tensor(lb[:], lbp[:, 0, :], lbm[:], ALU.mult).then_inc(lb_exps, 1)
            dve.wait_ge(lb_exps, 4)
            nc.vector.tensor_scalar(oml[:], lb[:], -1.0, 1.0, ALU.mult, ALU.add).then_inc(lb_exps, 1)
            dve.wait_ge(ws_transposed, 1)
            nc.vector.tensor_tensor(ws_t[:], half[1][:, 0, :].rearrange("p (g c) -> p g c", c=P),
                                    tri[:].to_broadcast([P, H, P]), ALU.mult).then_inc(setup_ready, 1)

            norm(pos, 0, 0, MT, 0, None, "nm", 0)
            for c in range(2):
                s = slice(4 * c, 4 * c + 4)
                rest_lo(pos, ("ckt", c), MT + c, kt_lo[:, s, :], kt_hi[:, s, :],
                        feature_tiles(out_of(pos, ("ckt", c)), NM))
            for c in range(2):
                s = slice(c * 512, c * 512 + 512)
                rest_lo(pos, ("cv", c), MT + 2 + c, v_lo[:, :, s], v_hi[:, :, s], out_of(pos, ("cv", c))[:, 0:MT, :])
            link.end()

            with dve.Fori(0, NB) as b:
                pos = ("block", b)
                link.start(pos)

                def blocks(t, u, w):
                    c, p = divmod(u, 2)
                    return t[:, 2 * p:2 * p + 2, c * P:c * P + P].rearrange("p j (n w) -> p j n w", w=w)

                def args(u):
                    d = dec[u % 2]
                    for l in range(1, LEVELS):
                        w = 1 << l
                        src = blocks(bb, u, w)
                        mid = src[:, :, :, w // 2 - 1:w // 2].to_broadcast([P, 2, P // w, w])
                        nc.vector.tensor_tensor(d[:, l - 1].rearrange("p j (n w) -> p j n w", w=w), src, mid,
                                                ALU.subtract)
                    c, p = divmod(u, 2)
                    src = bb[:, 2 * p:2 * p + 2, c * P:c * P + P]
                    nc.vector.tensor_copy(d[:, SLOTS - 2], src)
                    nc.vector.tensor_tensor(
                        d[:, SLOTS - 1], src[:, :, P - 1:P].to_broadcast([P, 2, P]), src, ALU.subtract).then_inc(args_ready.sem, 1)

                def scaled(u):
                    dve.wait_ge(decays_ready.sem, decays_ready.at(pos, u))
                    d = dec[u % 2]
                    c, p = divmod(u, 2)
                    nc.vector.tensor_copy(e_last[u % 2][:], d[:, SLOTS - 2, :, P - 1]).then_inc(dve_sem, 1)
                    dve.wait_ge(dve_sem, link.next())
                    tok = slice(c * P, c * P + P)
                    for slot, src in ((SLOTS - 2, qq), (SLOTS - 1, kk)):
                        nc.vector.tensor_tensor(d[:, slot], d[:, slot], src[:, 2 * p:2 * p + 2, tok], ALU.mult)
                    for l in range(1, LEVELS):
                        w = 1 << l
                        v = d[:, l - 1].rearrange("p j (n w) -> p j n w", w=w)
                        for part, src in ((slice(0, w // 2), kk), (slice(w // 2, w), qq)):
                            ins = nc.vector.tensor_tensor(v[:, :, :, part], v[:, :, :, part],
                                                          blocks(src, u, w)[:, :, :, part], ALU.mult)
                    ins.then_inc(scaled_ready.sem, 1)

                def attention(u):
                    dve.wait_ge(*done(pos, ("lv", u)))
                    ps = out_of(pos, ("lv", u))
                    for j in range(2):
                        ins = nc.vector.tensor_tensor(mtmp[:], ps[:, 2 * j:2 * j + 2, :].rearrange(
                            "p a (l c) -> p (a l) c", c=P), masks[:], ALU.mult)
                        if j == 1:
                            ins.then_inc(evacuated_of(pos, ("lv", u)), 1)
                            dve.wait_ge(*out(pos, ("lv", u)))
                        else:
                            ins.then_inc(dve_sem, 1)
                            dve.wait_ge(dve_sem, link.next())
                        ins = nc.vector.tensor_reduce(att[u % 2][:, j, :], mtmp[:].rearrange("p l c -> p c l"),
                                                      AX.X, ALU.add)
                        if j == 0:
                            ins.then_inc(dve_sem, 1)
                            dve.wait_ge(dve_sem, link.next())
                    ins.then_inc(att_ready.sem, 1)

                def new_state(u):
                    c, p = divmod(u, 2)
                    dve.wait_ge(*done(pos, ("out", u)))
                    ps = out_of(pos, ("out", u))
                    nc.vector.scalar_tensor_tensor(state[:, 2 * p, :], state[:, 2 * p, :], e_last[u % 2][:, 0:1],
                                                   ps[:, 1, 0:P], ALU.mult, ALU.add)
                    dve.wait_ge(o_ready.sem, o_ready.at(pos, u))
                    nc.vector.scalar_tensor_tensor(
                        state[:, 2 * p + 1, :], state[:, 2 * p + 1, :], e_last[u % 2][:, 1:2], ps[:, 1, P:2 * P],
                        ALU.mult, ALU.add).then_inc(evacuated_of(pos, ("out", u)), 1)

                def add_to_x(job, c, f=0):
                    h, use, t0, last, _ = jobs.of["block", job]
                    dve.wait_ge(w_used.sem, w_used.at(pos, last + f * (4 * KD)))
                    xs = x[:, :, c * 512:c * 512 + 512]
                    nc.vector.tensor_tensor(xs, half[h][:], xs, ALU.add).then_inc(evacuated[h].sem, 1)

                for t in range(TT):
                    dve.wait_ge(x_in[t].sem, x_in[t].at(pos, 0))
                norm(pos, 0, 0, TT, 0, 0, "n1", 0)
                dve.wait_ge(*out(pos, "zf"))
                for h in range(H):
                    nc.vector.tensor_scalar(kk[:, h, :], kk[:, h, :], oml[:, h:h + 1], None, ALU.mult)
                dve.wait_ge(sig_ready.sem, sig_ready.at(pos, 0))
                nc.vector.tensor_tensor(qq[:], qq[:], out_of(pos, "zq")[:], ALU.mult).then_inc(evacuated_of(pos, "zq"), 1)
                dve.wait_ge(logf_ready.sem, logf_ready.at(pos, 0))
                for h in range(H):
                    for c in range(TT):
                        s = bb[:, h, c * P:c * P + P]
                        ins = nc.vector.tensor_tensor_scan(s, ones[:], s, 0.0, ALU.mult, ALU.add)
                ins.then_inc(dve_sem, 1)
                dve.wait_ge(dve_sem, link.next())
                args(0)
                args(1)
                scaled(0)
                scaled(1)
                attention(0)
                for u in range(UNITS):
                    new_state(u)
                    if u + 2 < UNITS:
                        args(u + 2)
                    if u + 1 < UNITS:
                        attention(u + 1)
                    if u + 2 < UNITS:
                        scaled(u + 2)
                    if u == 0:
                        dve.wait_ge(*out(pos, "zg"))
                        nc.vector.tensor_tensor(gate[:], gate[:], hgg_row[:, None, :].to_broadcast([P, TT, HG]),
                                                ALU.mult)
                    if u == 2:
                        dve.wait_ge(*out(pos, "zv"))
                        for t in range(TT):
                            ins = nc.vector.bn_stats(stats[:, t, :], vn[:, t, :])
                        ins.then_inc(dve_sem, 1)
                        dve.wait_ge(dve_sem, link.next())
                        nc.vector.tensor_copy(yt[:, 0:1], stats[:, TT - 1, 0:1])
                        for t in range(TT):
                            ins = nc.vector.bn_aggr(mv[:, t, :], stats[:, t, :])
                        ins.then_inc(dve_sem, 1)
                        dve.wait_ge(dve_sem, link.next())
                        nc.vector.tensor_scalar(var[:, 0:TT], mv[:, :, 1], EPS, None, ALU.add).then_inc(var_ready.sem, 1)
                    if u == 3:
                        refine(pos, 1, TT)
                        for t in range(TT):
                            nc.vector.tensor_scalar(vn[:, t, :], vn[:, t, :], mv[:, t, 0:1], rstd[:, t:t + 1],
                                                    ALU.subtract, ALU.mult)
                        nc.vector.tensor_copy(yt[:, 0:1], rstd[:, 0:1]).then_inc(dve_sem, 1)
                        dve.wait_ge(dve_sem, link.next())
                        nc.vector.tensor_tensor(vn[:], vn[:], lng_row[:, None, :].to_broadcast([P, TT, HG]),
                                                     ALU.mult).then_inc(dve_sem, 1)
                        dve.wait_ge(dve_sem, link.next())
                        nc.vector.tensor_tensor(
                            vn[:], vn[:], lnb_row[:, None, :].to_broadcast([P, TT, HG]), ALU.add).then_inc(vn_ready.sem, 1)
                    if u == 5:
                        dve.wait_ge(*out(pos, "zu"))
                        for m2 in range(2):
                            dve.wait_ge(*done(pos, ("mix", m2)))
                            ps = out_of(pos, ("mix", m2))
                            for t in range(2):
                                for g in range(H):
                                    col = slice(g * P, g * P + P)
                                    ins = nc.vector.scalar_tensor_tensor(
                                        uu[:, 2 * m2 + t, col], ps[:, t, col], bs_col[:, g:g + 1],
                                        uu[:, 2 * m2 + t, col], ALU.add, ALU.mult)
                            ins.then_inc(evacuated_of(pos, ("mix", m2)), 1)
                newton(pos, 2, TT * H, 1.0 / P)
                for t in range(TT):
                    for h in range(H):
                        col = slice(h * P, h * P + P)
                        ins = nc.vector.scalar_tensor_tensor(vv[:, t, col], vv[:, t, col],
                                                             rstd[:, 4 * t + h:4 * t + h + 1], gate[:, t, col],
                                                             ALU.mult, ALU.mult)
                    ins.then_inc(mixed_ready.sem, 1)
                for t in range(TT):
                    rest_lo(pos, ("ot", t), TT + t, a_lo[:, :, t * P:t * P + P], a_hi[:, :, t * P:t * P + P],
                            feature_tiles(out_of(pos, ("ot", t))))
                for t in range(TT):
                    dve.wait_ge(x_in[t].sem, x_in[t].at(pos, 1))
                for c in range(2):
                    add_to_x(("wo", c), c)
                dve.wait_ge(*out(pos, ("wo", 1)))
                norm(pos, 1, 3, TT, TT, 1, "n2", 2 * TT)
                for c in range(2):
                    rest_lo(pos, ("cq", c), 3 * TT + c, b_lo[:, 4 * c:4 * c + 4, :], b_hi[:, 4 * c:4 * c + 4, :],
                            out_of(pos, ("cq", c))[:], ATT_SCALE)
                for t in range(TT + 1):
                    if t < TT:
                        dve.wait_ge(*done(pos, ("sc", t)))
                        nc.vector.tensor_reduce(
                            mx[:, t, :], out_of(pos, ("sc", t))[:, 0:2, :].rearrange("p a (h m) -> p (a h) m", m=NM),
                            AX.X, ALU.max, negate=True).then_inc(max_ready.sem, 1)
                    if t:
                        dve.wait_ge(*out(pos, ("sc", t - 1)))
                        nc.vector.reciprocal(rinv[:, t - 1, :], psums[:, t - 1, :]).then_inc(dve_sem, 1)
                        dve.wait_ge(dve_sem, link.next())
                        pv = pp[:, t - 1, :].rearrange("p (h m) -> p h m", m=NM)
                        nc.vector.tensor_tensor(pv, pv, rinv[:, t - 1, :, None].to_broadcast([P, H, NM]),
                                                           ALU.mult).then_inc(p_ready.sem, 1)
                i0 = 3 * TT + 2
                for job in ("pt", 0), ("pt", 1), ("ca", 0), ("pt", 2), ("ca", 1), ("pt", 3), ("ca", 2), ("ca", 3):
                    name, h = job
                    s = slice(2 * h, 2 * h + 2)
                    rest_lo(pos, job, i0, pt_lo[h % 2][:] if name == "pt" else a_lo[:, s, :],
                            pt_hi[h % 2][:] if name == "pt" else a_hi[:, s, :], out_of(pos, job)[:, 0:2, :])
                    i0 += 1
                for c in range(2):
                    add_to_x(("co", c), c)
                dve.wait_ge(*out(pos, ("co", 1)))
                norm(pos, 2, 4, TT, 2 * TT, 2, "n3", i0)

                def relu_square(e, f=0):
                    h, *_ = jobs.of["block", ("up", e)]
                    dve.wait_ge(relu_ready.sem, relu_ready.at(pos, e + f * 2))
                    nc.vector.tensor_tensor(relu[:], relu[:], half[h][:], ALU.mult).then_inc(sq_ready.sem, 1)
                    dve.wait_ge(ht_hi_ready.sem, ht_hi_ready.at(pos, e + f * 2))
                    nc.vector.tensor_tensor(ht_lo[e % 2][:], relu[:], ht_hi[e % 2][:].bitcast(F32),
                                                            ALU.subtract).then_inc(evacuated[h].sem, 1)

                relu_square(0)
                with dve.Fori(0, 3) as f:
                    for e in range(2):
                        relu_square(e + 1, f)
                        for c in range(2):
                            add_to_x(("dn", e, c), c, f)
                relu_square(7)
                for e in (6, 7):
                    for c in range(2):
                        add_to_x(("dn", e, c), c)
                dve.wait_ge(*out(pos, ("dn", 7, 1)))
                norm(pos, 3, 5, TT, 3 * TT, 3)
                link.end()

            link.start(("sample", 0))

            def newton_s(tag, n, inv):
                if inv:
                    nc.vector.tensor_scalar(var[SQ, 0:n], ss[SQ, 0:n], inv, EPS, ALU.mult, ALU.add).then_inc(dve_s.did("var_" + tag), 1)
                dve.wait_ge(*step("rstd_" + tag))
                nc.vector.scalar_tensor_tensor(yt[SQ, 0:n], y0[SQ, 0:n], -0.5, y0[SQ, 0:n], ALU.mult, ALU.mult).then_inc(dve_sem, 1)
                dve.wait_ge(dve_sem, link.next())
                nc.vector.tensor_tensor(yt[SQ, 0:n], yt[SQ, 0:n], var[SQ, 0:n], ALU.mult).then_inc(dve_sem, 1)
                dve.wait_ge(dve_sem, link.next())
                nc.vector.scalar_tensor_tensor(rstd[SQ, 0:n], yt[SQ, 0:n], 1.5, y0[SQ, 0:n], ALU.add, ALU.mult).then_inc(dve_sem, 1)
                dve.wait_ge(dve_sem, link.next())

            def norm_s(tag, name, g):
                nc.vector.tensor_tensor_reduce(out=xns[:], in0=xs[:], in1=xs[:], scale=1.0, scalar=0.0,
                                                    op0=ALU.mult, op1=ALU.add, accum_out=ss[SQ, 0:1]).then_inc(dve_sem, 1)
                dve.wait_ge(dve_sem, link.next())
                newton_s(tag, 1, 1.0 / D)
                nc.vector.scalar_tensor_tensor(xns[:], xs[:], rstd[SQ, 0:1], g, ALU.mult, ALU.mult).then_inc(dve_s.did(name), 1)

            def columns(job, name, b, n=KD, dst=xt):
                dve.wait_ge(*step(job))
                nc.vector.tensor_copy(dst[:, 0:n, :], bank(b)[:, 0:n * NS].rearrange(
                    "p (k s) -> p k s", s=NS)).then_inc(dve_s.did(name), 1)

            def add_to_xs(job, name, b, c):
                dve.wait_ge(*step(job))
                col = slice(c * 512, c * 512 + 512)
                nc.vector.tensor_tensor(xs[:, col], bank(b)[SQ, :], xs[:, col], ALU.add).then_inc(dve_s.did(name), 1)

            def requests(t):
                return t.rearrange("p h (b t) -> p (h b) t", t=DS)

            dve.wait_ge(s_first_in, 64)
            norm_s("n1", "xn1", gains[:, 0, :])
            dve.wait_ge(s_consts_in, 16 * (2 + 5 * DB))
            nc.vector.memset(qe_m[:], 0.0)
            nc.vector.tensor_tensor(ws_s[:], w4[:, :, None, :].to_broadcast([NS, H, DB, DS]),
                                    tri_own[:, None, :, :].to_broadcast([NS, H, DB, DS]), ALU.mult)
            columns("n1", "xt1", 0)
            dve.wait_ge(*step("sig"))
            for h in range(H):
                nc.vector.tensor_scalar(kk_s[:, h, :], kk_s[:, h, :], oml[:, h:h + 1], None, ALU.mult)
            nc.vector.tensor_tensor(qq_s[:], qq_s[:], bank(0)[:, H * NS:2 * H * NS].rearrange(
                "p (h s) -> p h s", s=NS), ALU.mult).then_inc(dve_s.did("qq"), 1)
            dve.wait_ge(*step("logf"))
            lf = requests(bb_s[:])
            for t in range(1, DS):
                nc.vector.tensor_tensor(lf[:, :, t], lf[:, :, t], lf[:, :, t - 1], ALU.add).then_inc(dve_sem, 1)
                dve.wait_ge(dve_sem, link.next())
            for l in range(1, SLV):
                w = 1 << l
                src, dst = (t.rearrange("p h (n w) -> p (h n) w", w=w) for t in (bb_s[:], dec_s[:, l - 1]))
                nc.vector.tensor_tensor(dst, src, src[:, :, w // 2 - 1:w // 2].to_broadcast([P, H * NS // w, w]),
                                        ALU.subtract)
            nc.vector.tensor_copy(dec_s[:, SLV - 1], bb_s[:])
            nc.vector.tensor_tensor(requests(dec_s[:, SLV]), lf[:, :, DS - 1:DS].to_broadcast(
                [P, H * DB, DS]), lf, ALU.subtract).then_inc(dve_s.did("args"), 1)
            dve.wait_ge(*step("decays"))
            for l in range(1, SLV):
                w = 1 << l
                v, k, q = (t.rearrange("p h (n w) -> p (h n) w", w=w) for t in (dec_s[:, l - 1], kk_s[:], qq_s[:]))
                nc.vector.tensor_tensor(v[:, :, 0:w // 2], v[:, :, 0:w // 2], k[:, :, 0:w // 2], ALU.mult)
                nc.vector.tensor_tensor(v[:, :, w // 2:w], v[:, :, w // 2:w], q[:, :, w // 2:w], ALU.mult)
            for h in range(H):
                nc.vector.tensor_copy(el_s[:, h, :], dec_s[:, SLV - 1, h].rearrange("p (b t) -> p b t", t=DS)[:, :, DS - 1])
                nc.vector.tensor_tensor(qe_m[:, h, :, 0:DS], dec_s[:, SLV - 1, h].rearrange("p (b t) -> p b t", t=DS),
                                        qq_s[:, h].rearrange("p (b t) -> p b t", t=DS), ALU.mult)
            nc.vector.tensor_tensor(dec_s[:, SLV], dec_s[:, SLV], kk_s[:], ALU.mult).then_inc(dve_s.did("scaled"), 1)
            dve.wait_ge(*step("v_rows"))
            nc.vector.tensor_tensor(vm[:], v_s[:, None, :].to_broadcast([NS, DB, HG]),
                                                   own[:, :, None].to_broadcast([NS, DB, HG]), ALU.mult).then_inc(dve_s.did("vm"), 1)
            dve.wait_ge(*step("gate"))
            nc.vector.tensor_tensor(gate_s[:], gate_s[:], hgg_row[SQ, :], ALU.mult)
            dve.wait_ge(*step("lv"))
            nc.vector.tensor_tensor(tmp_s[:], bank(1)[SQ, 0:H * SLV * NS].rearrange("p (h l s) -> p h l s", l=SLV, s=NS),
                                         masks[SQ, None, 0:SLV, 0:NS].to_broadcast([NS, H, SLV, NS]), ALU.mult).then_inc(dve_sem, 1)
            dve.wait_ge(dve_sem, link.next())
            nc.vector.tensor_reduce(att_s[:], tmp_s[:].rearrange("p h l s -> p h s l"), AX.X, ALU.add).then_inc(dve_s.did("att"), 1)
            dve.wait_ge(*step("zv_gelu"))
            nc.vector.bn_stats(st_s[:], vn_s[:]).then_inc(dve_sem, 1)
            dve.wait_ge(dve_sem, link.next())
            nc.vector.tensor_copy(yt[SQ, 0:1], st_s[:, 0:1])
            nc.vector.bn_aggr(mv_s[:], st_s[:]).then_inc(dve_sem, 1)
            dve.wait_ge(dve_sem, link.next())
            nc.vector.tensor_scalar(var[SQ, 0:1], mv_s[:, 1:2], EPS, None, ALU.add).then_inc(dve_s.did("var_ln"), 1)
            newton_s("ln", 1, None)
            nc.vector.tensor_scalar(vn_s[:], vn_s[:], mv_s[:, 0:1], rstd[SQ, 0:1], ALU.subtract, ALU.mult).then_inc(dve_sem, 1)
            dve.wait_ge(dve_sem, link.next())
            nc.vector.tensor_tensor(vn_s[:], vn_s[:], lng_row[SQ, :], ALU.mult).then_inc(dve_sem, 1)
            dve.wait_ge(dve_sem, link.next())
            nc.vector.tensor_tensor(vn_s[:], vn_s[:], lnb_row[SQ, :], ALU.add).then_inc(dve_s.did("vn"), 1)
            dve.wait_ge(*step("o_rows"))
            nc.vector.tensor_tensor(xns[:, 0:HG], o_s[:], o_s[:], ALU.mult).then_inc(dve_sem, 1)
            dve.wait_ge(dve_sem, link.next())
            nc.vector.tensor_reduce(ss[SQ, 0:H], xns[:, 0:HG].rearrange("p (h c) -> p h c", h=H), AX.X, ALU.add).then_inc(dve_sem, 1)
            dve.wait_ge(dve_sem, link.next())
            newton_s("o", H, 1.0 / P)
            dve.wait_ge(*step("mix"))
            dve.wait_ge(*step("zu_gelu"))
            for g in range(H):
                col = slice(g * P, g * P + P)
                ins = nc.vector.scalar_tensor_tensor(u_s[:, col], bank(7)[SQ, col], b4[:, g:g + 1], u_s[:, col],
                                                     ALU.add, ALU.mult)
            ins.then_inc(dve_s.did("mixed_cm"), 1)
            for h in range(H):
                col = slice(h * P, h * P + P)
                ins = nc.vector.scalar_tensor_tensor(o_s[:, col], o_s[:, col], rstd[SQ, h:h + 1], gate_s[:, col],
                                                     ALU.mult, ALU.mult)
            ins.then_inc(dve_s.did("mixed"), 1)
            columns("ot", "xt_ot", 0)
            for h in range(H):
                ins = nc.vector.tensor_tensor(s0[:, :, h, :], s0[:, :, h, :], el_s[:, h, :, None].to_broadcast([P, DB, P]),
                                              ALU.mult)
            ins.then_inc(dve_sem, 1)
            dve.wait_ge(dve_sem, link.next())
            for j in range(8):
                h, r0 = divmod(j, 2)
                dve.wait_ge(*step(f"st{j}"))
                s = s0[:, 4 * r0:4 * r0 + 4, h, :]
                nc.vector.tensor_tensor(s, bank(4 + j % 4).rearrange("p (b v) -> p b v", v=P), s,
                                                            ALU.add).then_inc(dve_s.did(f"new{j}"), 1)
                if j == 3:
                    add_to_xs("wo0", "x_wo0", 1, 0)
            add_to_xs("wo1", "x_wo1", 2, 1)
            dve.wait_ge(*step("x_wo1"))
            norm_s("n2", "xn2", gains[:, 1, :])
            columns("n2", "xt2", 0)
            dve.wait_ge(vn_out, 16)
            nc.vector.memset(qm[:], 0.0)
            nc.vector.memset(pm[:], 0.0).then_inc(dve_sem, 1)
            dve.wait_ge(dve_sem, link.next())

            def own_tokens(job, name, b, dst):
                dve.wait_ge(*step(job))
                for k in range(KD):
                    ins = nc.vector.tensor_copy(dst[:, k, :, 0:DS], bank(b)[:, k * NS:k * NS + NS].rearrange(
                        "p (b t) -> p b t", t=DS))
                ins.then_inc(dve_s.did(name), 1)

            own_tokens("qt", "qm", 3, qm)
            for r in range(DB):
                keys_part(dve, r, 1, nc.vector.tensor_copy).then_inc(dve_s.did(f"kts{r}_1"), 1)
            dve.wait_ge(*step(f"sc{DB - 1}"))
            nc.vector.tensor_reduce(mx_s[:], half[0][SQ, :, 0:NM], AX.X, ALU.max, negate=True).then_inc(dve_s.did("max"), 1)
            dve.wait_ge(*step("p_exp"))
            nc.vector.reciprocal(rinv_s[:], sum_s[:]).then_inc(dve_sem, 1)
            dve.wait_ge(dve_sem, link.next())
            pv = q_s[:].rearrange("p (h m) -> p h m", h=H)
            nc.vector.tensor_tensor(pv, pv, rinv_s[:, :, None].to_broadcast([NS, H, NM]), ALU.mult).then_inc(dve_s.did("p_rows"), 1)
            own_tokens("pt", "pm", 4, pm)
            columns("cat", "xt_ca", 4)
            for c in range(2):
                add_to_xs(f"co{c}", f"x_co{c}", 5 + c, c)
            dve.wait_ge(*step("x_co1"))
            norm_s("n3", "xn3", gains[:, 2, :])
            columns("n3", "xt3", 0)
            for e in range(9):
                if e < 8:
                    dve.wait_ge(*step(f"relu{e}"))
                    nc.vector.tensor_tensor(relu_s[e % 2][:], relu_s[e % 2][:], bank(1 + e % 2)[SQ, :],
                                                              ALU.mult).then_inc(dve_s.did(f"sq{e}"), 1)
                if e:
                    columns(f"ht{e - 1}", f"hts{e - 1}", 3 + (e - 1) % 2, 4, hts[:, 4 * (e - 1):4 * e, :])
            for c in range(2):
                add_to_xs(f"dn3_{c}", f"x_dn{c}", 5 + c, c)
            dve.wait_ge(*step("x_dn1"))
            norm_s("y", "y", gain[SQ, :])
            link.end()


_INS = ["x_prompt", "x_sample", "mem_prompt", "state_hgrn", "cache_mem_k", "cache_mem_v", "lb_param", "g_mix", "w_in",
        "hg_norm_g", "ln_v_g", "ln_v_b", "w_s", "b_s", "w_out", "g_cross", "g_mem", "w_cq", "w_ck", "w_cv", "w_co",
        "g_mlp", "w_up", "w_down", "g_final"]
_OUTS = [(1, 2048, 1024), (8, 4, 1024), (1, 1, 4, 128, 128), (1, 8, 4, 128, 128), (1, 1, 256, 4, 256),
         (1, 1, 256, 4, 256), (1, 8, 4, 512)]


def kernel(**inputs):
    import numpy as _np
    import concourse.bacc as _bacc
    from concourse import mybir as _mybir
    from concourse.bass_utils import run_bass_kernel_spmd as _run

    s, t = _np.arange(P)[:, None], _np.arange(P)[None, :]
    masks = [s == t]
    for l in range(1, LEVELS):
        w = 1 << l
        masks.append((s // w == t // w) & (s % w < w // 2) & (t % w >= w // 2))
    consts = {"c_ident": s == t, "c_ones": s < P + t, "c_tri": s <= t, "c_masks": _np.stack(masks, 1)}

    s, t = _np.arange(NS)[:, None], _np.arange(NS)[None, :]
    consts["c_own"] = s // DS == _np.arange(DB)[None, :]
    consts["c_tri_own"] = ((s // DS == t // DS) & (s <= t)).reshape(NS, DB, DS)

    nc = _bacc.Bacc("TRN2", target_bir_lowering=False, num_devices=1)
    arrays, I = {}, {}
    for name in _INS + list(consts):
        a = _np.ascontiguousarray(inputs[name] if name in inputs else consts[name].astype(_np.float32))
        arrays[f"in_{name}"] = a
        I[name] = nc.dram_tensor(f"in_{name}", a.shape, _mybir.dt.from_np(a.dtype), kind="ExternalInput").ap()
    O = [nc.dram_tensor(f"out_{i}", shape, F32, kind="ExternalOutput").ap() for i, shape in enumerate(_OUTS)]
    program(nc, I, O)
    r = _run(nc, [arrays], core_ids=[0])
    return tuple(r.results[0][f"out_{i}"] for i in range(len(_OUTS)))
```

```python
import concourse.bass as bass
from concourse import mybir
from contextlib import ExitStack

F32 = mybir.dt.float32
F32R = mybir.dt.float32r
ACT = mybir.ActivationFunctionType
ALU = mybir.AluOpType
AX = mybir.AxisListType

P = 128
D = 1024
KD = D // P
SEQ = 2048
BT = 512
NB = SEQ // BT
TT = BT // P
HG = 512
H = 4
FF = 4096
NM = 256
MT = NM // P
XD = 256
DB, DS = 8, 4
NS = DB * DS
EPS = 1e-6
RING = 8
RAW = 4
LEVELS = 8
SLOTS = LEVELS - 1 + 2
UNITS = TT * 2
ATT_SCALE = XD ** -0.5

W_TILES = {"mem": 4 * KD, "block": 28 * KD, "last": 28 * KD}
SWAP = 4
SG = NS + DS
SLV = 3
WS = 4
KV = 4

PE_STEPS = (["n1", "zf", "zq", "zt", "zi", "zg", "zv", "lv", "kt", "o", "zu", "mix", "ot"]
            + [f"st{j}" for j in range(4)] + ["wo0"] + [f"st{j}" for j in range(4, 8)] + ["wo1"]
            + ["n2", "cq0", "cq1", "qt"]
            + [s for b in range(DB + 1) for s in ([f"kt{b}_0", f"kt{b}_1"] if b < DB else [])
               + ([f"sc{b - 1}"] if b else [])]
            + ["pt"] + [f"ca{b}" for b in range(DB)] + ["cat", "co0", "co1", "n3"]
            + [s for e in range(9) for s in ([f"up{e}"] if e < 8 else []) + ([f"ht{e - 1}"] if e else [])]
            + [f"dn{r}_{c}" for r in range(4) for c in range(2)])
ACT_STEPS = (["rstd_n1", "zf_rows", "zq_rows", "sig", "v_rows", "gate", "logf", "decays", "zv_gelu", "kd_rows", "o_rows",
              "zu_gelu", "rstd_ln", "rstd_o", "rstd_n2", "q_rows0", "q_rows1"]
             + [f"kts{b}_0" for b in range(DB)] + ["p_exp"] + ["ca_rows", "rstd_n3"] + [f"relu{e}" for e in range(8)]
             + ["rstd_y"])
DVE_STEPS = (["var_n1", "xn1", "xt1", "qq", "args", "scaled", "vm", "att", "var_ln", "vn", "var_o", "mixed_cm", "mixed",
              "xt_ot"]
             + [f"new{j}" for j in range(4)] + ["x_wo0"] + [f"new{j}" for j in range(4, 8)] + ["x_wo1"]
             + ["var_n2", "xn2", "xt2", "qm"] + [f"kts{b}_1" for b in range(DB)]
             + ["max", "p_rows", "pm", "xt_ca", "x_co0", "x_co1", "var_n3", "xn3", "xt3"]
             + [s for e in range(9) for s in ([f"sq{e}"] if e < 8 else []) + ([f"hts{e - 1}"] if e else [])]
             + ["x_dn0", "x_dn1", "var_y", "y"])


PHASES = (("mem", 1), ("block", NB - 1), ("last", 1), ("sample", 1))


def before(per, pos):
    phase, b = pos
    n = 0
    for name, times in PHASES:
        if name == phase:
            return b * per[name], n
        n += times * per[name]


class Event:

    def __init__(self, sem, mem=0, block=0, last=None, step=1, prime=0):
        self.sem, self.step, self.prime = sem, step, prime
        self.names = {"mem": mem, "block": block, "last": block if last is None else last}
        self.per = {k: v if isinstance(v, int) else len(v) for k, v in self.names.items()}

    def at(self, pos, i):
        if isinstance(i, (str, tuple)):
            i = self.names[pos[0]].index(i)
        turns, n = before(self.per, pos)
        return turns * self.step + (i + (n + 1)) * self.step + self.prime


class Links:

    def __init__(self, sem, **per):
        self.sem, self.per = sem, per
        self.n, self.pos = 0, ("mem", 0)

    def start(self, pos):
        self.n, self.pos = 0, pos

    def next(self):
        self.n += 1
        turns, n = before(self.per, self.pos)
        return turns + (n + self.n)

    def end(self):
        want = self.per[self.pos[0]]
        assert self.n == want, (self.sem, self.pos[0], self.n, want)


def block_jobs(last):
    jobs = [(1, "zf"), (0, "zi"), (1, "zq"), (1, "kt"), (0, "zv"), (0, "zg")]
    for u in range(UNITS):
        h = 1 if u < SWAP else 0
        jobs += [(h, ("lv", u))] + {6: [(1, "zu")], 7: [(1, "mix")]}.get(u, []) + [(h, ("out", u))]
    jobs += [(1, "otu"), (0, "oto"), (1, ("wo", 0)), (1, ("n2", 0)), (0, ("wo", 1))]
    jobs += [(0, ("n2", 1)), (1, ("cq", 0)), (0, ("cq", 1))]
    small = [("sc", t) for t in range(TT)]
    small += [("pt", 0), ("pt", 1), ("ca", 0), ("pt", 2), ("ca", 1), ("pt", 3), ("ca", 2), ("ca", 3)]
    jobs += [((i + 1) % 2, job) for i, job in enumerate(small)]
    jobs += [(1, ("co", 0)), (1, ("n3", 0)), (0, ("co", 1)), (0, ("n3", 1)), (1, ("up", 0))]
    mlp = []
    for e in range(FF // 512 - 1):
        mlp += [("up", e + 1), ("dn", e, 0), ("dn", e, 1)]
    mlp += [("dn", FF // 512 - 1, 0), ("dn", FF // 512 - 1, 1)]
    for i, job in enumerate(mlp):
        if not last and job in (("dn", 6, 1), ("dn", 7, 1)):
            jobs += [(1, ("n1", job[1] - 6))]
        jobs += [(i % 2, job)]
    return jobs


def mem_jobs():
    jobs = [("nm", t) for t in range(MT)]
    for c in range(2):
        jobs += [("ck", c), ("ckt", c)]
    jobs += [("cv", 0), ("cv", 1), ("n1", 0), ("n1", 1)]
    return [(i % 2, job) for i, job in enumerate(jobs)]


def weight_tiles(job):
    name = job if isinstance(job, str) else job[0]
    if name in ("zf", "zq", "zi", "zg", "zv", "zu", "wo", "cq", "co", "up", "ck", "cv"):
        return KD
    return 4 if name == "dn" else 0


class Steps:

    def __init__(self, sem, names):
        self.sem, self.names, self.n = sem, names, 0

    def did(self, name):
        assert self.names[self.n] == name, (self.names[self.n], name)
        self.n += 1
        return self.sem


class Jobs:

    def __init__(self):
        self.lists = {"mem": mem_jobs(), "block": block_jobs(False), "last": block_jobs(True)}
        self.of, self.counts = {}, {}
        for phase, jobs in self.lists.items():
            tiles = done = 0
            uses = [0, 0]
            for h, job in jobs:
                n = weight_tiles(job)
                self.of[phase, job] = (h, uses[h], tiles, tiles + n - 1, done)
                uses[h] += 1
                tiles += n
                done += not n
            assert tiles == W_TILES[phase], (phase, tiles)
            self.counts[phase] = (uses[0], uses[1], tiles, done)


def program(nc, I, O):
    jobs = Jobs()
    ctx = ExitStack()

    def sb(name, shape, dt=F32, stack=ctx):
        return stack.enter_context(nc.sbuf_tensor(name, shape, dt))

    def sem(name):
        return ctx.enter_context(nc.semaphore(name))

    def event(name, mem=0, block=0, last=None, step=1, prime=0):
        return Event(sem(name), mem, block, last, step, prime)

    with ctx:
        w_raw = sb("w_raw", [P, RAW, 512])
        with ExitStack() as z:
            w_smp = [sb(f"w_smp{i}", [P, KD, 512], F32, z) for i in (2, 3)]
        w_hi = sb("w_hi", [P, RING, 512], F32R)
        w_lo = sb("w_lo", [P, RING, 512], F32R)
        zero = sb("zero", [P, 1])
        ident = sb("ident", [P, P])
        ones = sb("ones", [P, P])
        masks = sb("masks", [P, LEVELS, P])
        ws_t = sb("ws_t", [P, H, P])
        hgg_row = sb("hgg_row", [P, HG])
        lng_row = sb("lng_row", [P, HG])
        lnb_row = sb("lnb_row", [P, HG])
        bs_col = sb("bs_col", [P, H])
        lb = sb("lb", [P, H])
        oml = sb("oml", [P, H])
        gain = sb("gain", [P, D])
        ss = sb("ss", [P, 37])
        var = sb("var", [P, 37])
        lnv = sb("lnv", [P, 37])
        y0 = sb("y0", [P, 37])
        yt = sb("yt", [P, 37])
        rstd = sb("rstd", [P, 37])
        state = sb("state", [P, H, P])
        own = sb("own", [NS, DB])
        tri_own = sb("tri_own", [NS, DB, DS])
        w4 = sb("w4", [NS, H, DS])
        b4 = sb("b4", [NS, H])
        with ExitStack() as z:
            w_smp = [sb(f"w_smp{i}", [P, KD, 512], F32, z) for i in (0, 1)] + w_smp
        kt_hi = sb("kt_hi", [P, KD, NM], F32R)
        kt_lo = sb("kt_lo", [P, KD, NM], F32R)
        v_hi = sb("v_hi", [P, MT, D], F32R)
        v_lo = sb("v_lo", [P, MT, D], F32R)
        with ExitStack() as z:
            kv = [sb(f"kv{i}", [P, MT, D], F32, z) for i in range(KV)]
        a_hi = sb("a_hi", [P, KD, BT], F32R)
        a_lo = sb("a_lo", [P, KD, BT], F32R)
        with ExitStack() as y:
            s0 = sb("s0", [P, DB, H, P], F32, y)
            gains = sb("gains", [NS, 3, D], F32, y)
            xs = sb("xs", [NS, D], F32, y)
            xns = sb("xns", [NS, D], F32, y)
            xt = sb("xt", [P, KD, NS], F32, y)
            with ExitStack() as z:
                vm = sb("vm", [NS, DB, HG], F32, z)
                zfq = sb("zfq", [NS, 2, HG], F32, z)
                v_s, gate_s, vn_s, o_s = (sb(n, [NS, HG], F32, z) for n in ("v_s", "gate_s", "vn_s", "o_s"))
                u_s = sb("u_s", [NS, HG], F32, z)
                kk_s, qq_s, bb_s = (sb(n, [P, H, NS], F32, z) for n in ("kk_s", "qq_s", "bb_s"))
                dec_s = sb("dec_s", [P, SLV + 1, H, NS], F32, z)
                qe_m = sb("qe_m", [P, H, DB, SG], F32, z)
                el_s = sb("el_s", [P, H, DB], F32, z)
                tmp_s = sb("tmp_s", [NS, H, SLV, NS], F32, z)
                att_s = sb("att_s", [NS, H, NS], F32, z)
                kd_s = sb("kd_s", [NS, HG], F32, z)
                ws_s = sb("ws_s", [NS, H, DB, DS], F32, z)
                st_s = sb("st_s", [NS, 6], F32, z)
                mv_s = sb("mv_s", [NS, 2], F32, z)
            with ExitStack() as z:
                kts = [sb(f"kts{i}", [P, KD, NM], F32, z) for i in range(2)]
                qm = sb("qm", [P, KD, DB, SG], F32, z)
                pm = sb("pm", [P, KD, DB, SG], F32, z)
                q_s = sb("q_s", [NS, D], F32, z)
                mx_s, sum_s, rinv_s = (sb(n, [NS, H], F32, z) for n in ("mx_s", "sum_s", "rinv_s"))
            with ExitStack() as z:
                relu_s = [sb(f"relu_s{i}", [NS, 512], F32, z) for i in range(2)]
                hts = sb("hts", [P, FF // P, NS], F32, z)
        with ExitStack() as z:
            x = sb("x", [P, TT, D], F32, z)
        with ExitStack() as z:
            kk = sb("kk", [P, H, BT], F32, z)
            qq = sb("qq", [P, H, BT], F32, z)
        sb("zone_x", [P, TT, D])
        with ExitStack() as z:
            bb = sb("bb", [P, H, BT], F32, z)
            vv = sb("vv", [P, TT, HG], F32, z)
            gate = sb("gate", [P, TT, HG], F32, z)
            vn = sb("vn", [P, TT, HG], F32, z)
            uu = sb("uu", [P, TT, HG], F32, z)
            lvl = [sb(f"lvl{i}", [P, LEVELS - 1, 2, P], F32, z) for i in range(2)]
            ends = [sb(f"ends{i}", [P, 2, 2, P], F32, z) for i in range(3)]
            att = sb("att", [P, 2, P], F32, z)
            kdt = sb("kdt", [P, 2, P], F32, z)
            added = [sb(f"added{i}", [P, 2, P], F32, z) for i in range(2)]
            osq = sb("osq", [P, 2, P], F32, z)
            e_last = [sb(f"e_last{i}", [P, 2], F32, z) for i in range(3)]
            stats = sb("stats", [P, TT, 6], F32, z)
            mv = sb("mv", [P, TT, 2], F32, z)
        with ExitStack() as z:
            b_hi = sb("b_hi", [P, KD, BT], F32R, z)
            b_lo = sb("b_lo", [P, KD, BT], F32R, z)
            pp = sb("pp", [P, TT, D], F32, z)
            pt_hi = [sb(f"pt_hi{i}", [P, MT, BT], F32R, z) for i in range(2)]
            pt_lo = [sb(f"pt_lo{i}", [P, MT, BT], F32R, z) for i in range(2)]
            mx = sb("mx", [P, TT, H], F32, z)
            psums = sb("psums", [P, TT, H], F32, z)
            rinv = sb("rinv", [P, TT, H], F32, z)
        with ExitStack() as z:
            ht_hi = [sb(f"ht_hi{i}", [P, 4, BT], F32R, z) for i in range(2)]
            ht_lo = [sb(f"ht_lo{i}", [P, 4, BT], F32R, z) for i in range(2)]
            relu = sb("relu", [P, 4, BT], F32, z)
            xn = sb("xn", [P, TT, D], F32, z)
            nx = [sb(f"nx{i}", [P, D], F32, z) for i in range(2)]
        with ExitStack() as z:
            sb("below_junk", [P, 6 * D], F32, z)
            junk = sb("junk", [P, 2, D], F32, z)
            sb("below_xg", [P, 2 * D], F32, z)
            xg = [sb(f"xg{i}", [P, TT, 512], F32, z) for i in range(2)]
        with ExitStack() as z:
            kn = [sb(f"kn{i}", [P, MT, 512], F32, z) for i in range(4)]
            ws_raw = sb("ws_raw", [P, H, P], F32, z)
            tri = sb("tri", [P, 1, P], F32, z)
            lbp = sb("lbp", [P, 2, H], F32, z)
            lbm = sb("lbm", [P, H], F32, z)
        half = [ctx.enter_context(nc.psum_tensor(f"half{i}", [P, 4, 512], F32)) for i in range(2)]

        phases = ("mem", "block", "last")
        h0, h1, tl, dn = zip(*(jobs.counts[p] for p in phases))
        consts_in = sem("consts_in")
        w_in = [Event(sem(f"w_in{i}"), *(n // RAW for n in tl), step=16) for i in range(RAW)]
        w_rounded = sem("w_rounded")
        w_split = event("w_split", *tl, prime=RAW)
        w_used = event("w_used", *tl, prime=RING)
        pe_done = event("pe_done", *dn)
        evacuated = [event("evacuated0", *h0, prime=1), event("evacuated1", *h1, prime=1)]
        x_in = event("x_in", 0, TT, step=16)
        nx_in = [event(f"nx_in{i}", 2, 2, 0, step=16) for i in range(2)]
        gain_in = event("gain_in", ["n1"], ["n2", "n3", "n1", "y"], ["n2", "n3", "y"], step=16)
        mixers = ["ln", "oa", "ob"]
        norms = {"mem": ["nm", "n1a", "n1b"], "block": ["n2", "n3", "n1a", "n1b", "y"], "last": ["n2", "n3", "y"]}
        ssq_ready = event("ssq_ready", *(norms[p] for p in phases))
        all_norms = [norms["mem"], mixers + norms["block"], mixers + norms["last"]]
        var_ready = event("var_ready", *all_norms)
        rstd0_ready = event("rstd0_ready", *all_norms)
        n1_rows, y_rows = [("n1", t) for t in range(TT)], [("y", t) for t in range(TT)]
        halves = [(n, c) for n in ("n2", "n3") for c in range(2)]
        xn_ready = event("xn_ready", [("nm", t) for t in range(MT)] + n1_rows, halves + n1_rows + y_rows,
                         halves + y_rows)
        y_out = event("y_out", 0, TT, step=16, prime=16 * TT)
        n1_jobs = [("n1", 0), ("n1", 1)]
        attended_jobs = [("pt", 0), ("pt", 1), ("ca", 0), ("pt", 2), ("ca", 1), ("pt", 3), ("ca", 2), ("ca", 3)]
        split = ["otu", "oto", ("n2", 0), ("n2", 1), ("cq", 0), ("cq", 1)] + attended_jobs + [("n3", 0), ("n3", 1)]
        hi_ready = event("hi_ready", [("nm", 0), ("nm", 1), ("ckt", 0), ("ckt", 1), ("cv", 0), ("cv", 1)] + n1_jobs,
                         split + n1_jobs, split)
        sig_ready = event("sig_ready", 0, 1)
        logf_ready = event("logf_ready", 0, 1)
        vn_ready = event("vn_ready", 0, 1)
        args_ready = event("args_ready", 0, UNITS)
        decays_ready = event("decays_ready", 0, UNITS)
        scaled_ready = event("scaled_ready", 0, UNITS)
        o_ready = event("o_ready", 0, UNITS)
        added_used = event("added_used", 0, UNITS)
        mixed_ready = event("mixed_ready", 0, TT)
        max_ready = event("max_ready", 0, TT)
        p_ready = event("p_ready", 0, TT)
        relu_ready = event("relu_ready", 0, 8)
        sq_ready = event("sq_ready", 0, 8)
        ht_hi_ready = event("ht_hi_ready", 0, 8)
        ws_transposed, lb_args, lb_exps, setup_ready = (
            sem(n) for n in ("ws_transposed", "lb_args", "lb_exps", "setup_ready"))
        kn_out, s_out = sem("kn_out"), sem("s_out")
        act_sem, dve_sem = sem("act_chain"), sem("dve_chain")
        s_consts_in, s_first_in, s0_in, vn_out, s_out_done = (
            sem(n) for n in ("s_consts_in", "s_first_in", "s0_in", "vn_out", "s_out_done"))
        ws_in = [sem(f"ws_in{i}") for i in range(WS)]
        kv_in = [sem(f"kv_in{i}") for i in range(KV)]
        pe_s, act_s, dve_s = (Steps(sem(n), names) for n, names in (
            ("pe_steps", PE_STEPS), ("act_steps", ACT_STEPS), ("dve_steps", DVE_STEPS)))

        def step(name):
            steps, = (x for x in (pe_s, act_s, dve_s) if name in x.names)
            return steps.sem, steps.names.index(name) + 1

        def bank(i):
            return half[i // 4][:, i % 4, :]

        def own_columns(m):
            return m[:, :, :, 0:DS]

        def of_request(m, k, b):
            return m[:, k].rearrange("p b s -> p (b s)")[:, b * NS:b * NS + NS]

        last_block = ("last", 0)

        def stat(tag):
            return {"nm": 28, "n1a": 28, "n1b": 30, "y": 32, "ln": 16, "oa": 0, "ob": 12, "n2": 20, "n3": 24}[tag]

        SQ = slice(0, NS)

        def keys_part(eng, r, part, copy):
            eng.wait_ge(*step(f"kt{r}_{part}"))
            if r >= 2:
                eng.wait_ge(*step(f"sc{r - 2}"))
            ps = half[1][:, 2 * part:2 * part + 2, :].rearrange("p a (i m) -> p (a i) m", m=NM)
            return copy(kts[r % 2][:, 4 * part:4 * part + 4, :], ps)


        def done(pos, job, f=0):
            _, _, _, last, n = jobs.of[pos[0], job]
            if weight_tiles(job):
                return w_used.sem, w_used.at(pos, last + f * (4 * KD))
            return pe_done.sem, pe_done.at(pos, n)

        def out(pos, job, f=0):
            h, use, *_ = jobs.of[pos[0], job]
            return evacuated[h].sem, evacuated[h].at(pos, use + f * 3)

        def evacuated_of(pos, job):
            return evacuated[jobs.of[pos[0], job][0]].sem

        def out_of(pos, job):
            return half[jobs.of[pos[0], job][0]]

        def pair(pos, p, a):
            return (a[:, :, 2 * p * P:2 * p * P + 2 * P].rearrange("p k (t c) -> p k t c", c=P),
                    out_of(pos, ("n1", p)).rearrange("p (t a) (k c) -> p (a k) t c", t=2, c=P))

        def feature_tiles(ps, width=P):
            return ps[:, 0:2, :].rearrange("p a (k c) -> p (a k) c", c=width)

        block = ctx.enter_context(nc.Block())

        n_consts = 12

        @block.sync
        def _(sp):
            sp.sem_inc(y_out.sem, y_out.prime)
            for dst, src in ((ident[:], I["c_ident"]), (ones[:], I["c_ones"]), (tri[:, 0, :], I["c_tri"]),
                             (masks[:], I["c_masks"]),
                             (ws_raw[:], I["w_s"][0].rearrange("g t s -> t g s")),
                             (hgg_row[:], I["hg_norm_g"][0:1, :].broadcast_to([P, HG])),
                             (lng_row[:], I["ln_v_g"][0:1, :].broadcast_to([P, HG])),
                             (lnb_row[:], I["ln_v_b"][0:1, :].broadcast_to([P, HG])),
                             (bs_col[:], I["b_s"][0].rearrange("g t -> t g")),
                             (lbp[:], I["lb_param"].rearrange("r (h p) -> p r h", p=P)),
                             (x[:, 0:MT, :], I["mem_prompt"][0].rearrange("(t p) d -> p t d", p=P)),
                             (gain[:], I["g_mem"][0:1, :].broadcast_to([P, D]))):
                with nc.allow_non_contiguous_dma(reason="small constants"):
                    sp.dma_start(dst, src).then_inc(consts_in, 16)

            def load(pos, i0, w, row0, col0, ks=range(KD)):
                for i, k in enumerate(ks):
                    s = i % RAW
                    sp.wait_ge(w_split.sem, w_split.at(pos, i0 + i) - RAW)
                    sp.dma_start(w_raw[:, s, :], w[bass.ds(row0 + k * P, P), bass.ds(col0, 512)]
                                 ).then_inc(w_in[s].sem, 16)

            def load_gain(g):
                sp.dma_start(gain[:], g.broadcast_to([P, D])).then_inc(gain_in.sem, 16)

            def load_nx(t, row):
                sp.dma_start(nx[t % 2][:], I["x_prompt"][0, bass.ds(row + t * P, P), :]).then_inc(nx_in[t % 2].sem, 16)

            pos = ("mem", 0)
            load_nx(0, 0)
            load_nx(1, 0)
            for i, (w, c) in enumerate((w, c) for w in ("w_ck", "w_cv") for c in range(2)):
                load(pos, i * KD, I[w][0], 0, c * 512)
                if i == 1:
                    sp.wait_ge(xn_ready.sem, xn_ready.at(pos, ("nm", MT - 1)))
                    load_gain(I["g_mix"][0:1, :])
            for t in (2, 3):
                sp.wait_ge(xn_ready.sem, xn_ready.at(pos, ("n1", t - 2)))
                load_nx(t, 0)

            with nc.allow_non_contiguous_dma(reason="small constants"):
                sp.dma_start(own[:], I["c_own"]).then_inc(s_consts_in, 16)
                sp.dma_start(tri_own[:], I["c_tri_own"]).then_inc(s_consts_in, 16)
                for r in range(DB):
                    rows = slice(r * DS, r * DS + DS)
                    for g in range(H):
                        sp.dma_start(w4[rows, g, :], I["w_s"][0, g, 0:DS, 0:DS].rearrange("t s -> s t")).then_inc(
                            s_consts_in, 16)
                    sp.dma_start(b4[rows, :], I["b_s"][0, :, 0:DS].rearrange("g t -> t g")).then_inc(s_consts_in, 16)

            def block_loads(pos, row, last):
                w_in_ = I["w_in"][0]
                for i, c in enumerate((512, 1024, 0, 2560, 1536, 2048)):
                    load(pos, i * KD, w_in_, 0, c)
                    if i == 2:
                        sp.wait_ge(xn_ready.sem, xn_ready.at(pos, -1))
                        load_gain(I["g_cross"][0:1, :])
                load(pos, 6 * KD, I["w_out"][0], 0, 0, (4, 5, 6, 7, 0, 1, 2, 3))
                sp.wait_ge(*out(pos, ("lv", UNITS - 1)))
                for t in range(TT):
                    sp.dma_start(x[:, t, :], I["x_prompt"][0, bass.ds(row + t * P, P), :]).then_inc(x_in.sem, 16)
                load(pos, 7 * KD, I["w_out"][0], 0, 512)
                for c in range(2):
                    load(pos, (8 + c) * KD, I["w_cq"][0], 0, c * 512)
                sp.wait_ge(xn_ready.sem, xn_ready.at(pos, ("n2", 1)))
                load_gain(I["g_mlp"][0:1, :])
                for c in range(2):
                    load(pos, (10 + c) * KD, I["w_co"][0], 0, c * 512)
                load(pos, 12 * KD, I["w_up"][0], 0, 0)
                if not last:
                    sp.wait_ge(*out(pos, ("ca", H - 1)))
                    load_nx(0, row + BT)
                    load_nx(1, row + BT)
                sp.wait_ge(xn_ready.sem, xn_ready.at(pos, ("n3", 1)))
                load_gain(I["g_final"][None, :] if last else I["g_mix"][0:1, :])
                with sp.Fori(0, FF // 512 - 1) as e:
                    load(pos, 13 * KD + e * (2 * KD), I["w_up"][0], 0, e * 512 + 512)
                    for c in range(2):
                        load(pos, 14 * KD + 4 * c + e * (2 * KD), I["w_down"][0], e * 512, c * 512, range(4))
                load(pos, 27 * KD, I["w_down"][0], FF - 512, 0, range(4))
                for t in (2, 3) if not last else ():
                    sp.wait_ge(xn_ready.sem, xn_ready.at(pos, ("n1", t - 2)))
                    load_nx(t, row + BT)
                load(pos, 27 * KD + 4, I["w_down"][0], FF - 512, 512, range(4))
                if not last:
                    sp.wait_ge(xn_ready.sem, xn_ready.at(pos, ("n1", TT - 1)))
                    load_gain(I["g_final"][None, :])

            with sp.Fori(0, NB - 1) as b:
                block_loads(("block", b), b * BT, False)
            block_loads(last_block, (NB - 1) * BT, True)

            chunks = ([(n, I["w_in"][0], 0, col) for n, col in (("zf", 512), ("zq", 0), ("zi", 1024), ("zg", 1536),
                                                                 ("zv", 2560), ("zu", 2048))]
                      + [(f"{n}{c}", I[w][0], 0, c * 512) for n, w in (("wo", "w_out"), ("cq", "w_cq"), ("co", "w_co"))
                         for c in range(2)]
                      + [(f"up{e}", I["w_up"][0], 0, e * 512) for e in range(8)]
                      + [(f"dn{r}_{c}", I["w_down"][0], r * D, c * 512) for r in range(4) for c in range(2)])

            def load_s(i0, i1):
                for i in range(i0, i1):
                    if i >= WS:
                        sp.wait_ge(*step(chunks[i - WS][0]))
                    _, w, row, col = chunks[i]
                    sp.dma_start(w_smp[i % WS][:], w[row:row + D, col:col + 512].rearrange("(k p) c -> p k c", p=P)
                                 ).then_inc(ws_in[i % WS], 16)

            def load_kv(src, i0):
                for r in range(DB):
                    i = i0 + r
                    if i >= KV:
                        sp.wait_ge(*step(f"kt{i - KV}_1" if i - KV < DB else f"ca{i - KV - DB}"))
                    sp.dma_start(kv[i % KV][:], src[0, r].rearrange("(t p) h d -> p t (h d)", p=P)
                                 ).then_inc(kv_in[i % KV], 16)

            sp.wait_ge(*out(last_block, ("ca", H - 1)))
            load_s(0, 2)
            sp.wait_ge(y_out.sem, y_out.at(last_block, TT - 1))
            sp.dma_start(xs[:], I["x_sample"].rearrange("b t d -> (b t) d")).then_inc(s_first_in, 16)
            for i, g in enumerate(("g_mix", "g_cross", "g_mlp")):
                sp.dma_start(gains[:, i, :], I[g][0:1, :].broadcast_to([NS, D])).then_inc(s_first_in, 16)
            sp.wait_ge(w_used.sem, w_used.at(last_block, W_TILES["block"] - 1))
            load_s(2, 4)
            sp.dma_start(s0[:], I["state_hgrn"][0].rearrange("b h k v -> k b h v")).then_inc(s0_in, 16)
            sp.dma_start(O[2][0, 0].rearrange("h k v -> k h v"), state[:]).then_inc(s_out, 16)
            load_s(4, 10)
            load_kv(I["cache_mem_k"], 0)
            load_s(10, 11)
            load_kv(I["cache_mem_v"], DB)
            load_s(11, len(chunks))
            sp.wait_ge(s_out, 16)

        @block.gpsimd
        def _(pool):
            pool.sem_inc(w_split.sem, RAW)
            nc.gpsimd.memset(zero[:], 0.0).then_inc(w_rounded, 1)
            pool.wait_ge(w_rounded, 1)
            with pool.Fori(0, (W_TILES["mem"] + NB * W_TILES["block"]) // RING) as g:
                for k in range(RING):
                    s = k % RAW
                    pool.wait_ge(w_in[s].sem, g * (16 * RING // RAW) + 16 * (k // RAW + 1))
                    pool.wait_ge(w_used.sem, g * RING + (k + 1))
                    nc.gpsimd.tensor_tensor(w_hi[:, k, :], w_raw[:, s, :], zero[:].to_broadcast([P, 512]),
                                            ALU.add).then_inc(w_rounded, 1)
                    pool.wait_ge(w_rounded, g * RING + (k + 2))
                    nc.gpsimd.tensor_tensor(w_lo[:, k, :], w_raw[:, s, :], w_hi[:, k, :].bitcast(F32),
                                            ALU.subtract).then_inc(w_split.sem, 1)

        @block.tensor
        def _(pe):
            pe.sem_inc(w_used.sem, RING)
            for h in range(2):
                pe.sem_inc(evacuated[h].sem, 1)

            def begin(pos, job, f=0, needs=()):
                h, use, *_ = jobs.of[pos[0], job]
                last = {h: use - 1}
                for j in needs:
                    hj, uj, *_ = jobs.of[pos[0], j]
                    last[hj] = max(last.get(hj, uj), uj)
                for hj, uj in sorted(last.items()):
                    pe.wait_ge(evacuated[hj].sem, evacuated[hj].at(pos, uj + f * 3))
                return half[h]

            def gemm(pos, job, kind, hi, lo, tiles=4, f=0, needs=(), ks=range(KD), turns=None):
                n, t0 = weight_tiles(job), jobs.of[pos[0], job][2]
                ks = list(ks)[:n]
                turns = range(n) if turns is None else turns
                ps = begin(pos, job, f, needs) if turns[0] == 0 else out_of(pos, job)
                for i in turns:
                    k, s = ks[i], (t0 + i) % RING
                    pe.wait_ge(w_split.sem, w_split.at(pos, t0 + i + f * (4 * KD)))
                    for j in range(tiles):
                        c = slice(j * P, j * P + P)
                        if kind == "T":
                            parts = ((w_lo[:, s, c], hi[:, k, :]), (w_hi[:, s, c], lo[:, k, :]),
                                     (w_hi[:, s, c], hi[:, k, :]))
                        else:
                            parts = ((lo[:, k, c], w_hi[:, s, :]), (hi[:, k, c], w_lo[:, s, :]),
                                     (hi[:, k, c], w_hi[:, s, :]))
                        for q, (l, r) in enumerate(parts):
                            m = nc.tensor.matmul(ps[:, j, :], l, r, start=(i == 0 and q == 0),
                                                 stop=(i == n - 1 and q == 2))
                    m.then_inc(w_used.sem, 1)

            def transposes(pos, job, tiles, needs=()):
                ps = begin(pos, job, 0, needs)
                for i, t in enumerate(tiles):
                    m = nc.tensor.transpose(ps[:, i // 4, (i % 4) * P:(i % 4) * P + P], t, ident[:])
                m.then_inc(pe_done.sem, 1)

            def three(out, lhs, rhs, first, last):
                (lh, ll), (rh, rl) = lhs, rhs
                for i, (l, r) in enumerate(((ll, rh), (lh, rl), (lh, rh))):
                    m = nc.tensor.matmul(out, l, r, start=(first and i == 0), stop=(last and i == 2))
                return m

            def rows_transposed(pos, p):
                pe.wait_ge(xn_ready.sem, xn_ready.at(pos, ("n1", 2 * p + 1)))
                transposes(pos, ("n1", p), [xn[:, t, k * P:k * P + P] for t in (2 * p, 2 * p + 1) for k in range(KD)])

            def half_transposed(pos, tag, c):
                pe.wait_ge(xn_ready.sem, xn_ready.at(pos, (tag, c)))
                transposes(pos, (tag, c), [xg[c][:, t, k * P:k * P + P] for k in range(4) for t in range(TT)])

            pe.wait_ge(consts_in, 16 * n_consts)
            for g in range(H):
                m = nc.tensor.transpose(half[1][:, 0, g * P:g * P + P], ws_raw[:, g, :], ident[:])
            m.then_inc(ws_transposed, 1)
            pe.wait_ge(setup_ready, 1)

            pos = ("mem", 0)
            for t in range(MT):
                pe.wait_ge(xn_ready.sem, xn_ready.at(pos, ("nm", t)))
                transposes(pos, ("nm", t), [xn[:, t, k * P:k * P + P] for k in range(KD)])
            for c in range(2):
                gemm(pos, ("ck", c), "M", a_hi, a_lo, MT, needs=[("nm", MT - 1)])
                transposes(pos, ("ckt", c), [kn[c][:, t, j * P:j * P + P] for j in range(4) for t in range(MT)],
                           [("ck", c)])
            for c in range(2):
                gemm(pos, ("cv", c), "M", a_hi, a_lo, MT)
            rows_transposed(pos, 0)
            rows_transposed(pos, 1)

            def within_chunk(pos, u):
                c, p = divmod(u, 2)
                pe.wait_ge(scaled_ready.sem, scaled_ready.at(pos, u))
                ps = begin(pos, ("lv", u))
                for j in range(2):
                    tok = slice(c * P, c * P + P)
                    for l in range(LEVELS):
                        lhs, rhs = ((kk[:, 2 * p + j, tok], qq[:, 2 * p + j, tok]) if l == 0 else
                                    [lvl[u % 2][:, l - 1, j, :]] * 2)
                        m = nc.tensor.matmul(ps[:, 2 * j + l // 4, (l % 4) * P:(l % 4) * P + P], lhs, rhs,
                                             start=True, stop=True)
                m.then_inc(pe_done.sem, 1)

            def keys_to_rows(ps, u):
                for j in range(2):
                    m = nc.tensor.transpose(ps[:, 2, j * P:j * P + P], ends[u % 3][:, 1, j, :], ident[:])
                return m

            def rows_and_state(pos, u):
                c, p = divmod(u, 2)
                if u == 0:
                    pe.wait_ge(*out(pos, "zi"))
                if u >= 2:
                    pe.wait_ge(added_used.sem, added_used.at(pos, u - 2))
                if u + 1 < UNITS:
                    pe.wait_ge(scaled_ready.sem, scaled_ready.at(pos, u + 1))
                ps = begin(pos, ("out", u))
                for j in range(2):
                    h = 2 * p + j
                    v = vv[:, c, h * P:h * P + P]
                    o = ps[:, 0, j * P:j * P + P]
                    nc.tensor.matmul(o, att[:, j, :], v, start=True, stop=False)
                    nc.tensor.matmul(o, ends[u % 3][:, 0, j, :], state[:, h, :], start=False, stop=True)
                    m = nc.tensor.matmul(ps[:, 1, j * P:j * P + P], kdt[:, j, :], v, start=True, stop=True)
                if u + 1 < UNITS:
                    m = keys_to_rows(ps, u + 1)
                m.then_inc(pe_done.sem, 1)

            def block_products(pos, last):
                def fill(turns):
                    for i in turns:
                        gemm(pos, ("zv", "zg", "zu")[i // KD], "M", a_hi, a_lo, turns=[i % KD])

                gemm(pos, "zf", "T", a_hi, a_lo)
                gemm(pos, "zi", "M", a_hi, a_lo)
                gemm(pos, "zq", "T", a_hi, a_lo)
                fill(range(0, 4))
                pe.wait_ge(scaled_ready.sem, scaled_ready.at(pos, 0))
                keys_to_rows(begin(pos, "kt"), 0).then_inc(pe_done.sem, 1)
                for u in range(UNITS):
                    within_chunk(pos, u)
                    if u == UNITS - 1:
                        pe.wait_ge(vn_ready.sem, vn_ready.at(pos, 0))
                        ps = begin(pos, "mix")
                        for t in range(TT):
                            for g in range(H):
                                c = slice(g * P, g * P + P)
                                m = nc.tensor.matmul(ps[:, t, c], ws_t[:, g, :], vn[:, t, c], start=True, stop=True)
                        m.then_inc(pe_done.sem, 1)
                    fill(range(4 + 3 * u, min(7 + 3 * u, 3 * KD)))
                    rows_and_state(pos, u)
                transposes(pos, "otu", [uu[:, t, k * P:k * P + P] for k in range(H) for t in range(TT)])
                pe.wait_ge(mixed_ready.sem, mixed_ready.at(pos, TT - 1))
                transposes(pos, "oto", [vv[:, t, k * P:k * P + P] for k in range(H) for t in range(TT)])
                order = (4, 5, 6, 7, 0, 1, 2, 3)
                gemm(pos, ("wo", 0), "M", a_hi, a_lo, ks=order, turns=range(4), needs=["otu"])
                pe.wait_ge(*out(pos, "oto"))
                gemm(pos, ("wo", 0), "M", a_hi, a_lo, ks=order, turns=range(4, 8))

                def norm_between(tag, name, nxt, kind):
                    gemm(pos, (name, 1), "M", a_hi, a_lo, turns=range(5))
                    half_transposed(pos, tag, 0)
                    gemm(pos, (name, 1), "M", a_hi, a_lo, turns=range(5, 8))
                    gemm(pos, (nxt, 0), "T", a_hi, a_lo, turns=range(2), needs=[(tag, 0)])
                    half_transposed(pos, tag, 1)
                    gemm(pos, (nxt, 0), "T", a_hi, a_lo, turns=range(2, 4))
                    pe.wait_ge(*out(pos, (tag, 1)))
                    gemm(pos, (nxt, 0), "T", a_hi, a_lo, turns=range(4, 8))

                norm_between("n2", "wo", "cq", "T")
                gemm(pos, ("cq", 1), "T", a_hi, a_lo)
                for t in range(TT):
                    ps = begin(pos, ("sc", t), 0, [("cq", 1)])
                    q = slice(t * P, t * P + P)
                    for h in range(H):
                        for k in (2 * h, 2 * h + 1):
                            m = three(ps[:, h // 2, (h % 2) * NM:(h % 2) * NM + NM],
                                      (b_hi[:, k, q], b_lo[:, k, q]), (kt_hi[:, k, :], kt_lo[:, k, :]),
                                      k == 2 * h, k == 2 * h + 1)
                    m.then_inc(pe_done.sem, 1)

                def p_transposed(h):
                    if h == 0:
                        pe.wait_ge(p_ready.sem, p_ready.at(pos, TT - 1))
                    transposes(pos, ("pt", h), [pp[:, t, h * NM + m * P:h * NM + m * P + P]
                                                for m in range(MT) for t in range(TT)])

                def attended(h):
                    ps = begin(pos, ("ca", h), 0, [("pt", h)])
                    for dd in range(2):
                        for mm in range(MT):
                            c = slice(h * XD + dd * P, h * XD + dd * P + P)
                            m = three(ps[:, dd, :], (v_hi[:, mm, c], v_lo[:, mm, c]),
                                      (pt_hi[h % 2][:, mm, :], pt_lo[h % 2][:, mm, :]), mm == 0, mm == MT - 1)
                    m.then_inc(pe_done.sem, 1)

                p_transposed(0)
                for h in range(H):
                    if h + 1 < H:
                        p_transposed(h + 1)
                    attended(h)
                gemm(pos, ("co", 0), "M", a_hi, a_lo, needs=[("ca", H - 1)])
                norm_between("n3", "co", "up", "T")

                def down(e, f=0):
                    gemm(pos, ("dn", e, 0), "M", ht_hi[e % 2], ht_lo[e % 2], f=f, needs=[("up", e)])
                    gemm(pos, ("dn", e, 1), "M", ht_hi[e % 2], ht_lo[e % 2], turns=range(2), f=f, needs=[("up", e)])
                    if e >= 6 and not last:
                        rows_transposed(pos, e - 6)
                    gemm(pos, ("dn", e, 1), "M", ht_hi[e % 2], ht_lo[e % 2], turns=range(2, 4), f=f)

                with pe.Fori(0, 3) as f:
                    for e in range(2):
                        gemm(pos, ("up", e + 1), "T", a_hi, a_lo, f=f)
                        down(e, f)
                gemm(pos, ("up", 7), "T", a_hi, a_lo)
                down(6)
                down(7)

            with pe.Fori(0, NB - 1) as b:
                block_products(("block", b), False)
            block_products(last_block, True)

            def gemm_s(i, name, src, b, first=True, last=True):
                pe.wait_ge(ws_in[i % WS], 16 * (i // WS + 1))
                for k in range(KD):
                    m = nc.tensor.matmul(bank(b)[SQ, :], src[:, k, :], w_smp[i % WS][:, k, :],
                                         start=(first and k == 0), stop=(last and k == KD - 1))
                m.then_inc(pe_s.did(name), 1)

            def to_columns(name, b, tiles):
                for i, t in enumerate(tiles):
                    m = nc.tensor.transpose(bank(b)[:, i * NS:i * NS + NS], t, ident[0:NS, 0:NS])
                m.then_inc(pe_s.did(name), 1)

            def tiles_of(t, n=KD):
                return [t[:, k * P:k * P + P] for k in range(n)]

            for h in range(2):
                pe.wait_ge(evacuated[h].sem, evacuated[h].at(last_block, jobs.counts["last"][h] - 1))
            pe.wait_ge(*step("xn1"))
            to_columns("n1", 0, tiles_of(xns))
            pe.wait_ge(*step("xt1"))
            gemm_s(0, "zf", xt, 1)
            gemm_s(1, "zq", xt, 2)
            pe.wait_ge(*step("zf_rows"))
            pe.wait_ge(*step("zq_rows"))
            to_columns("zt", 0, tiles_of(zfq[:, 0, :], H) + tiles_of(zfq[:, 1, :], H))
            gemm_s(2, "zi", xt, 3)
            gemm_s(3, "zg", xt, 4)
            gemm_s(4, "zv", xt, 5)
            pe.wait_ge(*step("scaled"))
            for h in range(H):
                for l in range(SLV):
                    lhs, rhs = (kk_s[:, h, :], qq_s[:, h, :]) if l == 0 else [dec_s[:, l - 1, h, :]] * 2
                    c = (h * SLV + l) * NS
                    m = nc.tensor.matmul(bank(1)[SQ, c:c + NS], lhs, rhs, start=True, stop=True)
            m.then_inc(pe_s.did("lv"), 1)
            for h in range(H):
                m = nc.tensor.transpose(bank(2)[SQ, h * P:h * P + P], dec_s[:, SLV, h, :], ident[:])
            m.then_inc(pe_s.did("kt"), 1)
            pe.wait_ge(s0_in, 16)
            pe.wait_ge(*step("v_rows"))
            pe.wait_ge(*step("att"))
            for h in range(H):
                o = bank(3)[SQ, h * P:h * P + P]
                nc.tensor.matmul(o, att_s[:, h, :], v_s[:, h * P:h * P + P], start=True, stop=False)
                for r in range(DB):
                    m = nc.tensor.matmul(o, of_request(qe_m, h, r), s0[:, r, h, :], start=False, stop=(r == DB - 1))
            m.then_inc(pe_s.did("o"), 1)
            gemm_s(5, "zu", xt, 6)
            pe.wait_ge(*step("vn"))
            for g in range(H):
                m = nc.tensor.matmul(bank(7)[SQ, g * P:g * P + P], ws_s[:, g].rearrange("p b t -> p (b t)"),
                                     vn_s[:, g * P:g * P + P], start=True, stop=True)
            m.then_inc(pe_s.did("mix"), 1)
            pe.wait_ge(*step("mixed"))
            to_columns("ot", 0, tiles_of(o_s, H) + tiles_of(u_s, H))

            def new_tokens(j):
                h, r0 = divmod(j, 2)
                col = slice(h * P, h * P + P)
                if j >= 4:
                    pe.wait_ge(*step(f"new{j - 4}"))
                m = nc.tensor.matmul(bank(4 + j % 4), kd_s[:, col], vm[:, 4 * r0:4 * r0 + 4, col], start=True, stop=True)
                m.then_inc(pe_s.did(f"st{j}"), 1)

            pe.wait_ge(*step("gate"))
            pe.wait_ge(*step("zu_gelu"))
            pe.wait_ge(*step("mixed_cm"))
            pe.wait_ge(*step("kd_rows"))
            pe.wait_ge(*step("vm"))
            for j in range(4):
                new_tokens(j)
            pe.wait_ge(*step("xt_ot"))
            gemm_s(6, "wo0", xt, 1)
            for j in range(4, 8):
                new_tokens(j)
            gemm_s(7, "wo1", xt, 2)
            pe.wait_ge(*step("xn2"))
            to_columns("n2", 0, tiles_of(xns))
            pe.wait_ge(*step("xt2"))
            gemm_s(8, "cq0", xt, 1)
            gemm_s(9, "cq1", xt, 2)
            pe.wait_ge(*step("q_rows0"))
            pe.wait_ge(*step("q_rows1"))
            to_columns("qt", 3, tiles_of(q_s))
            pe.wait_ge(*step("qm"))
            for r in range(DB + 1):
                if r < DB:
                    pe.wait_ge(kv_in[r % KV], 16 * (r // KV + 1))
                    for part in range(2):
                        if r:
                            pe.wait_ge(*step(f"kts{r - 1}_{part}"))
                        for i in range(4):
                            for t in range(MT):
                                d0 = (4 * part + i) * P
                                m = nc.tensor.transpose(bank(4 + 2 * part + i // 2)[:, (i % 2) * NM + t * P:][:, 0:P],
                                                        kv[r % KV][:, t, d0:d0 + P], ident[:])
                        m.then_inc(pe_s.did(f"kt{r}_{part}"), 1)
                if r:
                    pe.wait_ge(*step(f"kts{r - 1}_0"))
                    pe.wait_ge(*step(f"kts{r - 1}_1"))
                    for k in range(KD):
                        m = nc.tensor.matmul(bank(k // 2)[SQ, 0:NM], of_request(qm, k, r - 1),
                                             kts[(r - 1) % 2][:, k, :], start=(r == 1 and k % 2 == 0),
                                             stop=(r == DB and k % 2 == 1))
                    m.then_inc(pe_s.did(f"sc{r - 1}"), 1)
            pe.wait_ge(*step("p_rows"))
            to_columns("pt", 4, tiles_of(q_s))
            pe.wait_ge(*step("pm"))
            for r in range(DB):
                i = DB + r
                pe.wait_ge(kv_in[i % KV], 16 * (i // KV + 1))
                for h in range(H):
                    for t in range(MT):
                        m = nc.tensor.matmul(bank(h)[SQ, 0:XD], of_request(pm, h * MT + t, r),
                                             kv[i % KV][:, t, h * XD:h * XD + XD],
                                             start=(r == 0 and t == 0), stop=(r == DB - 1 and t == MT - 1))
                m.then_inc(pe_s.did(f"ca{r}"), 1)
            pe.wait_ge(*step("ca_rows"))
            to_columns("cat", 4, tiles_of(xns))
            pe.wait_ge(*step("xt_ca"))
            gemm_s(10, "co0", xt, 5)
            gemm_s(11, "co1", xt, 6)
            pe.wait_ge(*step("xn3"))
            to_columns("n3", 0, tiles_of(xns))
            pe.wait_ge(*step("xt3"))
            for e in range(9):
                if e < 8:
                    if e >= 2:
                        pe.wait_ge(*step(f"sq{e - 2}"))
                    gemm_s(12 + e, f"up{e}", xt, 1 + e % 2)
                if e:
                    pe.wait_ge(*step(f"sq{e - 1}"))
                    if e >= 3:
                        pe.wait_ge(*step(f"hts{e - 3}"))
                    to_columns(f"ht{e - 1}", 3 + (e - 1) % 2, tiles_of(relu_s[(e - 1) % 2], 4))
            for r in range(4):
                pe.wait_ge(*step(f"hts{2 * r + 1}"))
                for c in range(2):
                    gemm_s(20 + 2 * r + c, f"dn{r}_{c}", hts[:, r * KD:r * KD + KD], 5 + c, r == 0, r == 3)

        @block.scalar
        def _(act):
            link = Links(act_sem, mem=3, block=UNITS + 8, last=UNITS + 6, sample=7)
            tables = nc.scalar.preload_act_table_set

            def rsqrt(pos, tag, n):
                tables("natural_log_exp_and_others")
                act.wait_ge(var_ready.sem, var_ready.at(pos, tag))
                c = slice(stat(tag), stat(tag) + n)
                nc.scalar.activation(lnv[:, c], var[:, c], ACT.Ln).then_inc(act_sem, 1)
                act.wait_ge(act_sem, link.next())
                nc.scalar.activation(y0[:, c], lnv[:, c], ACT.Exp, scale=-0.5).then_inc(rstd0_ready.sem, 1)

            def squares(tag, tiles, junk):
                for i, t in enumerate(tiles):
                    ins = nc.scalar.activation(junk[i], t, ACT.Square, accum_out=ss[:, stat(tag) + i:stat(tag) + i + 1])
                ins.then_inc(ssq_ready.sem, 1)

            def round_hi(pos, job, dst, src, scale=1.0):
                act.wait_ge(*done(pos, job))
                nc.scalar.activation(dst, src, ACT.Copy, scale=scale).then_inc(hi_ready.sem, 1)

            def n1_squares(pos, p):
                t = 2 * p
                tables("natural_log_exp_and_others")
                act.wait_ge(nx_in[0].sem, nx_in[0].at(pos, p))
                squares("n1" + "ab"[p], [nx[0][:]], [xn[:, t, :]])
                rsqrt(pos, "n1" + "ab"[p], 2)

            def n1_hi(pos, p):
                round_hi(pos, ("n1", p), *pair(pos, p, a_hi))

            tables("natural_log_exp_and_others")
            act.wait_ge(lb_args, 1)
            nc.scalar.activation(lbp[:], lbp[:], ACT.Exp).then_inc(lb_exps, 1)

            pos = ("mem", 0)
            link.start(pos)
            act.wait_ge(consts_in, 16 * n_consts)
            squares("nm", [x[:, 0, :]], [xn[:, 0, :]])
            rsqrt(pos, "nm", MT)
            for t in range(MT):
                round_hi(pos, ("nm", t), a_hi[:, :, t * P:t * P + P], feature_tiles(out_of(pos, ("nm", t))))
            for c in range(2):
                act.wait_ge(*done(pos, ("ck", c)))
                nc.scalar.copy(kn[c][:], out_of(pos, ("ck", c))[:, 0:MT, :]).then_inc(evacuated_of(pos, ("ck", c)), 1)
                act.wait_ge(*out(pos, ("ck", c)))
                act.dma_start(O[4][0, 0].rearrange("(t p) h d -> p t (h d)", p=P)[:, :, c * 512:c * 512 + 512],
                              kn[c][:]).then_inc(kn_out, 16)
                round_hi(pos, ("ckt", c), kt_hi[:, 4 * c:4 * c + 4, :], feature_tiles(out_of(pos, ("ckt", c)), NM))
            for c in range(2):
                ps = out_of(pos, ("cv", c))[:, 0:MT, :]
                act.wait_ge(*done(pos, ("cv", c)))
                nc.scalar.copy(kn[2 + c][:], ps)
                round_hi(pos, ("cv", c), v_hi[:, :, c * 512:c * 512 + 512], ps)
                act.wait_ge(hi_ready.sem, hi_ready.at(pos, ("cv", c)))
                act.dma_start(O[5][0, 0].rearrange("(t p) h d -> p t (h d)", p=P)[:, :, c * 512:c * 512 + 512],
                              kn[2 + c][:]).then_inc(kn_out, 16)
            for p in range(2):
                n1_squares(pos, p)
            for p in range(2):
                n1_hi(pos, p)
            act.wait_ge(kn_out, 64)
            link.end()

            def block_scalar(pos, b, last):
                link.start(pos)

                def decays(u):
                    tables("natural_log_exp_and_others")
                    act.wait_ge(args_ready.sem, args_ready.at(pos, u))
                    nc.scalar.activation(ends[u % 3][:], ends[u % 3][:], ACT.Abs)
                    nc.scalar.activation(lvl[u % 2][:], lvl[u % 2][:], ACT.Abs).then_inc(act_sem, 1)
                    act.wait_ge(act_sem, link.next())
                    nc.scalar.activation(ends[u % 3][:], ends[u % 3][:], ACT.Exp, scale=-1.0)
                    nc.scalar.activation(lvl[u % 2][:], lvl[u % 2][:], ACT.Exp, scale=-1.0
                                         ).then_inc(decays_ready.sem, 1)

                def rows_of(ps, b):
                    return ps[:, b, 0:2 * P].rearrange("p (j c) -> p j c", c=P)

                def unit_out(u):
                    c, p = divmod(u, 2)
                    if u >= 2:
                        act.wait_ge(added_used.sem, added_used.at(pos, u - 2))
                    act.wait_ge(*done(pos, ("out", u)))
                    ps = out_of(pos, ("out", u))
                    if u + 1 < UNITS:
                        nc.scalar.copy(kdt[:], rows_of(ps, 2))
                    nc.scalar.copy(added[u % 2][:], rows_of(ps, 1))
                    nc.scalar.copy(vv[:, c, 2 * p * P:2 * p * P + 2 * P], ps[:, 0, 0:2 * P]
                                   ).then_inc(evacuated_of(pos, ("out", u)), 1)
                    act.wait_ge(*out(pos, ("out", u)))
                    for j in range(2):
                        i = 2 * p + j
                        ins = nc.scalar.activation(osq[:, j, :], vv[:, c, i * P:i * P + P], ACT.Square,
                                                   accum_out=ss[:, 4 * c + i:4 * c + i + 1])
                    ins.then_inc(o_ready.sem, 1)

                tables("sigmoid_and_others")
                act.wait_ge(*done(pos, "zf"))
                nc.scalar.activation(kk[:], out_of(pos, "zf")[:], ACT.Sigmoid, scale=-1.0)
                nc.scalar.activation(bb[:], out_of(pos, "zf")[:], ACT.Sigmoid).then_inc(evacuated_of(pos, "zf"), 1)
                tables("natural_log_exp_and_others")
                act.wait_ge(*out(pos, "zf"))
                for h in range(H):
                    ins = nc.scalar.activation(bb[:, h, :], bb[:, h, :], ACT.Ln, scale=oml[:, h:h + 1],
                                               bias=lb[:, h:h + 1])
                ins.then_inc(logf_ready.sem, 1)
                decays(0)
                decays(1)
                act.wait_ge(*done(pos, "zi"))
                nc.scalar.copy(vv[:], out_of(pos, "zi")[:]).then_inc(evacuated_of(pos, "zi"), 1)
                tables("sigmoid_and_others")
                act.wait_ge(*done(pos, "zq"))
                nc.scalar.activation(qq[:], out_of(pos, "zq")[:], ACT.Sigmoid).then_inc(sig_ready.sem, 1)
                act.wait_ge(*done(pos, "kt"))
                nc.scalar.copy(kdt[:], rows_of(out_of(pos, "kt"), 2)).then_inc(evacuated_of(pos, "kt"), 1)
                for u in range(UNITS):
                    if u + 2 < UNITS:
                        decays(u + 2)
                    for at, name, dst in ((1, "zv", vn), (3, "zg", gate), (6, "zu", uu)):
                        if u == at:
                            tables("sigmoid_and_others" if name == "zg" else "gelu_apprx_tanh_and_others")
                            act.wait_ge(*done(pos, name))
                            nc.scalar.activation(dst[:], out_of(pos, name)[:], ACT.Sigmoid if name == "zg" else
                                                 ACT.Gelu_apprx_tanh).then_inc(evacuated_of(pos, name), 1)
                    unit_out(u)
                    if u == 2:
                        rsqrt(pos, "ln", TT)
                    if u == 6:
                        rsqrt(pos, "oa", 12)
                rsqrt(pos, "ob", 4)
                round_hi(pos, "otu", a_hi[:, 4:8, :], out_of(pos, "otu")[:])
                round_hi(pos, "oto", a_hi[:, 0:4, :], out_of(pos, "oto")[:])

                def norm_halves(tag, name):
                    for c in range(2):
                        round_hi(pos, (tag, c), a_hi[:, 4 * c:4 * c + 4, :], out_of(pos, (tag, c))[:])
                    tables("natural_log_exp_and_others")
                    act.wait_ge(*out(pos, (name, 1)))
                    squares(tag, [x[:, t, :] for t in range(2)],
                            [relu[:, 2 * t:2 * t + 2, :].rearrange("p a c -> p (a c)") for t in range(2)])
                    rsqrt(pos, tag, TT)

                norm_halves("n2", "wo")
                for c in range(2):
                    round_hi(pos, ("cq", c), b_hi[:, 4 * c:4 * c + 4, :], out_of(pos, ("cq", c))[:], ATT_SCALE)
                tables("natural_log_exp_and_others")
                for t in range(TT):
                    act.wait_ge(max_ready.sem, max_ready.at(pos, t))
                    ps = out_of(pos, ("sc", t))
                    for h in range(H):
                        ins = nc.scalar.activation(pp[:, t, h * NM:h * NM + NM],
                                                   ps[:, h // 2, (h % 2) * NM:(h % 2) * NM + NM], ACT.Exp,
                                                   scale=rstd[:, stat("n2") + t:stat("n2") + t + 1],
                                                   bias=mx[:, t, h:h + 1], accum_out=psums[:, t, h:h + 1])
                    ins.then_inc(evacuated_of(pos, ("sc", t)), 1)
                for job in attended_jobs:
                    name, h = job
                    ps = out_of(pos, job)[:, 0:2, :]
                    round_hi(pos, job, pt_hi[h % 2][:] if name == "pt" else a_hi[:, 2 * h:2 * h + 2, :], ps)
                norm_halves("n3", "co")

                def relu_square(e, f=0):
                    act.wait_ge(*done(pos, ("up", e), f))
                    if e:
                        act.wait_ge(*out(pos, ("up", e - 1), f))
                    nc.scalar.activation(relu[:], out_of(pos, ("up", e))[:], ACT.Relu).then_inc(relu_ready.sem, 1)
                    act.wait_ge(sq_ready.sem, sq_ready.at(pos, e + f * 2))
                    nc.scalar.copy(ht_hi[e % 2][:], relu[:]).then_inc(ht_hi_ready.sem, 1)

                relu_square(0)
                with act.Fori(0, 3) as f:
                    relu_square(1, f)
                    relu_square(2, f)
                relu_square(7)
                for p in range(2) if not last else ():
                    n1_squares(pos, p)
                    n1_hi(pos, p)
                tables("natural_log_exp_and_others")
                act.wait_ge(*out(pos, ("dn", 7, 1)))
                squares("y", [x[:, t, :] for t in range(2)], [xn[:, t, :] for t in range(2)])
                rsqrt(pos, "y", TT)
                for t in range(TT):
                    act.wait_ge(xn_ready.sem, xn_ready.at(pos, ("y", t)))
                    act.dma_start(O[0][0, bass.ds(b * BT + t * P, P), :], xn[:, t, :]).then_inc(y_out.sem, 16)
                link.end()

            with act.Fori(0, NB - 1) as b:
                block_scalar(("block", b), b, False)
            block_scalar(last_block, NB - 1, True)
            act.wait_ge(y_out.sem, y_out.at(last_block, TT - 1))

            link.start(("sample", 0))

            def rsqrt_s(tag, n):
                tables("natural_log_exp_and_others")
                act.wait_ge(*step("var_" + tag))
                nc.scalar.activation(lnv[SQ, 0:n], var[SQ, 0:n], ACT.Ln).then_inc(act_sem, 1)
                act.wait_ge(act_sem, link.next())
                nc.scalar.activation(y0[SQ, 0:n], lnv[SQ, 0:n], ACT.Exp, scale=-0.5).then_inc(act_s.did("rstd_" + tag), 1)

            rsqrt_s("n1", 1)
            for i, n in enumerate(("zf", "zq")):
                act.wait_ge(*step(n))
                nc.scalar.copy(zfq[:, i, :], bank(1 + i)[SQ, :]).then_inc(act_s.did(n + "_rows"), 1)
            tables("sigmoid_and_others")
            act.wait_ge(*step("zt"))
            zt = bank(0)[:, 0:2 * H * NS].rearrange("p (a h s) -> p a h s", a=2, h=H)
            nc.scalar.activation(kk_s[:], zt[:, 0], ACT.Sigmoid, scale=-1.0)
            nc.scalar.activation(bb_s[:], zt[:, 0], ACT.Sigmoid)
            nc.scalar.activation(qq_s[:], zt[:, 1], ACT.Sigmoid).then_inc(act_s.did("sig"), 1)
            act.wait_ge(*step("zi"))
            nc.scalar.copy(v_s[:], bank(3)[SQ, :]).then_inc(act_s.did("v_rows"), 1)
            act.wait_ge(*step("zg"))
            nc.scalar.activation(gate_s[:], bank(4)[SQ, :], ACT.Sigmoid).then_inc(act_s.did("gate"), 1)
            tables("natural_log_exp_and_others")
            act.wait_ge(*step("sig"))
            for h in range(H):
                ins = nc.scalar.activation(bb_s[:, h, :], bb_s[:, h, :], ACT.Ln, scale=oml[:, h:h + 1], bias=lb[:, h:h + 1])
            ins.then_inc(act_s.did("logf"), 1)
            act.wait_ge(*step("args"))
            nc.scalar.activation(dec_s[:], dec_s[:], ACT.Abs).then_inc(act_sem, 1)
            act.wait_ge(act_sem, link.next())
            nc.scalar.activation(dec_s[:], dec_s[:], ACT.Exp, scale=-1.0).then_inc(act_s.did("decays"), 1)
            tables("gelu_apprx_tanh_and_others")
            act.wait_ge(*step("zv"))
            nc.scalar.activation(vn_s[:], bank(5)[SQ, :], ACT.Gelu_apprx_tanh).then_inc(act_s.did("zv_gelu"), 1)
            act.wait_ge(*step("kt"))
            nc.scalar.copy(kd_s[:], bank(2)[SQ, :]).then_inc(act_s.did("kd_rows"), 1)
            act.wait_ge(*step("o"))
            nc.scalar.copy(o_s[:], bank(3)[SQ, :]).then_inc(act_s.did("o_rows"), 1)
            act.wait_ge(*step("zu"))
            nc.scalar.activation(u_s[:], bank(6)[SQ, :], ACT.Gelu_apprx_tanh).then_inc(act_s.did("zu_gelu"), 1)
            rsqrt_s("ln", 1)
            act.wait_ge(*step("vn"))
            act.dma_start(O[6][0].rearrange("b t c -> (b t) c"), vn_s[:]).then_inc(vn_out, 16)
            rsqrt_s("o", H)
            rsqrt_s("n2", 1)
            for c in range(2):
                act.wait_ge(*step(f"cq{c}"))
                nc.scalar.activation(q_s[:, c * 512:c * 512 + 512], bank(1 + c)[SQ, :],
                                                            ACT.Copy, scale=ATT_SCALE).then_inc(act_s.did(f"q_rows{c}"), 1)
            act.wait_ge(*step("new7"))
            act.dma_start(O[3][0].rearrange("b h k v -> k b h v"), s0[:]).then_inc(s_out_done, 16)

            for r in range(DB):
                keys_part(act, r, 0, nc.scalar.copy).then_inc(act_s.did(f"kts{r}_0"), 1)
            tables("natural_log_exp_and_others")
            act.wait_ge(*step("max"))
            for h in range(H):
                ins = nc.scalar.activation(q_s[:, h * NM:h * NM + NM], bank(h)[SQ, 0:NM], ACT.Exp,
                                           bias=mx_s[:, h:h + 1], accum_out=sum_s[:, h:h + 1])
            ins.then_inc(act_s.did("p_exp"), 1)
            act.wait_ge(*step(f"ca{DB - 1}"))
            nc.scalar.copy(xns[:].rearrange("p (h d) -> p h d", h=H), half[0][SQ, :, 0:XD]).then_inc(act_s.did("ca_rows"), 1)
            rsqrt_s("n3", 1)
            for e in range(8):
                act.wait_ge(*step(f"up{e}"))
                if e >= 2:
                    act.wait_ge(*step(f"ht{e - 2}"))
                nc.scalar.activation(relu_s[e % 2][:], bank(1 + e % 2)[SQ, :], ACT.Relu).then_inc(act_s.did(f"relu{e}"), 1)
            rsqrt_s("y", 1)
            act.wait_ge(*step("y"))
            act.dma_start(O[1].rearrange("b t d -> (b t) d"), xns[:]).then_inc(s_out_done, 16)
            act.wait_ge(vn_out, 16)
            act.wait_ge(s_out_done, 32)
            link.end()

        @block.vector
        def _(dve):
            link = Links(dve_sem, mem=13, block=67, last=59, sample=35)

            def newton(pos, tag, n, inv):
                c = slice(stat(tag), stat(tag) + n)
                nc.vector.tensor_scalar(var[:, c], ss[:, c], inv, EPS, ALU.mult, ALU.add).then_inc(var_ready.sem, 1)
                refine(pos, tag, n)

            def refine(pos, tag, n):
                c = slice(stat(tag), stat(tag) + n)
                dve.wait_ge(rstd0_ready.sem, rstd0_ready.at(pos, tag))
                nc.vector.scalar_tensor_tensor(yt[:, c], y0[:, c], -0.5, y0[:, c], ALU.mult, ALU.mult
                                               ).then_inc(dve_sem, 1)
                dve.wait_ge(dve_sem, link.next())
                nc.vector.tensor_tensor(yt[:, c], yt[:, c], var[:, c], ALU.mult).then_inc(dve_sem, 1)
                dve.wait_ge(dve_sem, link.next())
                nc.vector.scalar_tensor_tensor(rstd[:, c], yt[:, c], 1.5, y0[:, c], ALU.add, ALU.mult
                                               ).then_inc(dve_sem, 1)
                dve.wait_ge(dve_sem, link.next())

            def rest_lo(pos, job, dst, hi, src, scale=None):
                dve.wait_ge(hi_ready.sem, hi_ready.at(pos, job))
                if scale is None:
                    ins = nc.vector.tensor_tensor(dst, src, hi.bitcast(F32), ALU.subtract)
                else:
                    ins = nc.vector.scalar_tensor_tensor(dst, src, scale, hi.bitcast(F32), ALU.mult, ALU.subtract)
                ins.then_inc(evacuated_of(pos, job), 1)

            def mean_squares(pos, tag, n, tiles, junk):
                for i, t in enumerate(tiles):
                    c = stat(tag) + n - len(tiles) + i
                    ins = nc.vector.tensor_tensor_reduce(out=junk[i], in0=t, in1=t, scale=1.0, scalar=0.0,
                                                         op0=ALU.mult, op1=ALU.add, accum_out=ss[:, c:c + 1])
                ins.then_inc(dve_sem, 1)
                dve.wait_ge(dve_sem, link.next())
                dve.wait_ge(ssq_ready.sem, ssq_ready.at(pos, tag))
                newton(pos, tag, n, 1.0 / D)

            def scaled_row(tag, i, dst, src):
                c = stat(tag) + i
                nc.vector.scalar_tensor_tensor(dst, src, rstd[:, c:c + 1], gain[:], ALU.mult, ALU.mult
                                               ).then_inc(xn_ready.sem, 1)

            def n1_rows_scaled(pos, p):
                t = 2 * p
                if p == 0:
                    dve.wait_ge(gain_in.sem, gain_in.at(pos, "n1"))
                dve.wait_ge(nx_in[1].sem, nx_in[1].at(pos, p))
                mean_squares(pos, "n1" + "ab"[p], 2, [nx[1][:]], [xn[:, t + 1, :]])
                for i in range(2):
                    scaled_row("n1" + "ab"[p], i, xn[:, t + i, :], nx[i][:])

            def n1_lo(pos, p):
                dst, src = pair(pos, p, a_lo)
                rest_lo(pos, ("n1", p), dst, pair(pos, p, a_hi)[0], src)

            pos = ("mem", 0)
            link.start(pos)
            dve.wait_ge(consts_in, 16 * n_consts)
            nc.vector.memset(state[:], 0.0)
            nc.vector.tensor_tensor(lbm[:], lbp[:, 0, :], lbp[:, 1, :], ALU.max).then_inc(dve_sem, 1)
            dve.wait_ge(dve_sem, link.next())
            for r in range(2):
                ins = nc.vector.tensor_tensor(lbp[:, r, :], lbp[:, r, :], lbm[:], ALU.subtract)
            ins.then_inc(lb_args, 1)
            dve.wait_ge(lb_exps, 1)
            nc.vector.tensor_tensor(lbm[:], lbp[:, 0, :], lbp[:, 1, :], ALU.add).then_inc(lb_exps, 1)
            dve.wait_ge(lb_exps, 2)
            nc.vector.reciprocal(lbm[:], lbm[:]).then_inc(lb_exps, 1)
            dve.wait_ge(lb_exps, 3)
            nc.vector.tensor_tensor(lb[:], lbp[:, 0, :], lbm[:], ALU.mult).then_inc(lb_exps, 1)
            dve.wait_ge(lb_exps, 4)
            nc.vector.tensor_scalar(oml[:], lb[:], -1.0, 1.0, ALU.mult, ALU.add).then_inc(lb_exps, 1)
            dve.wait_ge(ws_transposed, 1)
            nc.vector.tensor_tensor(ws_t[:], half[1][:, 0, :].rearrange("p (g c) -> p g c", c=P),
                                    tri[:].to_broadcast([P, H, P]), ALU.mult).then_inc(setup_ready, 1)

            mean_squares(pos, "nm", MT, [x[:, 1, :]], [xn[:, 1, :]])
            for t in range(MT):
                scaled_row("nm", t, xn[:, t, :], x[:, t, :])
            for t in range(MT):
                rest_lo(pos, ("nm", t), a_lo[:, :, t * P:t * P + P], a_hi[:, :, t * P:t * P + P],
                        feature_tiles(out_of(pos, ("nm", t))))
            for c in range(2):
                s = slice(4 * c, 4 * c + 4)
                rest_lo(pos, ("ckt", c), kt_lo[:, s, :], kt_hi[:, s, :], feature_tiles(out_of(pos, ("ckt", c)), NM))
            for c in range(2):
                s = slice(c * 512, c * 512 + 512)
                rest_lo(pos, ("cv", c), v_lo[:, :, s], v_hi[:, :, s], out_of(pos, ("cv", c))[:, 0:MT, :])
            for p in range(2):
                n1_rows_scaled(pos, p)
            for p in range(2):
                n1_lo(pos, p)
            link.end()

            def block_vector(pos, last):
                link.start(pos)

                def blocks(t, u, w):
                    c, p = divmod(u, 2)
                    return t[:, 2 * p:2 * p + 2, c * P:c * P + P].rearrange("p j (n w) -> p j n w", w=w)

                def args(u):
                    for l in range(1, LEVELS):
                        w = 1 << l
                        src = blocks(bb, u, w)
                        mid = src[:, :, :, w // 2 - 1:w // 2].to_broadcast([P, 2, P // w, w])
                        nc.vector.tensor_tensor(lvl[u % 2][:, l - 1].rearrange("p j (n w) -> p j n w", w=w), src, mid,
                                                ALU.subtract)
                    c, p = divmod(u, 2)
                    src = bb[:, 2 * p:2 * p + 2, c * P:c * P + P]
                    nc.vector.tensor_copy(ends[u % 3][:, 0], src)
                    nc.vector.tensor_tensor(ends[u % 3][:, 1], src[:, :, P - 1:P].to_broadcast([P, 2, P]), src,
                                            ALU.subtract).then_inc(args_ready.sem, 1)

                def scaled(u):
                    dve.wait_ge(decays_ready.sem, decays_ready.at(pos, u))
                    c, p = divmod(u, 2)
                    nc.vector.tensor_copy(e_last[u % 3][:], ends[u % 3][:, 0, :, P - 1]).then_inc(dve_sem, 1)
                    tok = slice(c * P, c * P + P)
                    for l in range(1, LEVELS):
                        w = 1 << l
                        v = lvl[u % 2][:, l - 1].rearrange("p j (n w) -> p j n w", w=w)
                        for part, src in ((slice(0, w // 2), kk), (slice(w // 2, w), qq)):
                            nc.vector.tensor_tensor(v[:, :, :, part], v[:, :, :, part],
                                                    blocks(src, u, w)[:, :, :, part], ALU.mult)
                    dve.wait_ge(dve_sem, link.next())
                    for slot, src in ((0, qq), (1, kk)):
                        ins = nc.vector.tensor_tensor(ends[u % 3][:, slot], ends[u % 3][:, slot],
                                                      src[:, 2 * p:2 * p + 2, tok], ALU.mult)
                    ins.then_inc(scaled_ready.sem, 1)

                def attention(u):
                    ps = out_of(pos, ("lv", u))
                    for j in range(2):
                        v = ps[:, 2 * j:2 * j + 2, :].rearrange("p a (l c) -> p (a l) c", c=P)
                        nc.vector.tensor_tensor(v, v, masks[:], ALU.mult).then_inc(dve_sem, 1)
                        dve.wait_ge(dve_sem, link.next())
                        ins = nc.vector.tensor_reduce(att[:, j, :], v.rearrange("p l c -> p c l"), AX.X, ALU.add)
                    ins.then_inc(evacuated_of(pos, ("lv", u)), 1)

                def new_state(u):
                    p = u % 2
                    dve.wait_ge(*out(pos, ("out", u)))
                    for j in range(2):
                        h = 2 * p + j
                        ins = nc.vector.scalar_tensor_tensor(state[:, h, :], state[:, h, :], e_last[u % 3][:, j:j + 1],
                                                             added[u % 2][:, j, :], ALU.mult, ALU.add)
                    ins.then_inc(added_used.sem, 1)

                def mixed(t):
                    for h in range(H):
                        c = slice(h * P, h * P + P)
                        ins = nc.vector.scalar_tensor_tensor(vv[:, t, c], vv[:, t, c],
                                                             rstd[:, 4 * t + h:4 * t + h + 1], gate[:, t, c],
                                                             ALU.mult, ALU.mult)
                    ins.then_inc(mixed_ready.sem, 1)

                dve.wait_ge(*out(pos, "zf"))
                for h in range(H):
                    nc.vector.tensor_scalar(kk[:, h, :], kk[:, h, :], oml[:, h:h + 1], None, ALU.mult)
                dve.wait_ge(logf_ready.sem, logf_ready.at(pos, 0))
                for h in range(H):
                    for c in range(TT):
                        s = bb[:, h, c * P:c * P + P]
                        ins = nc.vector.tensor_tensor_scan(s, ones[:], s, 0.0, ALU.mult, ALU.add)
                ins.then_inc(dve_sem, 1)
                dve.wait_ge(dve_sem, link.next())
                dve.wait_ge(y_out.sem, y_out.at(pos, -1))
                args(0)
                args(1)
                dve.wait_ge(sig_ready.sem, sig_ready.at(pos, 0))
                nc.vector.tensor_tensor(qq[:], qq[:], out_of(pos, "zq")[:], ALU.mult
                                        ).then_inc(evacuated_of(pos, "zq"), 1)
                dve.wait_ge(*out(pos, "zq"))
                scaled(0)
                scaled(1)
                for u in range(UNITS):
                    dve.wait_ge(*done(pos, ("lv", u)))
                    if u + 2 < UNITS:
                        args(u + 2)
                    attention(u)
                    if u + 2 < UNITS:
                        scaled(u + 2)
                    new_state(u)
                    if u == 2:
                        dve.wait_ge(*out(pos, "zv"))
                        for t in range(TT):
                            ins = nc.vector.bn_stats(stats[:, t, :], vn[:, t, :])
                        ins.then_inc(dve_sem, 1)
                        dve.wait_ge(dve_sem, link.next())
                        nc.vector.tensor_copy(yt[:, 36:37], stats[:, TT - 1, 0:1])
                        for t in range(TT):
                            ins = nc.vector.bn_aggr(mv[:, t, :], stats[:, t, :])
                        ins.then_inc(dve_sem, 1)
                        dve.wait_ge(dve_sem, link.next())
                        nc.vector.tensor_scalar(var[:, 16:16 + TT], mv[:, :, 1], EPS, None, ALU.add
                                                ).then_inc(var_ready.sem, 1)
                    if u == 3:
                        refine(pos, "ln", TT)
                        for t in range(TT):
                            nc.vector.tensor_scalar(vn[:, t, :], vn[:, t, :], mv[:, t, 0:1], rstd[:, 16 + t:17 + t],
                                                    ALU.subtract, ALU.mult)
                        nc.vector.tensor_copy(yt[:, 36:37], rstd[:, 16:17]).then_inc(dve_sem, 1)
                        dve.wait_ge(dve_sem, link.next())
                        nc.vector.tensor_tensor(vn[:], vn[:], lng_row[:, None, :].to_broadcast([P, TT, HG]), ALU.mult
                                                ).then_inc(dve_sem, 1)
                        dve.wait_ge(dve_sem, link.next())
                        nc.vector.tensor_tensor(vn[:], vn[:], lnb_row[:, None, :].to_broadcast([P, TT, HG]), ALU.add
                                                ).then_inc(vn_ready.sem, 1)
                    if u == 4:
                        dve.wait_ge(*out(pos, "zg"))
                        nc.vector.tensor_tensor(gate[:], gate[:], hgg_row[:, None, :].to_broadcast([P, TT, HG]),
                                                ALU.mult)
                    if u == 6:
                        dve.wait_ge(o_ready.sem, o_ready.at(pos, 5))
                        newton(pos, "oa", 12, 1.0 / P)
                        for t in range(3):
                            mixed(t)
                dve.wait_ge(*out(pos, "zu"))
                dve.wait_ge(*done(pos, "mix"))
                ps = out_of(pos, "mix")
                for t in range(TT):
                    for g in range(H):
                        c = slice(g * P, g * P + P)
                        ins = nc.vector.scalar_tensor_tensor(uu[:, t, c], ps[:, t, c], bs_col[:, g:g + 1], uu[:, t, c],
                                                             ALU.add, ALU.mult)
                ins.then_inc(evacuated_of(pos, "mix"), 1)
                dve.wait_ge(o_ready.sem, o_ready.at(pos, UNITS - 1))
                newton(pos, "ob", 4, 1.0 / P)
                mixed(3)
                rest_lo(pos, "otu", a_lo[:, 4:8, :], a_hi[:, 4:8, :], out_of(pos, "otu")[:])
                rest_lo(pos, "oto", a_lo[:, 0:4, :], a_hi[:, 0:4, :], out_of(pos, "oto")[:])

                def add_to_x(job, c):
                    dve.wait_ge(*done(pos, job))
                    xc = x[:, :, c * 512:c * 512 + 512]
                    nc.vector.tensor_tensor(xc, out_of(pos, job)[:], xc, ALU.add).then_inc(evacuated_of(pos, job), 1)

                def norm_halves(tag, name):
                    for c in range(2):
                        add_to_x((name, c), c)
                        dve.wait_ge(*out(pos, (name, c)))
                        if c == 0:
                            dve.wait_ge(gain_in.sem, gain_in.at(pos, tag))
                        s = slice(c * 512, c * 512 + 512)
                        nc.vector.tensor_tensor(xg[c][:], x[:, :, s], gain[:, None, s].to_broadcast([P, TT, 512]),
                                                ALU.mult).then_inc(xn_ready.sem, 1)
                        s = slice(4 * c, 4 * c + 4)
                        rest_lo(pos, (tag, c), a_lo[:, s, :], a_hi[:, s, :], out_of(pos, (tag, c))[:])
                    mean_squares(pos, tag, TT, [x[:, t, :] for t in (2, 3)],
                                 [junk[:, t, :] for t in range(2)])

                dve.wait_ge(x_in.sem, x_in.at(pos, TT - 1))
                norm_halves("n2", "wo")
                for c in range(2):
                    rest_lo(pos, ("cq", c), b_lo[:, 4 * c:4 * c + 4, :], b_hi[:, 4 * c:4 * c + 4, :],
                            out_of(pos, ("cq", c))[:], ATT_SCALE)
                for t in range(TT + 1):
                    if t < TT:
                        dve.wait_ge(*done(pos, ("sc", t)))
                        nc.vector.tensor_reduce(
                            mx[:, t, :], out_of(pos, ("sc", t))[:, 0:2, :].rearrange("p a (h m) -> p (a h) m", m=NM),
                            AX.X, ALU.max, negate=True).then_inc(dve_sem, 1)
                        dve.wait_ge(dve_sem, link.next())
                        nc.vector.tensor_scalar(mx[:, t, :], mx[:, t, :], rstd[:, 20 + t:21 + t], None, ALU.mult
                                                ).then_inc(max_ready.sem, 1)
                    if t:
                        dve.wait_ge(*out(pos, ("sc", t - 1)))
                        nc.vector.reciprocal(rinv[:, t - 1, :], psums[:, t - 1, :]).then_inc(dve_sem, 1)
                        dve.wait_ge(dve_sem, link.next())
                        pv = pp[:, t - 1, :].rearrange("p (h m) -> p h m", m=NM)
                        nc.vector.tensor_tensor(pv, pv, rinv[:, t - 1, :, None].to_broadcast([P, H, NM]),
                                                ALU.mult).then_inc(p_ready.sem, 1)
                for job in attended_jobs:
                    name, h = job
                    s = slice(2 * h, 2 * h + 2)
                    rest_lo(pos, job, pt_lo[h % 2][:] if name == "pt" else a_lo[:, s, :],
                            pt_hi[h % 2][:] if name == "pt" else a_hi[:, s, :], out_of(pos, job)[:, 0:2, :])
                norm_halves("n3", "co")
                r3 = slice(stat("n3"), stat("n3") + TT)
                nc.vector.tensor_tensor(rstd[:, r3], rstd[:, r3], rstd[:, r3], ALU.mult).then_inc(dve_sem, 1)
                dve.wait_ge(dve_sem, link.next())

                def relu_square(e, f=0):
                    dve.wait_ge(relu_ready.sem, relu_ready.at(pos, e + f * 2))
                    nc.vector.tensor_tensor(relu[:], relu[:], out_of(pos, ("up", e))[:], ALU.mult
                                            ).then_inc(sq_ready.sem, 1)
                    dve.wait_ge(ht_hi_ready.sem, ht_hi_ready.at(pos, e + f * 2))
                    nc.vector.tensor_tensor(ht_lo[e % 2][:], relu[:], ht_hi[e % 2][:].bitcast(F32),
                                            ALU.subtract).then_inc(evacuated_of(pos, ("up", e)), 1)

                def add_down(e, c, f=0):
                    dve.wait_ge(*done(pos, ("dn", e, c), f))
                    for t in range(TT):
                        xc = x[:, t, c * 512:c * 512 + 512]
                        ins = nc.vector.scalar_tensor_tensor(xc, out_of(pos, ("dn", e, c))[:, t, :],
                                                             rstd[:, 24 + t:25 + t], xc, ALU.mult, ALU.add)
                    ins.then_inc(evacuated_of(pos, ("dn", e, c)), 1)

                relu_square(0)
                with dve.Fori(0, 3) as f:
                    for e in range(2):
                        relu_square(e + 1, f)
                        for c in range(2):
                            add_down(e, c, f)
                relu_square(7)
                for p in range(2):
                    if not last:
                        n1_rows_scaled(pos, p)
                    add_down(6 + p, 0)
                    if not last:
                        n1_lo(pos, p)
                    add_down(6 + p, 1)
                dve.wait_ge(*out(pos, ("dn", 7, 1)))
                mean_squares(pos, "y", TT, [x[:, t, :] for t in (2, 3)], [xn[:, t, :] for t in (2, 3)])
                dve.wait_ge(gain_in.sem, gain_in.at(pos, "y"))
                for t in range(TT):
                    scaled_row("y", t, xn[:, t, :], x[:, t, :])
                link.end()

            with dve.Fori(0, NB - 1) as b:
                block_vector(("block", b), False)
            block_vector(last_block, True)

            link.start(("sample", 0))

            def newton_s(tag, n, inv):
                if inv:
                    nc.vector.tensor_scalar(var[SQ, 0:n], ss[SQ, 0:n], inv, EPS, ALU.mult, ALU.add).then_inc(dve_s.did("var_" + tag), 1)
                dve.wait_ge(*step("rstd_" + tag))
                nc.vector.scalar_tensor_tensor(yt[SQ, 0:n], y0[SQ, 0:n], -0.5, y0[SQ, 0:n], ALU.mult, ALU.mult).then_inc(dve_sem, 1)
                dve.wait_ge(dve_sem, link.next())
                nc.vector.tensor_tensor(yt[SQ, 0:n], yt[SQ, 0:n], var[SQ, 0:n], ALU.mult).then_inc(dve_sem, 1)
                dve.wait_ge(dve_sem, link.next())
                nc.vector.scalar_tensor_tensor(rstd[SQ, 0:n], yt[SQ, 0:n], 1.5, y0[SQ, 0:n], ALU.add, ALU.mult).then_inc(dve_sem, 1)
                dve.wait_ge(dve_sem, link.next())

            def norm_s(tag, name, g):
                nc.vector.tensor_tensor_reduce(out=xns[:], in0=xs[:], in1=xs[:], scale=1.0, scalar=0.0,
                                                    op0=ALU.mult, op1=ALU.add, accum_out=ss[SQ, 0:1]).then_inc(dve_sem, 1)
                dve.wait_ge(dve_sem, link.next())
                newton_s(tag, 1, 1.0 / D)
                nc.vector.scalar_tensor_tensor(xns[:], xs[:], rstd[SQ, 0:1], g, ALU.mult, ALU.mult).then_inc(dve_s.did(name), 1)

            def columns(job, name, b, n=KD, dst=xt):
                dve.wait_ge(*step(job))
                nc.vector.tensor_copy(dst[:, 0:n, :], bank(b)[:, 0:n * NS].rearrange(
                    "p (k s) -> p k s", s=NS)).then_inc(dve_s.did(name), 1)

            def add_to_xs(job, name, b, c):
                dve.wait_ge(*step(job))
                col = slice(c * 512, c * 512 + 512)
                nc.vector.tensor_tensor(xs[:, col], bank(b)[SQ, :], xs[:, col], ALU.add).then_inc(dve_s.did(name), 1)

            def requests(t):
                return t.rearrange("p h (b t) -> p (h b) t", t=DS)

            dve.wait_ge(s_first_in, 64)
            norm_s("n1", "xn1", gains[:, 0, :])
            dve.wait_ge(s_consts_in, 16 * (2 + 5 * DB))
            nc.vector.memset(qe_m[:], 0.0)
            nc.vector.tensor_tensor(ws_s[:], w4[:, :, None, :].to_broadcast([NS, H, DB, DS]),
                                    tri_own[:, None, :, :].to_broadcast([NS, H, DB, DS]), ALU.mult)
            columns("n1", "xt1", 0)
            dve.wait_ge(*step("sig"))
            for h in range(H):
                nc.vector.tensor_scalar(kk_s[:, h, :], kk_s[:, h, :], oml[:, h:h + 1], None, ALU.mult)
            nc.vector.tensor_tensor(qq_s[:], qq_s[:], bank(0)[:, H * NS:2 * H * NS].rearrange(
                "p (h s) -> p h s", s=NS), ALU.mult).then_inc(dve_s.did("qq"), 1)
            dve.wait_ge(*step("logf"))
            lf = requests(bb_s[:])
            for t in range(1, DS):
                nc.vector.tensor_tensor(lf[:, :, t], lf[:, :, t], lf[:, :, t - 1], ALU.add).then_inc(dve_sem, 1)
                dve.wait_ge(dve_sem, link.next())
            for l in range(1, SLV):
                w = 1 << l
                src, dst = (t.rearrange("p h (n w) -> p (h n) w", w=w) for t in (bb_s[:], dec_s[:, l - 1]))
                nc.vector.tensor_tensor(dst, src, src[:, :, w // 2 - 1:w // 2].to_broadcast([P, H * NS // w, w]),
                                        ALU.subtract)
            nc.vector.tensor_copy(dec_s[:, SLV - 1], bb_s[:])
            nc.vector.tensor_tensor(requests(dec_s[:, SLV]), lf[:, :, DS - 1:DS].to_broadcast(
                [P, H * DB, DS]), lf, ALU.subtract).then_inc(dve_s.did("args"), 1)
            dve.wait_ge(*step("decays"))
            for l in range(1, SLV):
                w = 1 << l
                v, k, q = (t.rearrange("p h (n w) -> p (h n) w", w=w) for t in (dec_s[:, l - 1], kk_s[:], qq_s[:]))
                nc.vector.tensor_tensor(v[:, :, 0:w // 2], v[:, :, 0:w // 2], k[:, :, 0:w // 2], ALU.mult)
                nc.vector.tensor_tensor(v[:, :, w // 2:w], v[:, :, w // 2:w], q[:, :, w // 2:w], ALU.mult)
            for h in range(H):
                nc.vector.tensor_copy(el_s[:, h, :], dec_s[:, SLV - 1, h].rearrange("p (b t) -> p b t", t=DS)[:, :, DS - 1])
                nc.vector.tensor_tensor(qe_m[:, h, :, 0:DS], dec_s[:, SLV - 1, h].rearrange("p (b t) -> p b t", t=DS),
                                        qq_s[:, h].rearrange("p (b t) -> p b t", t=DS), ALU.mult)
            nc.vector.tensor_tensor(dec_s[:, SLV], dec_s[:, SLV], kk_s[:], ALU.mult).then_inc(dve_s.did("scaled"), 1)
            dve.wait_ge(*step("v_rows"))
            nc.vector.tensor_tensor(vm[:], v_s[:, None, :].to_broadcast([NS, DB, HG]),
                                                   own[:, :, None].to_broadcast([NS, DB, HG]), ALU.mult).then_inc(dve_s.did("vm"), 1)
            dve.wait_ge(*step("gate"))
            nc.vector.tensor_tensor(gate_s[:], gate_s[:], hgg_row[SQ, :], ALU.mult)
            dve.wait_ge(*step("lv"))
            nc.vector.tensor_tensor(tmp_s[:], bank(1)[SQ, 0:H * SLV * NS].rearrange("p (h l s) -> p h l s", l=SLV, s=NS),
                                         masks[SQ, None, 0:SLV, 0:NS].to_broadcast([NS, H, SLV, NS]), ALU.mult).then_inc(dve_sem, 1)
            dve.wait_ge(dve_sem, link.next())
            nc.vector.tensor_reduce(att_s[:], tmp_s[:].rearrange("p h l s -> p h s l"), AX.X, ALU.add).then_inc(dve_s.did("att"), 1)
            dve.wait_ge(*step("zv_gelu"))
            nc.vector.bn_stats(st_s[:], vn_s[:]).then_inc(dve_sem, 1)
            dve.wait_ge(dve_sem, link.next())
            nc.vector.tensor_copy(yt[SQ, 0:1], st_s[:, 0:1])
            nc.vector.bn_aggr(mv_s[:], st_s[:]).then_inc(dve_sem, 1)
            dve.wait_ge(dve_sem, link.next())
            nc.vector.tensor_scalar(var[SQ, 0:1], mv_s[:, 1:2], EPS, None, ALU.add).then_inc(dve_s.did("var_ln"), 1)
            newton_s("ln", 1, None)
            nc.vector.tensor_scalar(vn_s[:], vn_s[:], mv_s[:, 0:1], rstd[SQ, 0:1], ALU.subtract, ALU.mult).then_inc(dve_sem, 1)
            dve.wait_ge(dve_sem, link.next())
            nc.vector.tensor_tensor(vn_s[:], vn_s[:], lng_row[SQ, :], ALU.mult).then_inc(dve_sem, 1)
            dve.wait_ge(dve_sem, link.next())
            nc.vector.tensor_tensor(vn_s[:], vn_s[:], lnb_row[SQ, :], ALU.add).then_inc(dve_s.did("vn"), 1)
            dve.wait_ge(*step("o_rows"))
            nc.vector.tensor_tensor(xns[:, 0:HG], o_s[:], o_s[:], ALU.mult).then_inc(dve_sem, 1)
            dve.wait_ge(dve_sem, link.next())
            nc.vector.tensor_reduce(ss[SQ, 0:H], xns[:, 0:HG].rearrange("p (h c) -> p h c", h=H), AX.X, ALU.add).then_inc(dve_sem, 1)
            dve.wait_ge(dve_sem, link.next())
            newton_s("o", H, 1.0 / P)
            dve.wait_ge(*step("mix"))
            dve.wait_ge(*step("zu_gelu"))
            for g in range(H):
                col = slice(g * P, g * P + P)
                ins = nc.vector.scalar_tensor_tensor(u_s[:, col], bank(7)[SQ, col], b4[:, g:g + 1], u_s[:, col],
                                                     ALU.add, ALU.mult)
            ins.then_inc(dve_s.did("mixed_cm"), 1)
            for h in range(H):
                col = slice(h * P, h * P + P)
                ins = nc.vector.scalar_tensor_tensor(o_s[:, col], o_s[:, col], rstd[SQ, h:h + 1], gate_s[:, col],
                                                     ALU.mult, ALU.mult)
            ins.then_inc(dve_s.did("mixed"), 1)
            columns("ot", "xt_ot", 0)
            for h in range(H):
                ins = nc.vector.tensor_tensor(s0[:, :, h, :], s0[:, :, h, :], el_s[:, h, :, None].to_broadcast([P, DB, P]),
                                              ALU.mult)
            ins.then_inc(dve_sem, 1)
            dve.wait_ge(dve_sem, link.next())
            for j in range(8):
                h, r0 = divmod(j, 2)
                dve.wait_ge(*step(f"st{j}"))
                s = s0[:, 4 * r0:4 * r0 + 4, h, :]
                nc.vector.tensor_tensor(s, bank(4 + j % 4).rearrange("p (b v) -> p b v", v=P), s,
                                                            ALU.add).then_inc(dve_s.did(f"new{j}"), 1)
                if j == 3:
                    add_to_xs("wo0", "x_wo0", 1, 0)
            add_to_xs("wo1", "x_wo1", 2, 1)
            dve.wait_ge(*step("x_wo1"))
            norm_s("n2", "xn2", gains[:, 1, :])
            columns("n2", "xt2", 0)
            dve.wait_ge(vn_out, 16)
            nc.vector.memset(qm[:], 0.0)
            nc.vector.memset(pm[:], 0.0).then_inc(dve_sem, 1)
            dve.wait_ge(dve_sem, link.next())

            def own_tokens(job, name, b, dst):
                dve.wait_ge(*step(job))
                for k in range(KD):
                    ins = nc.vector.tensor_copy(dst[:, k, :, 0:DS], bank(b)[:, k * NS:k * NS + NS].rearrange(
                        "p (b t) -> p b t", t=DS))
                ins.then_inc(dve_s.did(name), 1)

            own_tokens("qt", "qm", 3, qm)
            for r in range(DB):
                keys_part(dve, r, 1, nc.vector.tensor_copy).then_inc(dve_s.did(f"kts{r}_1"), 1)
            dve.wait_ge(*step(f"sc{DB - 1}"))
            nc.vector.tensor_reduce(mx_s[:], half[0][SQ, :, 0:NM], AX.X, ALU.max, negate=True).then_inc(dve_s.did("max"), 1)
            dve.wait_ge(*step("p_exp"))
            nc.vector.reciprocal(rinv_s[:], sum_s[:]).then_inc(dve_sem, 1)
            dve.wait_ge(dve_sem, link.next())
            pv = q_s[:].rearrange("p (h m) -> p h m", h=H)
            nc.vector.tensor_tensor(pv, pv, rinv_s[:, :, None].to_broadcast([NS, H, NM]), ALU.mult).then_inc(dve_s.did("p_rows"), 1)
            own_tokens("pt", "pm", 4, pm)
            columns("cat", "xt_ca", 4)
            for c in range(2):
                add_to_xs(f"co{c}", f"x_co{c}", 5 + c, c)
            dve.wait_ge(*step("x_co1"))
            norm_s("n3", "xn3", gains[:, 2, :])
            columns("n3", "xt3", 0)
            for e in range(9):
                if e < 8:
                    dve.wait_ge(*step(f"relu{e}"))
                    nc.vector.tensor_tensor(relu_s[e % 2][:], relu_s[e % 2][:], bank(1 + e % 2)[SQ, :],
                                                              ALU.mult).then_inc(dve_s.did(f"sq{e}"), 1)
                if e:
                    columns(f"ht{e - 1}", f"hts{e - 1}", 3 + (e - 1) % 2, 4, hts[:, 4 * (e - 1):4 * e, :])
            for c in range(2):
                add_to_xs(f"dn3_{c}", f"x_dn{c}", 5 + c, c)
            dve.wait_ge(*step("x_dn1"))
            norm_s("y", "y", gain[SQ, :])
            link.end()


_INS = ["x_prompt", "x_sample", "mem_prompt", "state_hgrn", "cache_mem_k", "cache_mem_v", "lb_param", "g_mix", "w_in",
        "hg_norm_g", "ln_v_g", "ln_v_b", "w_s", "b_s", "w_out", "g_cross", "g_mem", "w_cq", "w_ck", "w_cv", "w_co",
        "g_mlp", "w_up", "w_down", "g_final"]
_OUTS = [(1, 2048, 1024), (8, 4, 1024), (1, 1, 4, 128, 128), (1, 8, 4, 128, 128), (1, 1, 256, 4, 256),
         (1, 1, 256, 4, 256), (1, 8, 4, 512)]


def kernel(**inputs):
    import numpy as _np
    import concourse.bacc as _bacc
    from concourse import mybir as _mybir
    from concourse.bass_utils import run_bass_kernel_spmd as _run

    s, t = _np.arange(P)[:, None], _np.arange(P)[None, :]
    masks = [s == t]
    for l in range(1, LEVELS):
        w = 1 << l
        masks.append((s // w == t // w) & (s % w < w // 2) & (t % w >= w // 2))
    consts = {"c_ident": s == t, "c_ones": s < P + t, "c_tri": s <= t, "c_masks": _np.stack(masks, 1)}

    s, t = _np.arange(NS)[:, None], _np.arange(NS)[None, :]
    consts["c_own"] = s // DS == _np.arange(DB)[None, :]
    consts["c_tri_own"] = ((s // DS == t // DS) & (s <= t)).reshape(NS, DB, DS)

    nc = _bacc.Bacc("TRN2", target_bir_lowering=False, num_devices=1)
    arrays, I = {}, {}
    for name in _INS + list(consts):
        a = _np.ascontiguousarray(inputs[name] if name in inputs else consts[name].astype(_np.float32))
        arrays[f"in_{name}"] = a
        I[name] = nc.dram_tensor(f"in_{name}", a.shape, _mybir.dt.from_np(a.dtype), kind="ExternalInput").ap()
    O = [nc.dram_tensor(f"out_{i}", shape, F32, kind="ExternalOutput").ap() for i, shape in enumerate(_OUTS)]
    program(nc, I, O)
    r = _run(nc, [arrays], core_ids=[0])
    return tuple(r.results[0][f"out_{i}"] for i in range(len(_OUTS)))
```

```python
import concourse.bass as bass
from concourse import mybir
from contextlib import ExitStack

F32 = mybir.dt.float32
F32R = mybir.dt.float32r
ACT = mybir.ActivationFunctionType
ALU = mybir.AluOpType
AX = mybir.AxisListType

P = 128
D = 1024
KD = D // P
SEQ = 2048
BT = 512
NB = SEQ // BT
TT = BT // P
HG = 512
H = 4
FF = 4096
NM = 256
MT = NM // P
XD = 256
DB, DS = 8, 4
NS = DB * DS
EPS = 1e-6
RING = 8
RAW = 4
LEVELS = 8
UNITS = TT * 2
ATT_SCALE = XD ** -0.5

W_TILES = {"mem": 4 * KD, "block": 28 * KD, "last": 28 * KD}
SWAP = 4
FILL = (5, 3, 3, 3, 2, 3, 3, 2)
ATTENDED = (("pt", 0), ("pt", 1), ("ca", 0), ("ca", 1), ("pt", 2), ("pt", 3), ("ca", 2), ("ca", 3))
SG = NS + DS
SLV = 3
WS = 4
KV = 4

PE_STEPS = (["n1", "zf", "zq", "zt", "zi", "zg", "zv", "lv", "kt", "o", "zu", "mix", "ot"]
            + [f"st{j}" for j in range(4)] + ["wo0"] + [f"st{j}" for j in range(4, 8)] + ["wo1"]
            + ["n2", "cq0", "cq1", "qt"]
            + [s for b in range(DB + 1) for s in ([f"kt{b}_0", f"kt{b}_1"] if b < DB else [])
               + ([f"sc{b - 1}"] if b else [])]
            + ["pt"] + [f"ca{b}" for b in range(DB)] + ["cat", "co0", "co1", "n3"]
            + [s for e in range(9) for s in ([f"up{e}"] if e < 8 else []) + ([f"ht{e - 1}"] if e else [])]
            + [f"dn{r}_{c}" for r in range(4) for c in range(2)])
ACT_STEPS = (["rstd_n1", "zf_rows", "zq_rows", "sig", "v_rows", "gate", "logf", "decays", "zv_gelu", "kd_rows", "rstd_ln",
              "o_rows", "rstd_o", "zu_gelu", "rstd_n2", "q_rows0", "q_rows1"]
             + [f"kts{b}_0" for b in range(DB)] + ["p_exp"] + ["ca_rows", "rstd_n3"] + [f"relu{e}" for e in range(8)]
             + ["rstd_y"])
DVE_STEPS = (["var_n1", "xn1", "xt1", "qq", "args", "scaled", "vm", "att", "var_ln", "vn", "var_o", "mixed_cm", "mixed",
              "xt_ot"]
             + [f"new{j}" for j in range(4)] + ["x_wo0"] + [f"new{j}" for j in range(4, 8)] + ["x_wo1"]
             + ["var_n2", "xn2", "xt2", "qm"] + [f"kts{b}_1" for b in range(DB)]
             + ["max", "p_rows", "pm", "xt_ca", "x_co0", "x_co1", "var_n3", "xn3", "xt3"]
             + [s for e in range(9) for s in ([f"sq{e}"] if e < 8 else []) + ([f"hts{e - 1}"] if e else [])]
             + ["x_dn0", "x_dn1", "var_y", "y"])


PHASES = (("mem", 1), ("block", NB - 1), ("last", 1), ("sample", 1))


def before(per, pos):
    phase, b = pos
    n = 0
    for name, times in PHASES:
        if name == phase:
            return b * per[name], n
        n += times * per[name]


class Event:

    def __init__(self, sem, mem=0, block=0, last=None, step=1, prime=0):
        self.sem, self.step, self.prime = sem, step, prime
        self.names = {"mem": mem, "block": block, "last": block if last is None else last}
        self.per = {k: v if isinstance(v, int) else len(v) for k, v in self.names.items()}

    def at(self, pos, i):
        if isinstance(i, (str, tuple)):
            i = self.names[pos[0]].index(i)
        turns, n = before(self.per, pos)
        return turns * self.step + (i + (n + 1)) * self.step + self.prime


class Links:

    def __init__(self, sem, **per):
        self.sem, self.per = sem, per
        self.n, self.pos = 0, ("mem", 0)

    def start(self, pos):
        self.n, self.pos = 0, pos

    def next(self):
        self.n += 1
        turns, n = before(self.per, self.pos)
        return turns + (n + self.n)

    def end(self):
        want = self.per[self.pos[0]]
        assert self.n == want, (self.sem, self.pos[0], self.n, want)


def block_jobs(last):
    jobs = [(1, "zf"), (0, "zi"), (1, "zq"), (1, "kt"), (0, "zv"), (0, "zg")]
    for u in range(UNITS):
        h = 1 if u < SWAP else 0
        jobs += [(h, ("lv", u))] + {6: [(1, "zu")], 7: [(1, "otu")]}.get(u, []) + [(h, ("out", u))]
        jobs += [(1, "mix")] if u == 6 else []
    jobs += [(1, ("wo", 0)), (0, "oto"), (1, ("n2", 0)), (0, ("wo", 1))]
    jobs += [(0, ("n2", 1)), (1, ("cq", 0)), (0, ("cq", 1)), (1, ("sc", 0)), (0, ("sc", 1))]
    jobs += [(1 if name == "pt" else 0, (name, h)) for name, h in ATTENDED]
    jobs += [(1, ("co", 0)), (1, ("n3", 0)), (0, ("co", 1)), (0, ("n3", 1)), (1, ("up", 0))]
    mlp = []
    for e in range(FF // 512 - 1):
        mlp += [("up", e + 1), ("dn", e, 0), ("dn", e, 1)]
    mlp += [("dn", FF // 512 - 1, 0), ("dn", FF // 512 - 1, 1)]
    for i, job in enumerate(mlp):
        if not last and job in (("dn", 6, 1), ("dn", 7, 1)):
            jobs += [(1, ("n1", job[1] - 6))]
        jobs += [(i % 2, job)]
    return jobs


def mem_jobs():
    jobs = [("nm", t) for t in range(MT)]
    for c in range(2):
        jobs += [("ck", c), ("ckt", c)]
    return [(i % 2, job) for i, job in enumerate(jobs + [("cv", 0), ("n1", 1), ("cv", 1), ("n1", 0)])]


def weight_tiles(job):
    name = job if isinstance(job, str) else job[0]
    if name in ("zf", "zq", "zi", "zg", "zv", "zu", "wo", "cq", "co", "up", "ck", "cv"):
        return KD
    return 4 if name == "dn" else 0


class Steps:

    def __init__(self, sem, names):
        self.sem, self.names, self.n = sem, names, 0

    def did(self, name):
        assert self.names[self.n] == name, (self.names[self.n], name)
        self.n += 1
        return self.sem


class Jobs:

    def __init__(self):
        self.lists = {"mem": mem_jobs(), "block": block_jobs(False), "last": block_jobs(True)}
        self.of, self.counts = {}, {}
        for phase, jobs in self.lists.items():
            tiles = done = 0
            uses = [0, 0]
            for h, job in jobs:
                n = weight_tiles(job)
                self.of[phase, job] = (h, uses[h], tiles, tiles + n - 1, done)
                uses[h] += 1
                tiles += n
                done += not n
            assert tiles == W_TILES[phase], (phase, tiles)
            self.counts[phase] = (uses[0], uses[1], tiles, done)


def program(nc, I, O):
    jobs = Jobs()
    ctx = ExitStack()

    def sb(name, shape, dt=F32, stack=ctx):
        return stack.enter_context(nc.sbuf_tensor(name, shape, dt))

    def sem(name):
        return ctx.enter_context(nc.semaphore(name))

    def event(name, mem=0, block=0, last=None, step=1, prime=0):
        return Event(sem(name), mem, block, last, step, prime)

    with ctx:
        w_raw = sb("w_raw", [P, RAW, 512])
        with ExitStack() as z:
            w_smp = [sb(f"w_smp{i}", [P, KD, 512], F32, z) for i in (2, 3)]
        w_hi = sb("w_hi", [P, RING, 512], F32R)
        w_lo = sb("w_lo", [P, RING, 512], F32R)
        zero = sb("zero", [P, 1])
        ident = sb("ident", [P, P])
        ones = sb("ones", [P, P])
        masks = sb("masks", [P, LEVELS, P])
        ws_t = sb("ws_t", [P, H, P])
        hgg_row = sb("hgg_row", [P, HG])
        lng_row = sb("lng_row", [P, HG])
        lnb_row = sb("lnb_row", [P, HG])
        bs_col = sb("bs_col", [P, H])
        lb = sb("lb", [P, H])
        oml = sb("oml", [P, H])
        gain = sb("gain", [P, D])
        ss = sb("ss", [P, 37])
        var = sb("var", [P, 37])
        lnv = sb("lnv", [P, 37])
        y0 = sb("y0", [P, 37])
        yt = sb("yt", [P, 37])
        rstd = sb("rstd", [P, 37])
        state = sb("state", [P, H, P])
        own = sb("own", [NS, DB])
        tri_own = sb("tri_own", [NS, DB, DS])
        masks_s = sb("masks_s", [NS, SLV, NS])
        w4 = sb("w4", [NS, H, DS])
        b4 = sb("b4", [NS, H])
        with ExitStack() as z:
            w_smp = [sb(f"w_smp{i}", [P, KD, 512], F32, z) for i in (0, 1)] + w_smp
        kt_hi = sb("kt_hi", [P, KD, NM], F32R)
        kt_lo = sb("kt_lo", [P, KD, NM], F32R)
        v_hi = sb("v_hi", [P, MT, D], F32R)
        v_lo = sb("v_lo", [P, MT, D], F32R)
        with ExitStack() as z:
            kv = [sb(f"kv{i}", [P, MT, D], F32, z) for i in range(KV)]
        a_hi = sb("a_hi", [P, KD, BT], F32R)
        a_lo = sb("a_lo", [P, KD, BT], F32R)
        with ExitStack() as y:
            s0 = sb("s0", [P, DB, H, P], F32, y)
            gains = sb("gains", [NS, 2, D], F32, y)
            xt = sb("xt", [P, KD, NS], F32, y)
            with ExitStack() as z:
                vm = sb("vm", [NS, DB, HG], F32, z)
                zfq = sb("zfq", [NS, 2, HG], F32, z)
                v_s, gate_s, vn_s, o_s = (sb(n, [NS, HG], F32, z) for n in ("v_s", "gate_s", "vn_s", "o_s"))
                u_s = sb("u_s", [NS, HG], F32, z)
                kk_s, qq_s, bb_s = (sb(n, [P, H, NS], F32, z) for n in ("kk_s", "qq_s", "bb_s"))
                dec_s = sb("dec_s", [P, SLV + 1, H, NS], F32, z)
                qe_m = sb("qe_m", [P, H, DB, SG], F32, z)
                el_s = sb("el_s", [P, H, DB], F32, z)
                tmp_s = sb("tmp_s", [NS, H, SLV, NS], F32, z)
                att_s = sb("att_s", [NS, H, NS], F32, z)
                kd_s = sb("kd_s", [NS, HG], F32, z)
                ws_s = sb("ws_s", [NS, H, DB, DS], F32, z)
                st_s = sb("st_s", [NS, 6], F32, z)
                mv_s = sb("mv_s", [NS, 2], F32, z)
            with ExitStack() as z:
                kts = [sb(f"kts{i}", [P, KD, NM], F32, z) for i in range(2)]
                qm = sb("qm", [P, KD, DB, SG], F32, z)
                pm = sb("pm", [P, KD, DB, SG], F32, z)
                q_s = sb("q_s", [NS, D], F32, z)
                mx_s, sum_s, rinv_s = (sb(n, [NS, H], F32, z) for n in ("mx_s", "sum_s", "rinv_s"))
            with ExitStack() as z:
                relu_s = [sb(f"relu_s{i}", [NS, 512], F32, z) for i in range(2)]
                hts = sb("hts", [P, FF // P, NS], F32, z)
        with ExitStack() as z:
            sb("below_xs", [P, 18 * D], F32, z)
            xs = sb("xs", [NS, D], F32, z)
            xns = sb("xns", [NS, D], F32, z)
        with ExitStack() as z:
            x = sb("x", [P, TT, D], F32, z)
        with ExitStack() as z:
            kk = sb("kk", [P, H, BT], F32, z)
            qq = sb("qq", [P, H, BT], F32, z)
        sb("zone_x", [P, TT, D])
        with ExitStack() as z:
            bb = sb("bb", [P, H, BT], F32, z)
            vv = sb("vv", [P, TT, HG], F32, z)
            gate = sb("gate", [P, TT, HG], F32, z)
            vn = sb("vn", [P, TT, HG], F32, z)
            uu = sb("uu", [P, TT, HG], F32, z)
            lvl = [sb(f"lvl{i}", [P, LEVELS - 1, 2, P], F32, z) for i in range(2)]
            ends = [sb(f"ends{i}", [P, 2, 2, P], F32, z) for i in range(3)]
            att = sb("att", [P, 2, P], F32, z)
            kdt = sb("kdt", [P, 2, P], F32, z)
            added = [sb(f"added{i}", [P, 2, P], F32, z) for i in range(2)]
            osq = sb("osq", [P, 2, P], F32, z)
            e_last = [sb(f"e_last{i}", [P, 2], F32, z) for i in range(3)]
            stats = sb("stats", [P, TT, 6], F32, z)
            mv = sb("mv", [P, TT, 2], F32, z)
        with ExitStack() as z:
            b_hi = sb("b_hi", [P, KD, BT], F32R, z)
            b_lo = sb("b_lo", [P, KD, BT], F32R, z)
            pp = sb("pp", [P, TT, D], F32, z)
            pt_hi = [sb(f"pt_hi{i}", [P, MT, BT], F32R, z) for i in range(2)]
            pt_lo = [sb(f"pt_lo{i}", [P, MT, BT], F32R, z) for i in range(2)]
            mx = sb("mx", [P, TT, H], F32, z)
            psums = sb("psums", [P, TT, H], F32, z)
            rinv = sb("rinv", [P, TT, H], F32, z)
        with ExitStack() as z:
            ht_hi = [sb(f"ht_hi{i}", [P, 4, BT], F32R, z) for i in range(2)]
            ht_lo = [sb(f"ht_lo{i}", [P, 4, BT], F32R, z) for i in range(2)]
            relu = sb("relu", [P, 4, BT], F32, z)
            xn = sb("xn", [P, TT, D], F32, z)
            nx = [sb(f"nx{i}", [P, D], F32, z) for i in range(2)]
        with ExitStack() as z:
            sb("below_junk", [P, 6 * D], F32, z)
            junk = sb("junk", [P, 2, D], F32, z)
            sb("below_xg", [P, 2 * D], F32, z)
            xg = [sb(f"xg{i}", [P, TT, 512], F32, z) for i in range(2)]
        with ExitStack() as z:
            kn = [sb(f"kn{i}", [P, MT, 512], F32, z) for i in range(4)]
            ws_raw = sb("ws_raw", [P, H, P], F32, z)
            lbp = sb("lbp", [P, 2, H], F32, z)
            lbm = sb("lbm", [P, H], F32, z)
        half = [ctx.enter_context(nc.psum_tensor(f"half{i}", [P, 4, 512], F32)) for i in range(2)]

        phases = ("mem", "block", "last")
        h0, h1, tl, dn = zip(*(jobs.counts[p] for p in phases))
        mem_in, consts_in = sem("mem_in"), sem("consts_in")
        w_in = [Event(sem(f"w_in{i}"), *(n // RAW for n in tl), step=16) for i in range(RAW)]
        w_rounded = sem("w_rounded")
        w_split = event("w_split", *tl, prime=RAW)
        w_used = event("w_used", *tl, prime=RING)
        pe_done = event("pe_done", *dn)
        evacuated = [event("evacuated0", *h0, prime=1), event("evacuated1", *h1, prime=1)]
        x_in = event("x_in", 0, TT, step=16)
        nx_in = [event(f"nx_in{i}", 2, 2, 0, step=16) for i in range(2)]
        gain_in = event("gain_in", ["n1"], ["n2", "n3", "n1", "y"], step=16)
        mixers = ["ln", "oa", "ob"]
        norms = {"mem": ["nm", "n1a", "n1b"], "block": ["n2", "n3", "n1a", "n1b", "y"], "last": ["n2", "n3", "y"]}
        ssq_ready = event("ssq_ready", *(norms[p] for p in phases))
        all_norms = [norms["mem"], mixers + norms["block"], mixers + norms["last"]]
        var_ready = event("var_ready", *all_norms)
        rstd0_ready = event("rstd0_ready", *all_norms)
        n1_rows, y_rows = [("n1", t) for t in range(TT)], [("y", t) for t in range(TT)]
        halves = [(n, c) for n in ("n2", "n3") for c in range(2)]
        xn_ready = event("xn_ready", [("nm", t) for t in range(MT)] + n1_rows, halves + n1_rows + y_rows,
                         halves + y_rows)
        y_out = event("y_out", 0, TT, step=16, prime=16 * TT)
        split = ["otu", "oto", ("n2", 0), ("n2", 1), ("cq", 0), ("cq", 1), *ATTENDED, ("n3", 0), ("n3", 1)]
        hi_ready = event("hi_ready", [("nm", 0), ("nm", 1), ("ckt", 0), ("ckt", 1), ("cv", 0), ("n1", 1), ("cv", 1),
                                      ("n1", 0)], split + [("n1", 0), ("n1", 1)], split)
        sig_ready = event("sig_ready", 0, 1)
        logf_ready = event("logf_ready", 0, 1)
        vn_ready = event("vn_ready", 0, 1)
        args_ready = event("args_ready", 0, UNITS)
        decays_ready = event("decays_ready", 0, UNITS)
        scaled_ready = event("scaled_ready", 0, UNITS)
        o_ready = event("o_ready", 0, UNITS)
        added_used = event("added_used", 0, UNITS)
        mixed_ready = event("mixed_ready", 0, TT)
        max_ready = event("max_ready", 0, 2 * TT)
        exp_ready = event("exp_ready", 0, 2 * TT - 2)
        p_ready = event("p_ready", 0, 2)
        relu_ready = event("relu_ready", 0, 8)
        sq_ready = event("sq_ready", 0, 8)
        ht_hi_ready = event("ht_hi_ready", 0, 8)
        ws_transposed, lb_args, lb_exps, setup_ready = (
            sem(n) for n in ("ws_transposed", "lb_args", "lb_exps", "setup_ready"))
        kn_out, s_out = sem("kn_out"), sem("s_out")
        act_sem, dve_sem = sem("act_chain"), sem("dve_chain")
        s_gains_in = sem("s_gains_in")
        s_consts_in, s_first_in, s0_in, vn_out, s_out_done = (
            sem(n) for n in ("s_consts_in", "s_first_in", "s0_in", "vn_out", "s_out_done"))
        ws_in = [sem(f"ws_in{i}") for i in range(WS)]
        kv_in = [sem(f"kv_in{i}") for i in range(KV)]
        pe_s, act_s, dve_s = (Steps(sem(n), names) for n, names in (
            ("pe_steps", PE_STEPS), ("act_steps", ACT_STEPS), ("dve_steps", DVE_STEPS)))

        def step(name):
            steps, = (x for x in (pe_s, act_s, dve_s) if name in x.names)
            return steps.sem, steps.names.index(name) + 1

        def bank(i):
            return half[i // 4][:, i % 4, :]

        def own_columns(m):
            return m[:, :, :, 0:DS]

        def of_request(m, k, b):
            return m[:, k].rearrange("p b s -> p (b s)")[:, b * NS:b * NS + NS]

        last_block = ("last", 0)

        def stat(tag):
            return {"nm": 28, "n1a": 28, "n1b": 30, "y": 32, "ln": 16, "oa": 0, "ob": 12, "n2": 20, "n3": 24}[tag]

        SQ = slice(0, NS)

        def keys_part(eng, r, part, copy):
            eng.wait_ge(*step(f"kt{r}_{part}"))
            if r >= 2:
                eng.wait_ge(*step(f"sc{r - 2}"))
            ps = half[1][:, 2 * part:2 * part + 2, :].rearrange("p a (i m) -> p (a i) m", m=NM)
            return copy(kts[r % 2][:, 4 * part:4 * part + 4, :], ps)


        def done(pos, job, f=0):
            _, _, _, last, n = jobs.of[pos[0], job]
            if weight_tiles(job):
                return w_used.sem, w_used.at(pos, last + f * (4 * KD))
            return pe_done.sem, pe_done.at(pos, n)

        def out(pos, job, f=0):
            h, use, *_ = jobs.of[pos[0], job]
            return evacuated[h].sem, evacuated[h].at(pos, use + f * 3)

        def evacuated_of(pos, job):
            return evacuated[jobs.of[pos[0], job][0]].sem

        def out_of(pos, job):
            return half[jobs.of[pos[0], job][0]]

        def pair(pos, p, a):
            return (a[:, :, 2 * p * P:2 * p * P + 2 * P].rearrange("p k (t c) -> p k t c", c=P),
                    out_of(pos, ("n1", p)).rearrange("p (t a) (k c) -> p (a k) t c", t=2, c=P))

        def feature_tiles(ps, width=P):
            return ps[:, 0:2, :].rearrange("p a (k c) -> p (a k) c", c=width)

        block = ctx.enter_context(nc.Block())

        n_consts = 8

        @block.sync
        def _(sp):
            sp.sem_inc(y_out.sem, y_out.prime)
            for dst, src in ((x[:, 0:MT, :], I["mem_prompt"][0].rearrange("(t p) d -> p t d", p=P)),
                             (ident[:], I["c_ident"]), (gain[:], I["g_mem"][0:1, :].broadcast_to([P, D]))):
                sp.dma_start(dst, src).then_inc(mem_in, 16)

            def load_consts():
                for dst, src in ((ws_raw[:], I["w_s"][0].rearrange("g t s -> t g s")),
                                 (lbp[:], I["lb_param"].rearrange("r (h p) -> p r h", p=P)),
                                 (ones[:], I["c_ones"]), (masks[:], I["c_masks"]),
                                 (hgg_row[:], I["hg_norm_g"][0:1, :].broadcast_to([P, HG])),
                                 (lng_row[:], I["ln_v_g"][0:1, :].broadcast_to([P, HG])),
                                 (lnb_row[:], I["ln_v_b"][0:1, :].broadcast_to([P, HG])),
                                 (bs_col[:], I["b_s"][0].rearrange("g t -> t g"))):
                    with nc.allow_non_contiguous_dma(reason="small constants"):
                        sp.dma_start(dst, src).then_inc(consts_in, 16)

            def load(pos, i0, w, row0, col0, ks=range(KD)):
                for i, k in enumerate(ks):
                    s = i % RAW
                    sp.wait_ge(w_split.sem, w_split.at(pos, i0 + i) - RAW)
                    sp.dma_start(w_raw[:, s, :], w[bass.ds(row0 + k * P, P), bass.ds(col0, 512)]
                                 ).then_inc(w_in[s].sem, 16)

            def load_gain(g):
                sp.dma_start(gain[:], g.broadcast_to([P, D])).then_inc(gain_in.sem, 16)

            def load_nx(t, row):
                sp.dma_start(nx[t % 2][:], I["x_prompt"][0, bass.ds(row + t * P, P), :]
                           ).then_inc(nx_in[t % 2].sem, 16)

            pos = ("mem", 0)
            for i, (w, c) in enumerate((w, c) for w in ("w_ck", "w_cv") for c in range(2)):
                load(pos, i * KD, I[w][0], 0, c * 512)
                if i == 0:
                    load_nx(0, 0)
                    load_nx(1, 0)
                    load_consts()
                    sp.wait_ge(xn_ready.sem, xn_ready.at(pos, ("nm", MT - 1)))
                    load_gain(I["g_mix"][0:1, :])
                for t in (2, 3) if i == 1 else ():
                    sp.wait_ge(xn_ready.sem, xn_ready.at(pos, ("n1", t - 2)))
                    load_nx(t, 0)

            def block_loads(pos, row, last):
                w_in_ = I["w_in"][0]
                for i, c in enumerate((512, 1024, 0, 2560, 1536, 2048)):
                    load(pos, i * KD, w_in_, 0, c)
                    if i == 2:
                        sp.wait_ge(xn_ready.sem, xn_ready.at(pos, -1))
                        load_gain(I["g_cross"][0:1, :])
                load(pos, 6 * KD, I["w_out"][0], 0, 0, (4, 5, 6, 7, 0, 1, 2, 3))
                sp.wait_ge(*out(pos, ("lv", UNITS - 1)))
                for t in range(TT):
                    sp.dma_start(x[:, t, :], I["x_prompt"][0, bass.ds(row + t * P, P), :]).then_inc(x_in.sem, 16)
                load(pos, 7 * KD, I["w_out"][0], 0, 512)
                for c in range(2):
                    load(pos, (8 + c) * KD, I["w_cq"][0], 0, c * 512)
                sp.wait_ge(xn_ready.sem, xn_ready.at(pos, ("n2", 1)))
                load_gain(I["g_mlp"][0:1, :])
                for c in range(2):
                    load(pos, (10 + c) * KD, I["w_co"][0], 0, c * 512)
                load(pos, 12 * KD, I["w_up"][0], 0, 0)
                sp.wait_ge(*out(pos, ("ca", H - 1)))
                if last:
                    with nc.allow_non_contiguous_dma(reason="small constants"):
                        sp.dma_start(own[:], I["c_own"]).then_inc(s_consts_in, 16)
                        sp.dma_start(tri_own[:], I["c_tri_own"]).then_inc(s_consts_in, 16)
                        sp.dma_start(masks_s[:], I["c_masks_s"]).then_inc(s_consts_in, 16)
                        for r in range(DB):
                            rows = slice(r * DS, r * DS + DS)
                            for g in range(H):
                                sp.dma_start(w4[rows, g, :], I["w_s"][0, g, 0:DS, 0:DS].rearrange("t s -> s t")
                                           ).then_inc(
                                    s_consts_in, 16)
                            sp.dma_start(b4[rows, :], I["b_s"][0, :, 0:DS].rearrange("g t -> t g")
                                       ).then_inc(s_consts_in, 16)
                    sp.dma_start(xs[:], I["x_sample"].rearrange("b t d -> (b t) d")).then_inc(s_first_in, 16)
                else:
                    load_nx(0, row + BT)
                    load_nx(1, row + BT)
                sp.wait_ge(xn_ready.sem, xn_ready.at(pos, ("n3", 1)))
                load_gain(I["g_mix"][0:1, :])
                with sp.Fori(0, FF // 512 - 1) as e:
                    load(pos, 13 * KD + e * (2 * KD), I["w_up"][0], 0, e * 512 + 512)
                    for c in range(2):
                        load(pos, 14 * KD + 4 * c + e * (2 * KD), I["w_down"][0], e * 512, c * 512, range(4))
                load(pos, 27 * KD, I["w_down"][0], FF - 512, 0, range(4))
                for t in (2, 3) if not last else ():
                    sp.wait_ge(xn_ready.sem, xn_ready.at(pos, ("n1", t - 2)))
                    load_nx(t, row + BT)
                load(pos, 27 * KD + 4, I["w_down"][0], FF - 512, 512, range(4))
                if last:
                    sp.wait_ge(*step("xn1"))
                else:
                    sp.wait_ge(xn_ready.sem, xn_ready.at(pos, ("n1", TT - 1)))
                load_gain(I["g_final"][None, :])

            with sp.Fori(0, NB - 1) as b:
                block_loads(("block", b), b * BT, False)
            block_loads(last_block, (NB - 1) * BT, True)

            chunks = ([(n, I["w_in"][0], 0, col) for n, col in (("zf", 512), ("zq", 0), ("zi", 1024), ("zg", 1536),
                                                                 ("zv", 2560), ("zu", 2048))]
                      + [(f"{n}{c}", I[w][0], 0, c * 512) for n, w in (("wo", "w_out"), ("cq", "w_cq"), ("co", "w_co"))
                         for c in range(2)]
                      + [(f"up{e}", I["w_up"][0], 0, e * 512) for e in range(8)]
                      + [(f"dn{r}_{c}", I["w_down"][0], r * D, c * 512) for r in range(4) for c in range(2)])

            def load_s(i0, i1):
                for i in range(i0, i1):
                    if i >= WS:
                        sp.wait_ge(*step(chunks[i - WS][0]))
                    _, w, row, col = chunks[i]
                    sp.dma_start(w_smp[i % WS][:], w[row:row + D, col:col + 512].rearrange("(k p) c -> p k c", p=P)
                                 ).then_inc(ws_in[i % WS], 16)

            def load_kv(src, i0):
                for r in range(DB):
                    i = i0 + r
                    if i >= KV:
                        sp.wait_ge(*step(f"kt{i - KV}_1" if i - KV < DB else f"ca{i - KV - DB}"))
                    sp.dma_start(kv[i % KV][:], src[0, r].rearrange("(t p) h d -> p t (h d)", p=P)
                                 ).then_inc(kv_in[i % KV], 16)

            sp.wait_ge(*out(last_block, ("ca", H - 1)))
            load_s(0, 2)
            sp.wait_ge(w_used.sem, w_used.at(last_block, W_TILES["block"] - 1))
            load_s(2, 4)
            sp.wait_ge(xn_ready.sem, xn_ready.at(last_block, ("y", TT - 1)))
            sp.dma_start(s0[:], I["state_hgrn"][0].rearrange("b h k v -> k b h v")).then_inc(s0_in, 16)
            load_s(4, 5)
            sp.wait_ge(y_out.sem, y_out.at(last_block, TT - 1))
            for i, g in enumerate(("g_cross", "g_mlp")):
                sp.dma_start(gains[:, i, :], I[g][0:1, :].broadcast_to([NS, D])).then_inc(s_gains_in, 16)
            sp.dma_start(O[2][0, 0].rearrange("h k v -> k h v"), state[:]).then_inc(s_out, 16)
            load_s(5, 10)
            load_kv(I["cache_mem_k"], 0)
            load_s(10, 11)
            load_kv(I["cache_mem_v"], DB)
            load_s(11, len(chunks))
            sp.wait_ge(s_out, 16)

        @block.gpsimd
        def _(pool):
            pool.sem_inc(w_split.sem, RAW)
            nc.gpsimd.memset(zero[:], 0.0).then_inc(w_rounded, 1)
            pool.wait_ge(w_rounded, 1)
            with pool.Fori(0, (W_TILES["mem"] + NB * W_TILES["block"]) // RING) as g:
                for k in range(RING):
                    s = k % RAW
                    pool.wait_ge(w_in[s].sem, g * (16 * RING // RAW) + 16 * (k // RAW + 1))
                    pool.wait_ge(w_used.sem, g * RING + (k + 1))
                    nc.gpsimd.tensor_tensor(w_hi[:, k, :], w_raw[:, s, :], zero[:].to_broadcast([P, 512]),
                                            ALU.add).then_inc(w_rounded, 1)
                    pool.wait_ge(w_rounded, g * RING + (k + 2))
                    nc.gpsimd.tensor_tensor(w_lo[:, k, :], w_raw[:, s, :], w_hi[:, k, :].bitcast(F32),
                                            ALU.subtract).then_inc(w_split.sem, 1)

        @block.tensor
        def _(pe):
            pe.sem_inc(w_used.sem, RING)
            for h in range(2):
                pe.sem_inc(evacuated[h].sem, 1)

            def begin(pos, job, f=0, needs=(), back=1):
                h, use, *_ = jobs.of[pos[0], job]
                last = {h: use - back}
                for j in needs:
                    hj, uj, *_ = jobs.of[pos[0], j]
                    last[hj] = max(last.get(hj, uj), uj)
                for hj, uj in sorted(last.items()):
                    pe.wait_ge(evacuated[hj].sem, evacuated[hj].at(pos, uj + f * 3))
                return half[h]

            def gemm(pos, job, kind, hi, lo, tiles=4, f=0, needs=(), ks=range(KD), turns=None):
                n, t0 = weight_tiles(job), jobs.of[pos[0], job][2]
                ks = list(ks)[:n]
                turns = range(n) if turns is None else turns
                ps = begin(pos, job, f, needs) if turns[0] == 0 else out_of(pos, job)
                for i in turns:
                    k, s = ks[i], (t0 + i) % RING
                    pe.wait_ge(w_split.sem, w_split.at(pos, t0 + i + f * (4 * KD)))
                    for j in range(tiles):
                        c = slice(j * P, j * P + P)
                        if kind == "T":
                            parts = ((w_lo[:, s, c], hi[:, k, :]), (w_hi[:, s, c], lo[:, k, :]),
                                     (w_hi[:, s, c], hi[:, k, :]))
                        else:
                            parts = ((lo[:, k, c], w_hi[:, s, :]), (hi[:, k, c], w_lo[:, s, :]),
                                     (hi[:, k, c], w_hi[:, s, :]))
                        for q, (l, r) in enumerate(parts):
                            m = nc.tensor.matmul(ps[:, j, :], l, r, start=(i == 0 and q == 0),
                                                 stop=(i == n - 1 and q == 2))
                    m.then_inc(w_used.sem, 1)

            def transposes(pos, job, tiles, needs=(), back=1, bank0=0):
                ps = begin(pos, job, 0, needs, back)
                for i, t in enumerate(tiles):
                    m = nc.tensor.transpose(ps[:, bank0 + i // 4, (i % 4) * P:(i % 4) * P + P], t, ident[:])
                m.then_inc(pe_done.sem, 1)

            def three(out, lhs, rhs, first, last):
                (lh, ll), (rh, rl) = lhs, rhs
                for i, (l, r) in enumerate(((ll, rh), (lh, rl), (lh, rh))):
                    m = nc.tensor.matmul(out, l, r, start=(first and i == 0), stop=(last and i == 2))
                return m

            def rows_transposed(pos, p):
                pe.wait_ge(xn_ready.sem, xn_ready.at(pos, ("n1", 2 * p + 1)))
                transposes(pos, ("n1", p), [xn[:, t, k * P:k * P + P] for t in (2 * p, 2 * p + 1) for k in range(KD)])

            def half_transposed(pos, tag, c):
                pe.wait_ge(xn_ready.sem, xn_ready.at(pos, (tag, c)))
                transposes(pos, (tag, c), [xg[c][:, t, k * P:k * P + P] for k in range(4) for t in range(TT)])

            pos = ("mem", 0)
            pe.wait_ge(mem_in, 48)
            for t in range(MT):
                pe.wait_ge(xn_ready.sem, xn_ready.at(pos, ("nm", t)))
                transposes(pos, ("nm", t), [xn[:, t, k * P:k * P + P] for k in range(KD)])
            for c in range(2):
                gemm(pos, ("ck", c), "M", a_hi, a_lo, MT, needs=[("nm", MT - 1)])
                transposes(pos, ("ckt", c), [kn[c][:, t, j * P:j * P + P] for j in range(4) for t in range(MT)],
                           [("ck", c)])
                if c == 0:
                    pe.wait_ge(consts_in, 16 * n_consts)
                    for g in range(H):
                        m = nc.tensor.transpose(half[1][:, 3, g * P:g * P + P], ws_raw[:, g, :], ident[:])
                    m.then_inc(ws_transposed, 1)
            gemm(pos, ("cv", 0), "M", a_hi, a_lo, MT)
            pe.wait_ge(setup_ready, 1)
            rows_transposed(pos, 1)
            gemm(pos, ("cv", 1), "M", a_hi, a_lo, MT)
            rows_transposed(pos, 0)

            def within_chunk(pos, u):
                c, p = divmod(u, 2)
                pe.wait_ge(scaled_ready.sem, scaled_ready.at(pos, u))
                if u in (0, SWAP):
                    begin(pos, ("lv", u))
                ps = out_of(pos, ("lv", u))
                tok = slice(c * P, c * P + P)
                for l in (4, 5, 6, 7, 0, 1, 2, 3):
                    if l == 0 and u not in (0, SWAP):
                        begin(pos, ("lv", u))
                    for j in range(2):
                        o = ps[:, l // 2, (2 * (l % 2) + j) * P:(2 * (l % 2) + j + 1) * P]
                        if l == 0:
                            m = nc.tensor.matmul(o, kk[:, 2 * p + j, tok], qq[:, 2 * p + j, tok], start=True, stop=True)
                            continue
                        o, q = (t.rearrange("p (n w) -> p n w", w=1 << l)[:, :, 1 << (l - 1):]
                                for t in (o, lvl[u % 2][:, l - 1, j, :]))
                        m = nc.tensor.matmul(o, lvl[u % 2][:, l - 1, j, :], q, start=True, stop=True)
                m.then_inc(pe_done.sem, 1)

            def keys_to_rows(ps, u):
                for j in range(2):
                    m = nc.tensor.transpose(ps[:, 1, (2 + j) * P:(3 + j) * P], ends[u % 3][:, 1, j, :], ident[:])
                return m

            def rows_and_state(pos, u):
                c, p = divmod(u, 2)
                if u == 0:
                    pe.wait_ge(*out(pos, "zi"))
                if u >= 2:
                    pe.wait_ge(added_used.sem, added_used.at(pos, u - 2))
                if u + 1 < UNITS:
                    pe.wait_ge(scaled_ready.sem, scaled_ready.at(pos, u + 1))
                ps = begin(pos, ("out", u))
                for j in range(2):
                    h = 2 * p + j
                    v = vv[:, c, h * P:h * P + P]
                    o = ps[:, 0, j * P:j * P + P]
                    nc.tensor.matmul(o, att[:, j, :], v, start=True, stop=False)
                    nc.tensor.matmul(o, ends[u % 3][:, 0, j, :], state[:, h, :], start=False, stop=True)
                    m = nc.tensor.matmul(ps[:, 1, j * P:j * P + P], kdt[:, j, :], v, start=True, stop=True)
                if u + 1 < UNITS:
                    m = keys_to_rows(ps, u + 1)
                m.then_inc(pe_done.sem, 1)

            def to_columns(name, b, tiles):
                for i, t in enumerate(tiles):
                    m = nc.tensor.transpose(bank(b)[:, i * NS:i * NS + NS], t, ident[0:NS, 0:NS])
                m.then_inc(pe_s.did(name), 1)

            def tiles_of(t, n=KD):
                return [t[:, k * P:k * P + P] for k in range(n)]

            def block_products(pos, last):
                def fill(part):
                    for i in range(sum(FILL[:part]), sum(FILL[:part + 1])):
                        gemm(pos, ("zv", "zg", "zu")[i // KD], "M", a_hi, a_lo, turns=[i % KD])

                gemm(pos, "zf", "T", a_hi, a_lo)
                gemm(pos, "zi", "M", a_hi, a_lo)
                gemm(pos, "zq", "T", a_hi, a_lo)
                fill(0)
                pe.wait_ge(scaled_ready.sem, scaled_ready.at(pos, 0))
                keys_to_rows(begin(pos, "kt"), 0).then_inc(pe_done.sem, 1)
                for u in range(UNITS):
                    within_chunk(pos, u)
                    if u == UNITS - 1:
                        transposes(pos, "otu", [uu[:, t, k * P:k * P + P] for k in range(H) for t in range(TT)])
                    fill(u + 1)
                    rows_and_state(pos, u)
                    if u == 6:
                        pe.wait_ge(vn_ready.sem, vn_ready.at(pos, 0))
                        ps = begin(pos, "mix")
                        for t in range(TT):
                            for g in range(H):
                                c = slice(g * P, g * P + P)
                                m = nc.tensor.matmul(ps[:, t, c], ws_t[:, g, :], vn[:, t, c], start=True, stop=True)
                        m.then_inc(pe_done.sem, 1)
                order = (4, 5, 6, 7, 0, 1, 2, 3)
                gemm(pos, ("wo", 0), "M", a_hi, a_lo, ks=order, turns=range(2))
                pe.wait_ge(mixed_ready.sem, mixed_ready.at(pos, TT - 1))
                transposes(pos, "oto", [vv[:, t, k * P:k * P + P] for k in range(H) for t in range(TT)])
                gemm(pos, ("wo", 0), "M", a_hi, a_lo, ks=order, turns=range(2, 4))
                pe.wait_ge(*out(pos, "oto"))
                gemm(pos, ("wo", 0), "M", a_hi, a_lo, ks=order, turns=range(4, 8))

                def norm_between(tag, name, nxt, kind):
                    gemm(pos, (name, 1), "M", a_hi, a_lo, turns=range(5))
                    half_transposed(pos, tag, 0)
                    gemm(pos, (name, 1), "M", a_hi, a_lo, turns=range(5, 8))
                    gemm(pos, (nxt, 0), "T", a_hi, a_lo, turns=range(2), needs=[(tag, 0)])
                    half_transposed(pos, tag, 1)
                    gemm(pos, (nxt, 0), "T", a_hi, a_lo, turns=range(2, 4))
                    pe.wait_ge(*out(pos, (tag, 1)))
                    gemm(pos, (nxt, 0), "T", a_hi, a_lo, turns=range(4, 8))

                norm_between("n2", "wo", "cq", "T")
                gemm(pos, ("cq", 1), "T", a_hi, a_lo)
                for g in range(2):
                    ps = begin(pos, ("sc", g), 0, [("cq", g)])
                    for t in range(TT):
                        q = slice(t * P, t * P + P)
                        for j in range(2):
                            h = 2 * g + j
                            for k in (2 * h, 2 * h + 1):
                                m = three(ps[:, t, j * NM:j * NM + NM], (b_hi[:, k, q], b_lo[:, k, q]),
                                          (kt_hi[:, k, :], kt_lo[:, k, :]), k == 2 * h, k == 2 * h + 1)
                    m.then_inc(pe_done.sem, 1)

                for name, h in ATTENDED:
                    b0 = 2 * (h % 2)
                    back = 1 if (name, h) == ("pt", 0) else 2
                    if name == "pt":
                        if h in (0, 2):
                            pe.wait_ge(p_ready.sem, p_ready.at(pos, h // 2))
                        transposes(pos, ("pt", h), [pp[:, t, h * NM + m * P:h * NM + m * P + P]
                                                    for m in range(MT) for t in range(TT)], back=back, bank0=b0)
                        continue
                    if h == 0:
                        pe.wait_ge(exp_ready.sem, exp_ready.at(pos, TT))
                    ps = begin(pos, ("ca", h), 0, [("pt", h)], back)
                    for dd in range(2):
                        for mm in range(MT):
                            c = slice(h * XD + dd * P, h * XD + dd * P + P)
                            m = three(ps[:, b0 + dd, :], (v_hi[:, mm, c], v_lo[:, mm, c]),
                                      (pt_hi[h % 2][:, mm, :], pt_lo[h % 2][:, mm, :]), mm == 0, mm == MT - 1)
                    m.then_inc(pe_done.sem, 1)
                gemm(pos, ("co", 0), "M", a_hi, a_lo, needs=[("ca", 1)], turns=range(4))
                pe.wait_ge(*out(pos, ("ca", H - 1)))
                gemm(pos, ("co", 0), "M", a_hi, a_lo, turns=range(4, 8))
                norm_between("n3", "co", "up", "T")

                def down(e, f=0):
                    gemm(pos, ("dn", e, 0), "M", ht_hi[e % 2], ht_lo[e % 2], f=f, needs=[("up", e)])
                    gemm(pos, ("dn", e, 1), "M", ht_hi[e % 2], ht_lo[e % 2], turns=range(2), f=f, needs=[("up", e)])
                    if e >= 6 and not last:
                        rows_transposed(pos, e - 6)
                    if e == 7 and last:
                        pe.wait_ge(*step("xn1"))
                        pe.wait_ge(*out(pos, ("dn", 7, 0)))
                        to_columns("n1", 4, tiles_of(xns))
                    gemm(pos, ("dn", e, 1), "M", ht_hi[e % 2], ht_lo[e % 2], turns=range(2, 4), f=f)

                with pe.Fori(0, 3) as f:
                    for e in range(2):
                        gemm(pos, ("up", e + 1), "T", a_hi, a_lo, f=f)
                        down(e, f)
                gemm(pos, ("up", 7), "T", a_hi, a_lo)
                down(6)
                down(7)

            with pe.Fori(0, NB - 1) as b:
                block_products(("block", b), False)
            block_products(last_block, True)

            def gemm_s(i, name, src, b, first=True, last=True):
                pe.wait_ge(ws_in[i % WS], 16 * (i // WS + 1))
                for k in range(KD):
                    m = nc.tensor.matmul(bank(b)[SQ, :], src[:, k, :], w_smp[i % WS][:, k, :],
                                         start=(first and k == 0), stop=(last and k == KD - 1))
                m.then_inc(pe_s.did(name), 1)

            pe.wait_ge(*step("xt1"))
            gemm_s(0, "zf", xt, 5)
            gemm_s(1, "zq", xt, 6)
            pe.wait_ge(*step("zf_rows"))
            pe.wait_ge(*step("zq_rows"))
            to_columns("zt", 7, tiles_of(zfq[:, 0, :], H) + tiles_of(zfq[:, 1, :], H))
            pe.wait_ge(*out(last_block, ("dn", 7, 1)))
            gemm_s(2, "zi", xt, 3)
            gemm_s(3, "zg", xt, 4)
            gemm_s(4, "zv", xt, 5)
            pe.wait_ge(*step("scaled"))
            for h in range(H):
                for l in range(SLV):
                    lhs, rhs = (kk_s[:, h, :], qq_s[:, h, :]) if l == 0 else [dec_s[:, l - 1, h, :]] * 2
                    c = (h * SLV + l) * NS
                    m = nc.tensor.matmul(bank(1)[SQ, c:c + NS], lhs, rhs, start=True, stop=True)
            m.then_inc(pe_s.did("lv"), 1)
            for h in range(H):
                m = nc.tensor.transpose(bank(2)[SQ, h * P:h * P + P], dec_s[:, SLV, h, :], ident[:])
            m.then_inc(pe_s.did("kt"), 1)
            pe.wait_ge(s0_in, 16)
            pe.wait_ge(*step("v_rows"))
            pe.wait_ge(*step("att"))
            for h in range(H):
                o = bank(3)[SQ, h * P:h * P + P]
                nc.tensor.matmul(o, att_s[:, h, :], v_s[:, h * P:h * P + P], start=True, stop=False)
                for r in range(DB):
                    m = nc.tensor.matmul(o, of_request(qe_m, h, r), s0[:, r, h, :], start=False, stop=(r == DB - 1))
            m.then_inc(pe_s.did("o"), 1)
            gemm_s(5, "zu", xt, 6)
            pe.wait_ge(*step("vn"))
            for g in range(H):
                m = nc.tensor.matmul(bank(7)[SQ, g * P:g * P + P], ws_s[:, g].rearrange("p b t -> p (b t)"),
                                     vn_s[:, g * P:g * P + P], start=True, stop=True)
            m.then_inc(pe_s.did("mix"), 1)
            pe.wait_ge(*step("mixed"))
            to_columns("ot", 0, tiles_of(o_s, H) + tiles_of(u_s, H))

            def new_tokens(j):
                h, r0 = divmod(j, 2)
                col = slice(h * P, h * P + P)
                if j >= 4:
                    pe.wait_ge(*step(f"new{j - 4}"))
                m = nc.tensor.matmul(bank(4 + j % 4), kd_s[:, col], vm[:, 4 * r0:4 * r0 + 4, col], start=True, stop=True)
                m.then_inc(pe_s.did(f"st{j}"), 1)

            pe.wait_ge(*step("gate"))
            pe.wait_ge(*step("zu_gelu"))
            pe.wait_ge(*step("mixed_cm"))
            pe.wait_ge(*step("kd_rows"))
            pe.wait_ge(*step("vm"))
            for j in range(4):
                new_tokens(j)
            pe.wait_ge(*step("xt_ot"))
            gemm_s(6, "wo0", xt, 1)
            for j in range(4, 8):
                new_tokens(j)
            gemm_s(7, "wo1", xt, 2)
            pe.wait_ge(*step("xn2"))
            to_columns("n2", 0, tiles_of(xns))
            pe.wait_ge(*step("xt2"))
            gemm_s(8, "cq0", xt, 1)
            gemm_s(9, "cq1", xt, 2)
            pe.wait_ge(*step("q_rows0"))
            pe.wait_ge(*step("q_rows1"))
            to_columns("qt", 3, tiles_of(q_s))
            pe.wait_ge(*step("qm"))
            for r in range(DB + 1):
                if r < DB:
                    pe.wait_ge(kv_in[r % KV], 16 * (r // KV + 1))
                    for part in range(2):
                        if r:
                            pe.wait_ge(*step(f"kts{r - 1}_{part}"))
                        for i in range(4):
                            for t in range(MT):
                                d0 = (4 * part + i) * P
                                m = nc.tensor.transpose(bank(4 + 2 * part + i // 2)[:, (i % 2) * NM + t * P:][:, 0:P],
                                                        kv[r % KV][:, t, d0:d0 + P], ident[:])
                        m.then_inc(pe_s.did(f"kt{r}_{part}"), 1)
                if r:
                    pe.wait_ge(*step(f"kts{r - 1}_0"))
                    pe.wait_ge(*step(f"kts{r - 1}_1"))
                    for k in range(KD):
                        m = nc.tensor.matmul(bank(k // 2)[SQ, 0:NM], of_request(qm, k, r - 1),
                                             kts[(r - 1) % 2][:, k, :], start=(r == 1 and k % 2 == 0),
                                             stop=(r == DB and k % 2 == 1))
                    m.then_inc(pe_s.did(f"sc{r - 1}"), 1)
            pe.wait_ge(*step("p_rows"))
            to_columns("pt", 4, tiles_of(q_s))
            pe.wait_ge(*step("pm"))
            for r in range(DB):
                i = DB + r
                pe.wait_ge(kv_in[i % KV], 16 * (i // KV + 1))
                for h in range(H):
                    for t in range(MT):
                        m = nc.tensor.matmul(bank(h)[SQ, 0:XD], of_request(pm, h * MT + t, r),
                                             kv[i % KV][:, t, h * XD:h * XD + XD],
                                             start=(r == 0 and t == 0), stop=(r == DB - 1 and t == MT - 1))
                m.then_inc(pe_s.did(f"ca{r}"), 1)
            pe.wait_ge(*step("ca_rows"))
            to_columns("cat", 4, tiles_of(xns))
            pe.wait_ge(*step("xt_ca"))
            gemm_s(10, "co0", xt, 5)
            gemm_s(11, "co1", xt, 6)
            pe.wait_ge(*step("xn3"))
            to_columns("n3", 0, tiles_of(xns))
            pe.wait_ge(*step("xt3"))
            for e in range(9):
                if e < 8:
                    if e >= 2:
                        pe.wait_ge(*step(f"sq{e - 2}"))
                    gemm_s(12 + e, f"up{e}", xt, 1 + e % 2)
                if e:
                    pe.wait_ge(*step(f"sq{e - 1}"))
                    if e >= 3:
                        pe.wait_ge(*step(f"hts{e - 3}"))
                    to_columns(f"ht{e - 1}", 3 + (e - 1) % 2, tiles_of(relu_s[(e - 1) % 2], 4))
            for r in range(4):
                pe.wait_ge(*step(f"hts{2 * r + 1}"))
                for c in range(2):
                    gemm_s(20 + 2 * r + c, f"dn{r}_{c}", hts[:, r * KD:r * KD + KD], 5 + c, r == 0, r == 3)

        @block.scalar
        def _(act):
            link = Links(act_sem, mem=3, block=UNITS + 8, last=UNITS + 7, sample=6)
            tables = nc.scalar.preload_act_table_set

            def rsqrt(pos, tag, n):
                tables("natural_log_exp_and_others")
                act.wait_ge(var_ready.sem, var_ready.at(pos, tag))
                c = slice(stat(tag), stat(tag) + n)
                nc.scalar.activation(lnv[:, c], var[:, c], ACT.Ln).then_inc(act_sem, 1)
                act.wait_ge(act_sem, link.next())
                nc.scalar.activation(y0[:, c], lnv[:, c], ACT.Exp, scale=-0.5).then_inc(rstd0_ready.sem, 1)

            def squares(tag, tiles, junk):
                for i, t in enumerate(tiles):
                    ins = nc.scalar.activation(junk[i], t, ACT.Square, accum_out=ss[:, stat(tag) + i:stat(tag) + i + 1])
                ins.then_inc(ssq_ready.sem, 1)

            def round_hi(pos, job, dst, src, scale=1.0):
                act.wait_ge(*done(pos, job))
                nc.scalar.activation(dst, src, ACT.Copy, scale=scale).then_inc(hi_ready.sem, 1)

            def n1_squares(pos, p):
                t = 2 * p
                tables("natural_log_exp_and_others")
                act.wait_ge(nx_in[0].sem, nx_in[0].at(pos, p))
                squares("n1" + "ab"[p], [nx[0][:]], [xn[:, t, :]])
                rsqrt(pos, "n1" + "ab"[p], 2)

            def n1_hi(pos, p):
                round_hi(pos, ("n1", p), *pair(pos, p, a_hi))


            pos = ("mem", 0)
            link.start(pos)
            tables("natural_log_exp_and_others")
            act.wait_ge(mem_in, 48)
            squares("nm", [x[:, 0, :]], [xn[:, 0, :]])
            rsqrt(pos, "nm", MT)
            for t in range(MT):
                round_hi(pos, ("nm", t), a_hi[:, :, t * P:t * P + P], feature_tiles(out_of(pos, ("nm", t))))
            n1_squares(pos, 0)
            for c in range(2):
                act.wait_ge(*done(pos, ("ck", c)))
                nc.scalar.copy(kn[c][:], out_of(pos, ("ck", c))[:, 0:MT, :]).then_inc(evacuated_of(pos, ("ck", c)), 1)
                act.wait_ge(*out(pos, ("ck", c)))
                act.dma_start(O[4][0, 0].rearrange("(t p) h d -> p t (h d)", p=P)[:, :, c * 512:c * 512 + 512],
                              kn[c][:]).then_inc(kn_out, 16)
                round_hi(pos, ("ckt", c), kt_hi[:, 4 * c:4 * c + 4, :], feature_tiles(out_of(pos, ("ckt", c)), NM))
                if c == 0:
                    act.wait_ge(lb_args, 1)
                    nc.scalar.activation(lbp[:], lbp[:], ACT.Exp).then_inc(lb_exps, 1)
                    n1_squares(pos, 1)
            for c in range(2):
                ps = out_of(pos, ("cv", c))[:, 0:MT, :]
                act.wait_ge(*done(pos, ("cv", c)))
                nc.scalar.copy(kn[2 + c][:], ps)
                round_hi(pos, ("cv", c), v_hi[:, :, c * 512:c * 512 + 512], ps)
                act.wait_ge(hi_ready.sem, hi_ready.at(pos, ("cv", c)))
                act.dma_start(O[5][0, 0].rearrange("(t p) h d -> p t (h d)", p=P)[:, :, c * 512:c * 512 + 512],
                              kn[2 + c][:]).then_inc(kn_out, 16)
                n1_hi(pos, 1 - c)
            act.wait_ge(kn_out, 64)
            link.end()

            def rsqrt_s(tag, n):
                tables("natural_log_exp_and_others")
                act.wait_ge(*step("var_" + tag))
                nc.scalar.activation(lnv[SQ, 0:n], var[SQ, 0:n], ACT.Ln).then_inc(act_sem, 1)
                act.wait_ge(act_sem, link.next())
                nc.scalar.activation(y0[SQ, 0:n], lnv[SQ, 0:n], ACT.Exp, scale=-0.5
                           ).then_inc(act_s.did("rstd_" + tag), 1)

            def block_scalar(pos, b, last):
                link.start(pos)

                def decays(u):
                    tables("natural_log_exp_and_others")
                    act.wait_ge(args_ready.sem, args_ready.at(pos, u))
                    nc.scalar.activation(ends[u % 3][:], ends[u % 3][:], ACT.Abs)
                    nc.scalar.activation(lvl[u % 2][:], lvl[u % 2][:], ACT.Abs).then_inc(act_sem, 1)
                    act.wait_ge(act_sem, link.next())
                    nc.scalar.activation(ends[u % 3][:], ends[u % 3][:], ACT.Exp, scale=-1.0)
                    nc.scalar.activation(lvl[u % 2][:], lvl[u % 2][:], ACT.Exp, scale=-1.0
                                         ).then_inc(decays_ready.sem, 1)

                def rows_of(ps, b):
                    return ps[:, b // 2, (b % 2) * 2 * P:(b % 2) * 2 * P + 2 * P].rearrange("p (j c) -> p j c", c=P)

                def unit_out(u):
                    c, p = divmod(u, 2)
                    if u >= 2:
                        act.wait_ge(added_used.sem, added_used.at(pos, u - 2))
                    act.wait_ge(*done(pos, ("out", u)))
                    ps = out_of(pos, ("out", u))
                    if u + 1 < UNITS:
                        nc.scalar.copy(kdt[:], rows_of(ps, 3))
                    nc.scalar.copy(added[u % 2][:], rows_of(ps, 2))
                    nc.scalar.copy(vv[:, c, 2 * p * P:2 * p * P + 2 * P], ps[:, 0, 0:2 * P]
                                   ).then_inc(evacuated_of(pos, ("out", u)), 1)
                    act.wait_ge(*out(pos, ("out", u)))
                    for j in range(2):
                        i = 2 * p + j
                        ins = nc.scalar.activation(osq[:, j, :], vv[:, c, i * P:i * P + P], ACT.Square,
                                                   accum_out=ss[:, 4 * c + i:4 * c + i + 1])
                    ins.then_inc(o_ready.sem, 1)

                tables("sigmoid_and_others")
                act.wait_ge(*done(pos, "zf"))
                nc.scalar.activation(kk[:], out_of(pos, "zf")[:], ACT.Sigmoid, scale=-1.0)
                nc.scalar.activation(bb[:], out_of(pos, "zf")[:], ACT.Sigmoid).then_inc(evacuated_of(pos, "zf"), 1)
                tables("natural_log_exp_and_others")
                act.wait_ge(*out(pos, "zf"))
                for h in range(H):
                    ins = nc.scalar.activation(bb[:, h, :], bb[:, h, :], ACT.Ln, scale=oml[:, h:h + 1],
                                               bias=lb[:, h:h + 1])
                ins.then_inc(logf_ready.sem, 1)
                decays(0)
                decays(1)
                act.wait_ge(*done(pos, "zi"))
                nc.scalar.copy(vv[:], out_of(pos, "zi")[:]).then_inc(evacuated_of(pos, "zi"), 1)
                tables("sigmoid_and_others")
                act.wait_ge(*done(pos, "zq"))
                nc.scalar.activation(qq[:], out_of(pos, "zq")[:], ACT.Sigmoid).then_inc(sig_ready.sem, 1)
                act.wait_ge(*done(pos, "kt"))
                nc.scalar.copy(kdt[:], rows_of(out_of(pos, "kt"), 3)).then_inc(evacuated_of(pos, "kt"), 1)
                for u in range(UNITS):
                    if u + 2 < UNITS:
                        decays(u + 2)
                    for at, name, dst in ((0, "zv", vn), (3, "zg", gate), (6, "zu", uu)):
                        if u == at:
                            tables("sigmoid_and_others" if name == "zg" else "gelu_apprx_tanh_and_others")
                            act.wait_ge(*done(pos, name))
                            nc.scalar.activation(dst[:], out_of(pos, name)[:], ACT.Sigmoid if name == "zg" else
                                                 ACT.Gelu_apprx_tanh).then_inc(evacuated_of(pos, name), 1)
                    if u == UNITS - 1:
                        round_hi(pos, "otu", a_hi[:, 4:8, :], out_of(pos, "otu")[:])
                    unit_out(u)
                    if u == 1:
                        rsqrt(pos, "ln", TT)
                    if u == 5:
                        rsqrt(pos, "oa", 12)
                rsqrt(pos, "ob", 4)
                round_hi(pos, "oto", a_hi[:, 0:4, :], out_of(pos, "oto")[:])

                def norm_halves(tag, name):
                    for c in range(2):
                        round_hi(pos, (tag, c), a_hi[:, 4 * c:4 * c + 4, :], out_of(pos, (tag, c))[:])
                    tables("natural_log_exp_and_others")
                    act.wait_ge(*out(pos, (name, 1)))
                    squares(tag, [x[:, t, :] for t in range(2)],
                            [relu[:, 2 * t:2 * t + 2, :].rearrange("p a c -> p (a c)") for t in range(2)])
                    rsqrt(pos, tag, TT)

                norm_halves("n2", "wo")
                for c in range(2):
                    round_hi(pos, ("cq", c), b_hi[:, 4 * c:4 * c + 4, :], out_of(pos, ("cq", c))[:], ATT_SCALE)
                tables("natural_log_exp_and_others")

                def exps(g, t):
                    act.wait_ge(max_ready.sem, max_ready.at(pos, g * TT + t))
                    ps = out_of(pos, ("sc", g))
                    for j in range(2):
                        h = 2 * g + j
                        ins = nc.scalar.activation(pp[:, t, h * NM:h * NM + NM], ps[:, t, j * NM:j * NM + NM], ACT.Exp,
                                                   scale=rstd[:, stat("n2") + t:stat("n2") + t + 1],
                                                   bias=mx[:, t, h:h + 1], accum_out=psums[:, t, h:h + 1])
                    ins.then_inc(evacuated_of(pos, ("sc", g)) if t == TT - 1 else exp_ready.sem, 1)

                def attended_hi(name, h):
                    b0 = 2 * (h % 2)
                    round_hi(pos, (name, h), pt_hi[h % 2][:] if name == "pt" else a_hi[:, 2 * h:2 * h + 2, :],
                             out_of(pos, (name, h))[:, b0:b0 + 2, :])

                for t in range(TT):
                    exps(0, t)
                for g in range(2):
                    exps(1, 2 * g)
                    exps(1, 2 * g + 1)
                    attended_hi(*ATTENDED[g])
                for job in ATTENDED[2:]:
                    attended_hi(*job)
                norm_halves("n3", "co")

                def relu_square(e, f=0):
                    act.wait_ge(*done(pos, ("up", e), f))
                    if e:
                        act.wait_ge(*out(pos, ("up", e - 1), f))
                    nc.scalar.activation(relu[:], out_of(pos, ("up", e))[:], ACT.Relu).then_inc(relu_ready.sem, 1)
                    act.wait_ge(sq_ready.sem, sq_ready.at(pos, e + f * 2))
                    nc.scalar.copy(ht_hi[e % 2][:], relu[:]).then_inc(ht_hi_ready.sem, 1)

                relu_square(0)
                with act.Fori(0, 3) as f:
                    relu_square(1, f)
                    relu_square(2, f)
                relu_square(7)
                for p in range(2) if not last else ():
                    n1_squares(pos, p)
                    n1_hi(pos, p)
                if last:
                    rsqrt_s("n1", 1)
                tables("natural_log_exp_and_others")
                act.wait_ge(*out(pos, ("dn", 7, 1)))
                squares("y", [x[:, t, :] for t in range(2)], [xn[:, t, :] for t in range(2)])
                rsqrt(pos, "y", TT)
                for t in range(TT):
                    act.wait_ge(xn_ready.sem, xn_ready.at(pos, ("y", t)))
                    act.dma_start(O[0][0, bass.ds(b * BT + t * P, P), :], xn[:, t, :]).then_inc(y_out.sem, 16)
                link.end()

            with act.Fori(0, NB - 1) as b:
                block_scalar(("block", b), b, False)
            block_scalar(last_block, NB - 1, True)

            link.start(("sample", 0))

            for i, n in enumerate(("zf", "zq")):
                act.wait_ge(*step(n))
                nc.scalar.copy(zfq[:, i, :], bank(5 + i)[SQ, :]).then_inc(act_s.did(n + "_rows"), 1)
            tables("sigmoid_and_others")
            act.wait_ge(y_out.sem, y_out.at(last_block, TT - 1))
            act.wait_ge(*step("zt"))
            zt = bank(7)[:, 0:2 * H * NS].rearrange("p (a h s) -> p a h s", a=2, h=H)
            nc.scalar.activation(kk_s[:], zt[:, 0], ACT.Sigmoid, scale=-1.0)
            nc.scalar.activation(bb_s[:], zt[:, 0], ACT.Sigmoid)
            nc.scalar.activation(qq_s[:], zt[:, 1], ACT.Sigmoid).then_inc(act_s.did("sig"), 1)
            act.wait_ge(*step("zi"))
            nc.scalar.copy(v_s[:], bank(3)[SQ, :]).then_inc(act_s.did("v_rows"), 1)
            act.wait_ge(*step("zg"))
            nc.scalar.activation(gate_s[:], bank(4)[SQ, :], ACT.Sigmoid).then_inc(act_s.did("gate"), 1)
            tables("natural_log_exp_and_others")
            act.wait_ge(*step("sig"))
            for h in range(H):
                ins = nc.scalar.activation(bb_s[:, h, :], bb_s[:, h, :], ACT.Ln, scale=oml[:, h:h + 1], bias=lb[:, h:h + 1])
            ins.then_inc(act_s.did("logf"), 1)
            act.wait_ge(*step("args"))
            nc.scalar.activation(dec_s[:], dec_s[:], ACT.Abs).then_inc(act_sem, 1)
            act.wait_ge(act_sem, link.next())
            nc.scalar.activation(dec_s[:], dec_s[:], ACT.Exp, scale=-1.0).then_inc(act_s.did("decays"), 1)
            tables("gelu_apprx_tanh_and_others")
            act.wait_ge(*step("zv"))
            nc.scalar.activation(vn_s[:], bank(5)[SQ, :], ACT.Gelu_apprx_tanh).then_inc(act_s.did("zv_gelu"), 1)
            act.wait_ge(*step("kt"))
            nc.scalar.copy(kd_s[:], bank(2)[SQ, :]).then_inc(act_s.did("kd_rows"), 1)
            rsqrt_s("ln", 1)
            act.wait_ge(*step("o"))
            nc.scalar.copy(o_s[:], bank(3)[SQ, :]).then_inc(act_s.did("o_rows"), 1)
            act.wait_ge(*step("vn"))
            act.dma_start(O[6][0].rearrange("b t c -> (b t) c"), vn_s[:]).then_inc(vn_out, 16)
            rsqrt_s("o", H)
            tables("gelu_apprx_tanh_and_others")
            act.wait_ge(*step("zu"))
            nc.scalar.activation(u_s[:], bank(6)[SQ, :], ACT.Gelu_apprx_tanh).then_inc(act_s.did("zu_gelu"), 1)
            rsqrt_s("n2", 1)
            for c in range(2):
                act.wait_ge(*step(f"cq{c}"))
                nc.scalar.activation(q_s[:, c * 512:c * 512 + 512], bank(1 + c)[SQ, :],
                                                            ACT.Copy, scale=ATT_SCALE
                                                                       ).then_inc(act_s.did(f"q_rows{c}"), 1)
            act.wait_ge(*step("new7"))
            act.dma_start(O[3][0].rearrange("b h k v -> k b h v"), s0[:]).then_inc(s_out_done, 16)

            for r in range(DB):
                keys_part(act, r, 0, nc.scalar.copy).then_inc(act_s.did(f"kts{r}_0"), 1)
            tables("natural_log_exp_and_others")
            act.wait_ge(*step("max"))
            for h in range(H):
                ins = nc.scalar.activation(q_s[:, h * NM:h * NM + NM], bank(h)[SQ, 0:NM], ACT.Exp,
                                           bias=mx_s[:, h:h + 1], accum_out=sum_s[:, h:h + 1])
            ins.then_inc(act_s.did("p_exp"), 1)
            act.wait_ge(*step(f"ca{DB - 1}"))
            nc.scalar.copy(xns[:].rearrange("p (h d) -> p h d", h=H), half[0][SQ, :, 0:XD]
                       ).then_inc(act_s.did("ca_rows"), 1)
            rsqrt_s("n3", 1)
            for e in range(8):
                act.wait_ge(*step(f"up{e}"))
                if e >= 2:
                    act.wait_ge(*step(f"ht{e - 2}"))
                nc.scalar.activation(relu_s[e % 2][:], bank(1 + e % 2)[SQ, :], ACT.Relu
                           ).then_inc(act_s.did(f"relu{e}"), 1)
            rsqrt_s("y", 1)
            act.wait_ge(*step("y"))
            act.dma_start(O[1].rearrange("b t d -> (b t) d"), xns[:]).then_inc(s_out_done, 16)
            act.wait_ge(vn_out, 16)
            act.wait_ge(s_out_done, 32)
            link.end()

        @block.vector
        def _(dve):
            link = Links(dve_sem, mem=13, block=83, last=79, sample=31)

            def mean_square(pos, tag, n, inv):
                c = slice(stat(tag), stat(tag) + n)
                nc.vector.tensor_scalar(var[:, c], ss[:, c], inv, EPS, ALU.mult, ALU.add).then_inc(var_ready.sem, 1)

            def newton(pos, tag, n, inv):
                mean_square(pos, tag, n, inv)
                refine(pos, tag, n)

            def refine(pos, tag, n):
                c = slice(stat(tag), stat(tag) + n)
                dve.wait_ge(rstd0_ready.sem, rstd0_ready.at(pos, tag))
                nc.vector.scalar_tensor_tensor(yt[:, c], y0[:, c], -0.5, y0[:, c], ALU.mult, ALU.mult
                                               ).then_inc(dve_sem, 1)
                dve.wait_ge(dve_sem, link.next())
                nc.vector.tensor_tensor(yt[:, c], yt[:, c], var[:, c], ALU.mult).then_inc(dve_sem, 1)
                dve.wait_ge(dve_sem, link.next())
                nc.vector.scalar_tensor_tensor(rstd[:, c], yt[:, c], 1.5, y0[:, c], ALU.add, ALU.mult
                                               ).then_inc(dve_sem, 1)
                dve.wait_ge(dve_sem, link.next())

            def rest_lo(pos, job, dst, hi, src, scale=None):
                dve.wait_ge(hi_ready.sem, hi_ready.at(pos, job))
                if scale is None:
                    ins = nc.vector.tensor_tensor(dst, src, hi.bitcast(F32), ALU.subtract)
                else:
                    ins = nc.vector.scalar_tensor_tensor(dst, src, scale, hi.bitcast(F32), ALU.mult, ALU.subtract)
                ins.then_inc(evacuated_of(pos, job), 1)

            def mean_squares(pos, tag, n, tiles, junk):
                for i, t in enumerate(tiles):
                    c = stat(tag) + n - len(tiles) + i
                    ins = nc.vector.tensor_tensor_reduce(out=junk[i], in0=t, in1=t, scale=1.0, scalar=0.0,
                                                         op0=ALU.mult, op1=ALU.add, accum_out=ss[:, c:c + 1])
                ins.then_inc(dve_sem, 1)
                dve.wait_ge(dve_sem, link.next())
                dve.wait_ge(ssq_ready.sem, ssq_ready.at(pos, tag))
                newton(pos, tag, n, 1.0 / D)

            def scaled_row(tag, i, dst, src):
                c = stat(tag) + i
                nc.vector.scalar_tensor_tensor(dst, src, rstd[:, c:c + 1], gain[:], ALU.mult, ALU.mult
                                               ).then_inc(xn_ready.sem, 1)

            def n1_rows_scaled(pos, p):
                t = 2 * p
                if p == 0:
                    dve.wait_ge(gain_in.sem, gain_in.at(pos, "n1"))
                dve.wait_ge(nx_in[1].sem, nx_in[1].at(pos, p))
                mean_squares(pos, "n1" + "ab"[p], 2, [nx[1][:]], [xn[:, t + 1, :]])
                for i in range(2):
                    scaled_row("n1" + "ab"[p], i, xn[:, t + i, :], nx[i][:])

            def n1_lo(pos, p):
                dst, src = pair(pos, p, a_lo)
                rest_lo(pos, ("n1", p), dst, pair(pos, p, a_hi)[0], src)

            pos = ("mem", 0)
            link.start(pos)
            dve.wait_ge(mem_in, 48)
            mean_squares(pos, "nm", MT, [x[:, 1, :]], [xn[:, 1, :]])
            for t in range(MT):
                scaled_row("nm", t, xn[:, t, :], x[:, t, :])
            for t in range(MT):
                rest_lo(pos, ("nm", t), a_lo[:, :, t * P:t * P + P], a_hi[:, :, t * P:t * P + P],
                        feature_tiles(out_of(pos, ("nm", t))))
            n1_rows_scaled(pos, 0)
            for c in range(2):
                s = slice(4 * c, 4 * c + 4)
                rest_lo(pos, ("ckt", c), kt_lo[:, s, :], kt_hi[:, s, :], feature_tiles(out_of(pos, ("ckt", c)), NM))
                if c == 0:
                    dve.wait_ge(consts_in, 16 * n_consts)
                    nc.vector.memset(state[:], 0.0)
                    nc.vector.tensor_tensor(lbm[:], lbp[:, 0, :], lbp[:, 1, :], ALU.max).then_inc(dve_sem, 1)
                    dve.wait_ge(dve_sem, link.next())
                    for r in range(2):
                        ins = nc.vector.tensor_tensor(lbp[:, r, :], lbp[:, r, :], lbm[:], ALU.subtract)
                    ins.then_inc(lb_args, 1)
                    dve.wait_ge(lb_exps, 1)
                    nc.vector.tensor_tensor(lbm[:], lbp[:, 0, :], lbp[:, 1, :], ALU.add).then_inc(lb_exps, 1)
                    dve.wait_ge(lb_exps, 2)
                    nc.vector.reciprocal(lbm[:], lbm[:]).then_inc(lb_exps, 1)
                    dve.wait_ge(lb_exps, 3)
                    nc.vector.tensor_tensor(lb[:], lbp[:, 0, :], lbm[:], ALU.mult).then_inc(lb_exps, 1)
                    dve.wait_ge(lb_exps, 4)
                    nc.vector.tensor_scalar(oml[:], lb[:], -1.0, 1.0, ALU.mult, ALU.add).then_inc(lb_exps, 1)
                    dve.wait_ge(ws_transposed, 1)
                    nc.vector.tensor_tensor(ws_t[:], half[1][:, 3, :].rearrange("p (g c) -> p g c", c=P),
                                            masks[:, 7:8, :].to_broadcast([P, H, P]), ALU.mult
                                                       ).then_inc(setup_ready, 1)
                    n1_rows_scaled(pos, 1)
            for c in range(2):
                s = slice(c * 512, c * 512 + 512)
                rest_lo(pos, ("cv", c), v_lo[:, :, s], v_hi[:, :, s], out_of(pos, ("cv", c))[:, 0:MT, :])
                n1_lo(pos, 1 - c)
            link.end()

            def newton_s(tag, n, inv):
                if inv:
                    nc.vector.tensor_scalar(var[SQ, 0:n], ss[SQ, 0:n], inv, EPS, ALU.mult, ALU.add
                               ).then_inc(dve_s.did("var_" + tag), 1)
                dve.wait_ge(*step("rstd_" + tag))
                nc.vector.scalar_tensor_tensor(yt[SQ, 0:n], y0[SQ, 0:n], -0.5, y0[SQ, 0:n], ALU.mult, ALU.mult
                           ).then_inc(dve_sem, 1)
                dve.wait_ge(dve_sem, link.next())
                nc.vector.tensor_tensor(yt[SQ, 0:n], yt[SQ, 0:n], var[SQ, 0:n], ALU.mult).then_inc(dve_sem, 1)
                dve.wait_ge(dve_sem, link.next())
                nc.vector.scalar_tensor_tensor(rstd[SQ, 0:n], yt[SQ, 0:n], 1.5, y0[SQ, 0:n], ALU.add, ALU.mult
                           ).then_inc(dve_sem, 1)
                dve.wait_ge(dve_sem, link.next())

            def norm_s(tag, name, g):
                nc.vector.tensor_tensor_reduce(out=xns[:], in0=xs[:], in1=xs[:], scale=1.0, scalar=0.0,
                                                    op0=ALU.mult, op1=ALU.add, accum_out=ss[SQ, 0:1]
                                                               ).then_inc(dve_sem, 1)
                dve.wait_ge(dve_sem, link.next())
                newton_s(tag, 1, 1.0 / D)
                nc.vector.scalar_tensor_tensor(xns[:], xs[:], rstd[SQ, 0:1], g, ALU.mult, ALU.mult
                           ).then_inc(dve_s.did(name), 1)

            def columns(job, name, b, n=KD, dst=xt):
                dve.wait_ge(*step(job))
                nc.vector.tensor_copy(dst[:, 0:n, :], bank(b)[:, 0:n * NS].rearrange(
                    "p (k s) -> p k s", s=NS)).then_inc(dve_s.did(name), 1)

            def block_vector(pos, last):
                link.start(pos)

                def blocks(t, u, w):
                    c, p = divmod(u, 2)
                    return t[:, 2 * p:2 * p + 2, c * P:c * P + P].rearrange("p j (n w) -> p j n w", w=w)

                def args(u):
                    for l in range(1, LEVELS):
                        w = 1 << l
                        src = blocks(bb, u, w)
                        mid = src[:, :, :, w // 2 - 1:w // 2].to_broadcast([P, 2, P // w, w])
                        nc.vector.tensor_tensor(lvl[u % 2][:, l - 1].rearrange("p j (n w) -> p j n w", w=w), src, mid,
                                                ALU.subtract)
                    c, p = divmod(u, 2)
                    src = bb[:, 2 * p:2 * p + 2, c * P:c * P + P]
                    nc.vector.tensor_copy(ends[u % 3][:, 0], src)
                    nc.vector.tensor_tensor(ends[u % 3][:, 1], src[:, :, P - 1:P].to_broadcast([P, 2, P]), src,
                                            ALU.subtract).then_inc(args_ready.sem, 1)

                def scaled(u):
                    dve.wait_ge(decays_ready.sem, decays_ready.at(pos, u))
                    c, p = divmod(u, 2)
                    nc.vector.tensor_copy(e_last[u % 3][:], ends[u % 3][:, 0, :, P - 1]).then_inc(dve_sem, 1)
                    tok = slice(c * P, c * P + P)
                    for l in range(1, LEVELS):
                        w = 1 << l
                        v = lvl[u % 2][:, l - 1].rearrange("p j (n w) -> p j n w", w=w)
                        for part, src in ((slice(0, w // 2), kk), (slice(w // 2, w), qq)):
                            nc.vector.tensor_tensor(v[:, :, :, part], v[:, :, :, part],
                                                    blocks(src, u, w)[:, :, :, part], ALU.mult)
                    dve.wait_ge(dve_sem, link.next())
                    for slot, src in ((0, qq), (1, kk)):
                        ins = nc.vector.tensor_tensor(ends[u % 3][:, slot], ends[u % 3][:, slot],
                                                      src[:, 2 * p:2 * p + 2, tok], ALU.mult)
                    ins.then_inc(scaled_ready.sem, 1)

                def attention(u):
                    v = out_of(pos, ("lv", u)).rearrange("p b (e j c) -> p b e j c", e=2, j=2)
                    if u + 2 >= UNITS:
                        nc.vector.tensor_copy(yt[:, 36:37], ident[:, 0:1])
                    nc.vector.copy_predicated(v[:, :, 0], own_size(0, 4), v[:, :, 1]).then_inc(dve_sem, 1)
                    dve.wait_ge(dve_sem, link.next())
                    nc.vector.tensor_copy(yt[:, 36:37], ident[:, 0:1])
                    nc.vector.copy_predicated(v[:, 0:4:2, 0], own_size(4, 6), v[:, 1:4:2, 0]).then_inc(dve_sem, 1)
                    dve.wait_ge(dve_sem, link.next())
                    nc.vector.tensor_copy(yt[:, 36:37], ident[:, 0:1])
                    nc.vector.copy_predicated(v[:, 0:1, 0], own_size(6, 7), v[:, 2:3, 0]).then_inc(dve_sem, 1)
                    dve.wait_ge(dve_sem, link.next())
                    nc.vector.tensor_tensor(att[:], v[:, 0, 0], masks[:, 7:8, :].to_broadcast([P, 2, P]), ALU.mult
                                            ).then_inc(evacuated_of(pos, ("lv", u)), 1)

                def own_size(i0, i1):
                    return masks[:, i0:i1, None, :].bitcast(mybir.dt.int32).to_broadcast([P, i1 - i0, 2, P])

                def new_state(u):
                    p = u % 2
                    dve.wait_ge(*out(pos, ("out", u)))
                    for j in range(2):
                        h = 2 * p + j
                        ins = nc.vector.scalar_tensor_tensor(state[:, h, :], state[:, h, :], e_last[u % 3][:, j:j + 1],
                                                             added[u % 2][:, j, :], ALU.mult, ALU.add)
                    ins.then_inc(added_used.sem, 1)

                def mixed(t):
                    for h in range(H):
                        c = slice(h * P, h * P + P)
                        ins = nc.vector.scalar_tensor_tensor(vv[:, t, c], vv[:, t, c],
                                                             rstd[:, 4 * t + h:4 * t + h + 1], gate[:, t, c],
                                                             ALU.mult, ALU.mult)
                    ins.then_inc(mixed_ready.sem, 1)

                dve.wait_ge(*out(pos, "zf"))
                for h in range(H):
                    nc.vector.tensor_scalar(kk[:, h, :], kk[:, h, :], oml[:, h:h + 1], None, ALU.mult)
                dve.wait_ge(logf_ready.sem, logf_ready.at(pos, 0))
                for h in range(H):
                    for c in range(TT):
                        s = bb[:, h, c * P:c * P + P]
                        ins = nc.vector.tensor_tensor_scan(s, ones[:], s, 0.0, ALU.mult, ALU.add)
                ins.then_inc(dve_sem, 1)
                dve.wait_ge(dve_sem, link.next())
                dve.wait_ge(y_out.sem, y_out.at(pos, -1))
                args(0)
                args(1)
                dve.wait_ge(sig_ready.sem, sig_ready.at(pos, 0))
                nc.vector.tensor_tensor(qq[:], qq[:], out_of(pos, "zq")[:], ALU.mult
                                        ).then_inc(evacuated_of(pos, "zq"), 1)
                dve.wait_ge(*out(pos, "zq"))
                scaled(0)
                scaled(1)
                for u in range(UNITS):
                    dve.wait_ge(*done(pos, ("lv", u)))
                    if u + 2 < UNITS:
                        args(u + 2)
                    attention(u)
                    if u == 1:
                        dve.wait_ge(*out(pos, "zv"))
                        for t in range(TT):
                            ins = nc.vector.bn_stats(stats[:, t, :], vn[:, t, :])
                        ins.then_inc(dve_sem, 1)
                        dve.wait_ge(dve_sem, link.next())
                        nc.vector.tensor_copy(yt[:, 36:37], stats[:, TT - 1, 0:1])
                        for t in range(TT):
                            ins = nc.vector.bn_aggr(mv[:, t, :], stats[:, t, :])
                        ins.then_inc(dve_sem, 1)
                        dve.wait_ge(dve_sem, link.next())
                        nc.vector.tensor_scalar(var[:, 16:16 + TT], mv[:, :, 1], EPS, None, ALU.add
                                                ).then_inc(var_ready.sem, 1)
                    if u == 2:
                        refine(pos, "ln", TT)
                        for t in range(TT):
                            ins = nc.vector.tensor_scalar(vn[:, t, :], vn[:, t, :], mv[:, t, 0:1],
                                                          rstd[:, 16 + t:17 + t], ALU.subtract, ALU.mult)
                        ins.then_inc(dve_sem, 1)
                        dve.wait_ge(dve_sem, link.next())
                    if u == 3:
                        nc.vector.tensor_tensor(vn[:], vn[:], lng_row[:, None, :].to_broadcast([P, TT, HG]), ALU.mult
                                                ).then_inc(dve_sem, 1)
                        dve.wait_ge(dve_sem, link.next())
                    if u == 4:
                        nc.vector.tensor_tensor(vn[:], vn[:], lnb_row[:, None, :].to_broadcast([P, TT, HG]), ALU.add
                                                ).then_inc(vn_ready.sem, 1)
                    if u == 5:
                        dve.wait_ge(*out(pos, "zg"))
                        nc.vector.tensor_tensor(gate[:], gate[:], hgg_row[:, None, :].to_broadcast([P, TT, HG]),
                                                ALU.mult)
                    if u + 2 < UNITS:
                        scaled(u + 2)
                    if u == UNITS - 1:
                        rest_lo(pos, "otu", a_lo[:, 4:8, :], a_hi[:, 4:8, :], out_of(pos, "otu")[:])
                    if u == 6:
                        refine(pos, "oa", 12)
                        for t in range(3):
                            mixed(t)
                    new_state(u)
                    if u == 5:
                        dve.wait_ge(o_ready.sem, o_ready.at(pos, 5))
                        mean_square(pos, "oa", 12, 1.0 / P)
                    if u == 6:
                        dve.wait_ge(*out(pos, "zu"))
                        dve.wait_ge(*done(pos, "mix"))
                        ps = out_of(pos, "mix")
                        for t in range(TT):
                            for g in range(H):
                                c = slice(g * P, g * P + P)
                                ins = nc.vector.scalar_tensor_tensor(uu[:, t, c], ps[:, t, c], bs_col[:, g:g + 1],
                                                                     uu[:, t, c], ALU.add, ALU.mult)
                        ins.then_inc(evacuated_of(pos, "mix"), 1)
                dve.wait_ge(o_ready.sem, o_ready.at(pos, UNITS - 1))
                newton(pos, "ob", 4, 1.0 / P)
                mixed(3)
                rest_lo(pos, "oto", a_lo[:, 0:4, :], a_hi[:, 0:4, :], out_of(pos, "oto")[:])

                def add_to_x(job, c):
                    dve.wait_ge(*done(pos, job))
                    xc = x[:, :, c * 512:c * 512 + 512]
                    nc.vector.tensor_tensor(xc, out_of(pos, job)[:], xc, ALU.add).then_inc(evacuated_of(pos, job), 1)

                def norm_halves(tag, name):
                    for c in range(2):
                        add_to_x((name, c), c)
                        dve.wait_ge(*out(pos, (name, c)))
                        if c == 0:
                            dve.wait_ge(gain_in.sem, gain_in.at(pos, tag))
                        s = slice(c * 512, c * 512 + 512)
                        nc.vector.tensor_tensor(xg[c][:], x[:, :, s], gain[:, None, s].to_broadcast([P, TT, 512]),
                                                ALU.mult).then_inc(xn_ready.sem, 1)
                        s = slice(4 * c, 4 * c + 4)
                        rest_lo(pos, (tag, c), a_lo[:, s, :], a_hi[:, s, :], out_of(pos, (tag, c))[:])
                    mean_squares(pos, tag, TT, [x[:, t, :] for t in (2, 3)],
                                 [junk[:, t, :] for t in range(2)])

                dve.wait_ge(x_in.sem, x_in.at(pos, TT - 1))
                norm_halves("n2", "wo")
                for c in range(2):
                    rest_lo(pos, ("cq", c), b_lo[:, 4 * c:4 * c + 4, :], b_hi[:, 4 * c:4 * c + 4, :],
                            out_of(pos, ("cq", c))[:], ATT_SCALE)

                def row_max(g, t):
                    hs = slice(2 * g, 2 * g + 2)
                    nc.vector.tensor_reduce(mx[:, t, hs], out_of(pos, ("sc", g))[:, t, :].rearrange(
                        "p (h m) -> p h m", m=NM), AX.X, ALU.max, negate=True).then_inc(dve_sem, 1)
                    dve.wait_ge(dve_sem, link.next())
                    nc.vector.tensor_scalar(mx[:, t, hs], mx[:, t, hs], rstd[:, 20 + t:21 + t], None, ALU.mult
                                            ).then_inc(max_ready.sem, 1)

                def normalised(g, t):
                    if t == TT - 1:
                        dve.wait_ge(*out(pos, ("sc", g)))
                    else:
                        dve.wait_ge(exp_ready.sem, exp_ready.at(pos, g * (TT - 1) + t))
                    hs = slice(2 * g, 2 * g + 2)
                    nc.vector.reciprocal(rinv[:, t, hs], psums[:, t, hs]).then_inc(dve_sem, 1)
                    dve.wait_ge(dve_sem, link.next())
                    pv = pp[:, t, 2 * g * NM:2 * g * NM + 2 * NM].rearrange("p (h m) -> p h m", m=NM)
                    ins = nc.vector.tensor_tensor(pv, pv, rinv[:, t, hs, None].to_broadcast([P, 2, NM]), ALU.mult)
                    if t == TT - 1:
                        ins.then_inc(p_ready.sem, 1)

                def attended_lo(name, h):
                    s, b0 = slice(2 * h, 2 * h + 2), 2 * (h % 2)
                    rest_lo(pos, (name, h), pt_lo[h % 2][:] if name == "pt" else a_lo[:, s, :],
                            pt_hi[h % 2][:] if name == "pt" else a_hi[:, s, :], out_of(pos, (name, h))[:, b0:b0 + 2, :])

                dve.wait_ge(*done(pos, ("sc", 0)))
                for t in range(TT + 1):
                    if t < TT:
                        row_max(0, t)
                    if t:
                        normalised(0, t - 1)
                dve.wait_ge(*done(pos, ("sc", 1)))
                for t in range(TT):
                    row_max(1, t)
                for g in range(2):
                    attended_lo(*ATTENDED[g])
                    normalised(1, 2 * g)
                    normalised(1, 2 * g + 1)
                for job in ATTENDED[2:]:
                    attended_lo(*job)
                norm_halves("n3", "co")
                r3 = slice(stat("n3"), stat("n3") + TT)
                nc.vector.tensor_tensor(rstd[:, r3], rstd[:, r3], rstd[:, r3], ALU.mult).then_inc(dve_sem, 1)
                dve.wait_ge(dve_sem, link.next())

                def relu_square(e, f=0):
                    dve.wait_ge(relu_ready.sem, relu_ready.at(pos, e + f * 2))
                    nc.vector.tensor_tensor(relu[:], relu[:], out_of(pos, ("up", e))[:], ALU.mult
                                            ).then_inc(sq_ready.sem, 1)
                    dve.wait_ge(ht_hi_ready.sem, ht_hi_ready.at(pos, e + f * 2))
                    nc.vector.tensor_tensor(ht_lo[e % 2][:], relu[:], ht_hi[e % 2][:].bitcast(F32),
                                            ALU.subtract).then_inc(evacuated_of(pos, ("up", e)), 1)

                def add_down(e, c, f=0):
                    dve.wait_ge(*done(pos, ("dn", e, c), f))
                    for t in range(TT):
                        xc = x[:, t, c * 512:c * 512 + 512]
                        ins = nc.vector.scalar_tensor_tensor(xc, out_of(pos, ("dn", e, c))[:, t, :],
                                                             rstd[:, 24 + t:25 + t], xc, ALU.mult, ALU.add)
                    ins.then_inc(evacuated_of(pos, ("dn", e, c)), 1)

                relu_square(0)
                with dve.Fori(0, 3) as f:
                    for e in range(2):
                        relu_square(e + 1, f)
                        for c in range(2):
                            add_down(e, c, f)
                relu_square(7)
                for p in range(2):
                    if not last:
                        n1_rows_scaled(pos, p)
                    elif p == 0:
                        dve.wait_ge(s_first_in, 16)
                        dve.wait_ge(gain_in.sem, gain_in.at(pos, "n1"))
                        norm_s("n1", "xn1", gain[SQ, :])
                    add_down(6 + p, 0)
                    if not last:
                        n1_lo(pos, p)
                    elif p == 1:
                        columns("n1", "xt1", 4)
                    add_down(6 + p, 1)
                dve.wait_ge(*out(pos, ("dn", 7, 1)))
                mean_squares(pos, "y", TT, [x[:, t, :] for t in (2, 3)], [xn[:, t, :] for t in (2, 3)])
                dve.wait_ge(gain_in.sem, gain_in.at(pos, "y"))
                for t in range(TT):
                    scaled_row("y", t, xn[:, t, :], x[:, t, :])
                link.end()

            with dve.Fori(0, NB - 1) as b:
                block_vector(("block", b), False)
            block_vector(last_block, True)

            link.start(("sample", 0))

            def add_to_xs(job, name, b, c):
                dve.wait_ge(*step(job))
                col = slice(c * 512, c * 512 + 512)
                nc.vector.tensor_tensor(xs[:, col], bank(b)[SQ, :], xs[:, col], ALU.add).then_inc(dve_s.did(name), 1)

            def requests(t):
                return t.rearrange("p h (b t) -> p (h b) t", t=DS)

            dve.wait_ge(y_out.sem, y_out.at(last_block, TT - 1))
            dve.wait_ge(s_consts_in, 16 * (3 + 5 * DB))
            nc.vector.memset(qe_m[:], 0.0)
            nc.vector.tensor_tensor(ws_s[:], w4[:, :, None, :].to_broadcast([NS, H, DB, DS]),
                                    tri_own[:, None, :, :].to_broadcast([NS, H, DB, DS]), ALU.mult)
            dve.wait_ge(*step("sig"))
            for h in range(H):
                nc.vector.tensor_scalar(kk_s[:, h, :], kk_s[:, h, :], oml[:, h:h + 1], None, ALU.mult)
            nc.vector.tensor_tensor(qq_s[:], qq_s[:], bank(7)[:, H * NS:2 * H * NS].rearrange(
                "p (h s) -> p h s", s=NS), ALU.mult).then_inc(dve_s.did("qq"), 1)
            dve.wait_ge(*step("logf"))
            lf = requests(bb_s[:])
            for t in range(1, DS):
                nc.vector.tensor_tensor(lf[:, :, t], lf[:, :, t], lf[:, :, t - 1], ALU.add).then_inc(dve_sem, 1)
                dve.wait_ge(dve_sem, link.next())
            for l in range(1, SLV):
                w = 1 << l
                src, dst = (t.rearrange("p h (n w) -> p (h n) w", w=w) for t in (bb_s[:], dec_s[:, l - 1]))
                nc.vector.tensor_tensor(dst, src, src[:, :, w // 2 - 1:w // 2].to_broadcast([P, H * NS // w, w]),
                                        ALU.subtract)
            nc.vector.tensor_copy(dec_s[:, SLV - 1], bb_s[:])
            nc.vector.tensor_tensor(requests(dec_s[:, SLV]), lf[:, :, DS - 1:DS].to_broadcast(
                [P, H * DB, DS]), lf, ALU.subtract).then_inc(dve_s.did("args"), 1)
            dve.wait_ge(*step("decays"))
            for l in range(1, SLV):
                w = 1 << l
                v, k, q = (t.rearrange("p h (n w) -> p (h n) w", w=w) for t in (dec_s[:, l - 1], kk_s[:], qq_s[:]))
                nc.vector.tensor_tensor(v[:, :, 0:w // 2], v[:, :, 0:w // 2], k[:, :, 0:w // 2], ALU.mult)
                nc.vector.tensor_tensor(v[:, :, w // 2:w], v[:, :, w // 2:w], q[:, :, w // 2:w], ALU.mult)
            for h in range(H):
                nc.vector.tensor_copy(el_s[:, h, :], dec_s[:, SLV - 1, h].rearrange("p (b t) -> p b t", t=DS)[:, :, DS - 1])
                nc.vector.tensor_tensor(qe_m[:, h, :, 0:DS], dec_s[:, SLV - 1, h].rearrange("p (b t) -> p b t", t=DS),
                                        qq_s[:, h].rearrange("p (b t) -> p b t", t=DS), ALU.mult)
            nc.vector.tensor_tensor(dec_s[:, SLV], dec_s[:, SLV], kk_s[:], ALU.mult).then_inc(dve_s.did("scaled"), 1)
            dve.wait_ge(*step("v_rows"))
            nc.vector.tensor_tensor(vm[:], v_s[:, None, :].to_broadcast([NS, DB, HG]),
                                                   own[:, :, None].to_broadcast([NS, DB, HG]), ALU.mult
                                                              ).then_inc(dve_s.did("vm"), 1)
            dve.wait_ge(*step("gate"))
            nc.vector.tensor_tensor(gate_s[:], gate_s[:], hgg_row[SQ, :], ALU.mult)
            dve.wait_ge(*step("lv"))
            nc.vector.tensor_tensor(tmp_s[:], bank(1)[SQ, 0:H * SLV * NS].rearrange("p (h l s) -> p h l s", l=SLV, s=NS),
                                         masks_s[:, None, :, :].to_broadcast([NS, H, SLV, NS]), ALU.mult
                                                    ).then_inc(dve_sem, 1)
            dve.wait_ge(dve_sem, link.next())
            nc.vector.tensor_reduce(att_s[:], tmp_s[:].rearrange("p h l s -> p h s l"), AX.X, ALU.add
                       ).then_inc(dve_s.did("att"), 1)
            dve.wait_ge(*step("zv_gelu"))
            nc.vector.bn_stats(st_s[:], vn_s[:]).then_inc(dve_sem, 1)
            dve.wait_ge(dve_sem, link.next())
            nc.vector.tensor_copy(yt[SQ, 0:1], st_s[:, 0:1])
            nc.vector.bn_aggr(mv_s[:], st_s[:]).then_inc(dve_sem, 1)
            dve.wait_ge(dve_sem, link.next())
            nc.vector.tensor_scalar(var[SQ, 0:1], mv_s[:, 1:2], EPS, None, ALU.add).then_inc(dve_s.did("var_ln"), 1)
            newton_s("ln", 1, None)
            nc.vector.tensor_scalar(vn_s[:], vn_s[:], mv_s[:, 0:1], rstd[SQ, 0:1], ALU.subtract, ALU.mult
                       ).then_inc(dve_sem, 1)
            dve.wait_ge(dve_sem, link.next())
            nc.vector.tensor_tensor(vn_s[:], vn_s[:], lng_row[SQ, :], ALU.mult).then_inc(dve_sem, 1)
            dve.wait_ge(dve_sem, link.next())
            nc.vector.tensor_tensor(vn_s[:], vn_s[:], lnb_row[SQ, :], ALU.add).then_inc(dve_s.did("vn"), 1)
            dve.wait_ge(*step("o_rows"))
            nc.vector.tensor_tensor(xns[:, 0:HG], o_s[:], o_s[:], ALU.mult).then_inc(dve_sem, 1)
            dve.wait_ge(dve_sem, link.next())
            nc.vector.tensor_reduce(ss[SQ, 0:H], xns[:, 0:HG].rearrange("p (h c) -> p h c", h=H), AX.X, ALU.add
                       ).then_inc(dve_sem, 1)
            dve.wait_ge(dve_sem, link.next())
            newton_s("o", H, 1.0 / P)
            dve.wait_ge(*step("mix"))
            dve.wait_ge(*step("zu_gelu"))
            for g in range(H):
                col = slice(g * P, g * P + P)
                ins = nc.vector.scalar_tensor_tensor(u_s[:, col], bank(7)[SQ, col], b4[:, g:g + 1], u_s[:, col],
                                                     ALU.add, ALU.mult)
            ins.then_inc(dve_s.did("mixed_cm"), 1)
            for h in range(H):
                col = slice(h * P, h * P + P)
                ins = nc.vector.scalar_tensor_tensor(o_s[:, col], o_s[:, col], rstd[SQ, h:h + 1], gate_s[:, col],
                                                     ALU.mult, ALU.mult)
            ins.then_inc(dve_s.did("mixed"), 1)
            columns("ot", "xt_ot", 0)
            for h in range(H):
                ins = nc.vector.tensor_tensor(s0[:, :, h, :], s0[:, :, h, :], el_s[:, h, :, None].to_broadcast([P, DB, P]),
                                              ALU.mult)
            ins.then_inc(dve_sem, 1)
            dve.wait_ge(dve_sem, link.next())
            for j in range(8):
                h, r0 = divmod(j, 2)
                dve.wait_ge(*step(f"st{j}"))
                s = s0[:, 4 * r0:4 * r0 + 4, h, :]
                nc.vector.tensor_tensor(s, bank(4 + j % 4).rearrange("p (b v) -> p b v", v=P), s,
                                                            ALU.add).then_inc(dve_s.did(f"new{j}"), 1)
                if j == 3:
                    add_to_xs("wo0", "x_wo0", 1, 0)
            add_to_xs("wo1", "x_wo1", 2, 1)
            dve.wait_ge(*step("x_wo1"))
            dve.wait_ge(s_gains_in, 32)
            norm_s("n2", "xn2", gains[:, 0, :])
            columns("n2", "xt2", 0)
            dve.wait_ge(vn_out, 16)
            nc.vector.memset(qm[:], 0.0)
            nc.vector.memset(pm[:], 0.0).then_inc(dve_sem, 1)
            dve.wait_ge(dve_sem, link.next())

            def own_tokens(job, name, b, dst):
                dve.wait_ge(*step(job))
                for k in range(KD):
                    ins = nc.vector.tensor_copy(dst[:, k, :, 0:DS], bank(b)[:, k * NS:k * NS + NS].rearrange(
                        "p (b t) -> p b t", t=DS))
                ins.then_inc(dve_s.did(name), 1)

            own_tokens("qt", "qm", 3, qm)
            for r in range(DB):
                keys_part(dve, r, 1, nc.vector.tensor_copy).then_inc(dve_s.did(f"kts{r}_1"), 1)
            dve.wait_ge(*step(f"sc{DB - 1}"))
            nc.vector.tensor_reduce(mx_s[:], half[0][SQ, :, 0:NM], AX.X, ALU.max, negate=True
                       ).then_inc(dve_s.did("max"), 1)
            dve.wait_ge(*step("p_exp"))
            nc.vector.reciprocal(rinv_s[:], sum_s[:]).then_inc(dve_sem, 1)
            dve.wait_ge(dve_sem, link.next())
            pv = q_s[:].rearrange("p (h m) -> p h m", h=H)
            nc.vector.tensor_tensor(pv, pv, rinv_s[:, :, None].to_broadcast([NS, H, NM]), ALU.mult
                       ).then_inc(dve_s.did("p_rows"), 1)
            own_tokens("pt", "pm", 4, pm)
            columns("cat", "xt_ca", 4)
            for c in range(2):
                add_to_xs(f"co{c}", f"x_co{c}", 5 + c, c)
            dve.wait_ge(*step("x_co1"))
            norm_s("n3", "xn3", gains[:, 1, :])
            columns("n3", "xt3", 0)
            for e in range(9):
                if e < 8:
                    dve.wait_ge(*step(f"relu{e}"))
                    nc.vector.tensor_tensor(relu_s[e % 2][:], relu_s[e % 2][:], bank(1 + e % 2)[SQ, :],
                                                              ALU.mult).then_inc(dve_s.did(f"sq{e}"), 1)
                if e:
                    columns(f"ht{e - 1}", f"hts{e - 1}", 3 + (e - 1) % 2, 4, hts[:, 4 * (e - 1):4 * e, :])
            for c in range(2):
                add_to_xs(f"dn3_{c}", f"x_dn{c}", 5 + c, c)
            dve.wait_ge(*step("x_dn1"))
            norm_s("y", "y", gain[SQ, :])
            link.end()


_INS = ["x_prompt", "x_sample", "mem_prompt", "state_hgrn", "cache_mem_k", "cache_mem_v", "lb_param", "g_mix", "w_in",
        "hg_norm_g", "ln_v_g", "ln_v_b", "w_s", "b_s", "w_out", "g_cross", "g_mem", "w_cq", "w_ck", "w_cv", "w_co",
        "g_mlp", "w_up", "w_down", "g_final"]
_OUTS = [(1, 2048, 1024), (8, 4, 1024), (1, 1, 4, 128, 128), (1, 8, 4, 128, 128), (1, 1, 256, 4, 256),
         (1, 1, 256, 4, 256), (1, 8, 4, 512)]


def kernel(**inputs):
    import numpy as _np
    import concourse.bacc as _bacc
    from concourse import mybir as _mybir
    from concourse.bass_utils import run_bass_kernel_spmd as _run

    s, t = _np.arange(P)[:, None], _np.arange(P)[None, :]
    masks = [s == t]
    for l in range(1, LEVELS):
        w = 1 << l
        masks.append((s // w == t // w) & (s % w < w // 2) & (t % w >= w // 2))
    m = masks
    select = [m[1], m[3], m[5], m[7], m[2] | m[3], m[6] | m[7], m[4] | m[5] | m[6] | m[7], s <= t]
    consts = {"c_ident": s == t, "c_ones": s < P + t, "c_masks": _np.stack(select, 1),
              "c_masks_s": _np.stack(m[0:SLV], 1)[0:NS, :, 0:NS]}

    s, t = _np.arange(NS)[:, None], _np.arange(NS)[None, :]
    consts["c_own"] = s // DS == _np.arange(DB)[None, :]
    consts["c_tri_own"] = ((s // DS == t // DS) & (s <= t)).reshape(NS, DB, DS)

    nc = _bacc.Bacc("TRN2", target_bir_lowering=False, num_devices=1)
    arrays, I = {}, {}
    for name in _INS + list(consts):
        a = _np.ascontiguousarray(inputs[name] if name in inputs else consts[name].astype(_np.float32))
        arrays[f"in_{name}"] = a
        I[name] = nc.dram_tensor(f"in_{name}", a.shape, _mybir.dt.from_np(a.dtype), kind="ExternalInput").ap()
    O = [nc.dram_tensor(f"out_{i}", shape, F32, kind="ExternalOutput").ap() for i, shape in enumerate(_OUTS)]
    program(nc, I, O)
    r = _run(nc, [arrays], core_ids=[0])
    return tuple(r.results[0][f"out_{i}"] for i in range(len(_OUTS)))
```
